# Optimizing a Trainium2 kernel written in Bass

```python
import jax, jax.numpy as jnp
from jax import lax
import numpy as np

D_MODEL = 1024
BATCH = 1
SEQ = 512
DEPTH = 1
DEC_BATCH = 8
DEC_SEQ = 1
PAST_LEN = 4096
PAGE_SIZE = 128

N_HEADS = 8
N_KV_HEADS = 2
HEAD_DIM = 64
Q_GROUP = N_HEADS // N_KV_HEADS
WINDOW = 128
ATT_BLOCK = WINDOW
ATT_W = N_HEADS * HEAD_DIM
KV_W = N_KV_HEADS * HEAD_DIM
POOL_WINDOWS = (2, 4, 8, 16)
POOL_GROUPS = 4
POOL_W = D_MODEL // 2
POOL_GC = POOL_W // POOL_GROUPS
POOL_HIST = max(POOL_WINDOWS) - 1
IN_W = ATT_W + 2 * KV_W + POOL_W + 2 * D_MODEL
PEER_HEADS = 8
PEER_NKEYS = 128
PEER_EXPERTS = PEER_NKEYS * PEER_NKEYS
PEER_DQ = 256
PEER_TOPK = 16
PEER_BLOCK = 128
NORM_EPS = 1e-6

kernel_name = 'hybrid_swa_pool_peer_step'

def rms_norm(x, g):
    xf = x.astype(jnp.float32)
    y = xf * lax.rsqrt(jnp.mean(xf * xf, axis=-1, keepdims=True) + NORM_EPS)
    return (y * g.astype(jnp.float32)).astype(x.dtype)

def alibi_slopes():
    return jnp.exp2(-8.0 * jnp.arange(1, N_HEADS + 1, dtype=jnp.float32) / N_HEADS)

def adaln(c, w_ada, b_ada):
    m = jax.nn.silu(c) @ w_ada + b_ada
    return jnp.split(m[:, None, :], 6, axis=-1)

def sink_attention(q, k, v, dist, valid, sinks):
    s = jnp.einsum('...qkgd,...skd->...kgqs', q, k).astype(jnp.float32) * (HEAD_DIM ** -0.5)
    slopes = alibi_slopes().reshape(N_KV_HEADS, Q_GROUP, 1, 1)
    s = s - slopes * dist[..., None, None, :, :].astype(jnp.float32)
    s = jnp.where(valid[..., None, None, :, :], s, -1e30)
    sink = jnp.broadcast_to(sinks.astype(jnp.float32).reshape(N_KV_HEADS, Q_GROUP, 1, 1), s.shape[:-1] + (1,))
    p = jax.nn.softmax(jnp.concatenate([s, sink], axis=-1), axis=-1)[..., :-1]
    return jnp.einsum('...kgqs,...skd->...qkgd', p.astype(v.dtype), v)

def attn_prompt(q, k, v, sinks):
    B, S = q.shape[:2]
    nb = S // ATT_BLOCK
    qb = q.reshape(B, nb, ATT_BLOCK, N_KV_HEADS, Q_GROUP, HEAD_DIM)

    def band(t):
        tp = jnp.pad(t, ((0, 0), (ATT_BLOCK, 0), (0, 0), (0, 0)))
        tp = tp.reshape(B, nb + 1, ATT_BLOCK, N_KV_HEADS, HEAD_DIM)
        return jnp.concatenate([tp[:, :-1], tp[:, 1:]], axis=2)

    qi = jnp.arange(ATT_BLOCK)[:, None]
    kj = jnp.arange(2 * ATT_BLOCK)[None, :]
    dist = qi + ATT_BLOCK - kj
    key_pos = (jnp.arange(nb)[:, None, None] - 1) * ATT_BLOCK + kj[None]
    valid = (dist >= 0) & (dist <= WINDOW) & (key_pos >= 0)
    o = sink_attention(qb, band(k), band(v), dist, valid, sinks)
    return o.reshape(B, S, ATT_W)

def attn_sample(q, k, v, ck, cv, sinks):
    Bd, Sd = q.shape[:2]
    W = ck.shape[1]
    kk = jnp.concatenate([ck, k], axis=1)
    vv = jnp.concatenate([cv, v], axis=1)
    s_rel = jnp.arange(W + Sd)[None, :] - W
    dist = jnp.arange(Sd)[:, None] - s_rel
    valid = (dist >= 0) & (dist <= WINDOW)
    o = sink_attention(q.reshape(Bd, Sd, N_KV_HEADS, Q_GROUP, HEAD_DIM), kk, vv, dist, valid, sinks)
    return o.reshape(Bd, Sd, ATT_W), kk[:, -W:], vv[:, -W:]

def multiscale_pool(u_ext, n_hist, w_pool, pool_scale):
    B, L, _ = u_ext.shape
    uf = u_ext.astype(jnp.float32).reshape(B, L, POOL_GROUPS, POOL_GC)
    cs = jnp.concatenate([jnp.zeros_like(uf[:, :1]), jnp.cumsum(uf, axis=1)], axis=1)
    hi = jnp.arange(n_hist, L) + 1
    win = jnp.asarray(POOL_WINDOWS, dtype=jnp.int32)
    lo = jnp.maximum(hi[:, None] - win[None, :], 0)
    grp = jnp.arange(POOL_GROUPS)[None, :]
    total = cs[:, hi] - cs[:, lo, grp]
    mean = total / (hi[:, None] - lo).astype(jnp.float32)[None, :, :, None]
    d = (mean - uf[:, n_hist:]).astype(u_ext.dtype)
    y = jnp.einsum('btgc,gce->btge', d, w_pool) * pool_scale.reshape(POOL_GROUPS, POOL_GC)
    return y.reshape(B, L - n_hist, POOL_W)

def peer_ffn(h, w_q, sub_keys, u_tab, v_tab):
    B, S, D = h.shape
    T = B * S
    hf = h.reshape(T, D)
    q = (hf @ w_q).reshape(T, PEER_HEADS, 2, PEER_DQ // 2)
    sc = jnp.einsum('thcd,hcnd->thcn', q, sub_keys).astype(jnp.float32)
    s_half, i_half = lax.top_k(sc, PEER_TOPK)
    cand = (s_half[:, :, 0, :, None] + s_half[:, :, 1, None, :]).reshape(T, PEER_HEADS, PEER_TOPK * PEER_TOPK)
    best, pos = lax.top_k(cand, PEER_TOPK)
    ia = jnp.take_along_axis(i_half[:, :, 0], pos // PEER_TOPK, axis=-1)
    ib = jnp.take_along_axis(i_half[:, :, 1], pos % PEER_TOPK, axis=-1)
    expert = ia * PEER_NKEYS + ib
    gate = jax.nn.softmax(best, axis=-1).astype(h.dtype)
    pad = (-T) % PEER_BLOCK
    nblk = (T + pad) // PEER_BLOCK

    def padr(a):
        a = jnp.pad(a, ((0, pad),) + ((0, 0),) * (a.ndim - 1))
        return a.reshape((nblk, PEER_BLOCK) + a.shape[1:])

    def block(args):
        hb, eb, gb = args
        act = jax.nn.gelu(jnp.einsum('td,thkd->thk', hb, u_tab[eb]))
        return jnp.einsum('thk,thkd->td', gb * act, v_tab[eb])

    out = lax.map(block, (padr(hf), padr(expert), padr(gate)))
    return out.reshape(nblk * PEER_BLOCK, D)[:T].reshape(B, S, D)

def mixer_projections(x, c, norm1_g, w_ada, b_ada, w_in, q_norm_g, k_norm_g):
    sh1, sc1, g1, sh2, sc2, g2 = adaln(c, w_ada, b_ada)
    h = rms_norm(x, norm1_g) * (1 + sc1) + sh1
    z = h @ w_in
    cuts = [ATT_W, ATT_W + KV_W, ATT_W + 2 * KV_W, ATT_W + 2 * KV_W + POOL_W, ATT_W + 2 * KV_W + POOL_W + D_MODEL]
    q, k, v, p, ga, gb = jnp.split(z, cuts, axis=-1)
    B, S = x.shape[:2]
    q = rms_norm(q.reshape(B, S, N_HEADS, HEAD_DIM), q_norm_g)
    k = rms_norm(k.reshape(B, S, N_KV_HEADS, HEAD_DIM), k_norm_g)
    v = v.reshape(B, S, N_KV_HEADS, HEAD_DIM)
    return q, k, v, p, ga, gb, (g1, sh2, sc2, g2)

def merge_and_channel_mix(x, attn_o, pool_o, ga, gb, mods, w_branch_attn, w_branch_pool, w_out,
                          norm2_g, peer_wq, peer_subkeys, peer_u, peer_v):
    g1, sh2, sc2, g2 = mods
    merged = jax.nn.sigmoid(ga) * (attn_o @ w_branch_attn) + jax.nn.sigmoid(gb) * (pool_o @ w_branch_pool)
    x = x + g1 * (merged @ w_out)
    h2 = rms_norm(x, norm2_g) * (1 + sc2) + sh2
    return x + g2 * peer_ffn(h2, peer_wq, peer_subkeys, peer_u, peer_v)

def setup_inputs(seed: int = 0):
    key = jax.random.key(seed)
    ks = jax.random.split(key, 24)

    def nrm(k, shape, scale=1.0):
        return jax.random.normal(k, shape, jnp.float32) * scale

    win_buf = min(WINDOW, PAST_LEN)
    L = DEPTH
    return {
        'x_prompt': nrm(ks[0], (BATCH, SEQ, D_MODEL)),
        'x_sample': nrm(ks[1], (DEC_BATCH, DEC_SEQ, D_MODEL)),
        'cache_k': nrm(ks[2], (L, DEC_BATCH, win_buf, N_KV_HEADS, HEAD_DIM)),
        'cache_v': nrm(ks[3], (L, DEC_BATCH, win_buf, N_KV_HEADS, HEAD_DIM)),
        'state_pool': nrm(ks[4], (L, DEC_BATCH, POOL_HIST, POOL_W)),
        'c_prompt': nrm(ks[5], (BATCH, D_MODEL)),
        'c_sample': nrm(ks[6], (DEC_BATCH, D_MODEL)),
        'norm1_g': 1.0 + nrm(ks[7], (L, D_MODEL), 0.1),
        'norm2_g': 1.0 + nrm(ks[8], (L, D_MODEL), 0.1),
        'w_ada': nrm(ks[9], (L, D_MODEL, 6 * D_MODEL), 0.5 * D_MODEL ** -0.5),
        'b_ada': nrm(ks[10], (L, 6 * D_MODEL), 0.02),
        'w_in': nrm(ks[11], (L, D_MODEL, IN_W), D_MODEL ** -0.5),
        'q_norm_g': 1.0 + nrm(ks[12], (L, HEAD_DIM), 0.1),
        'k_norm_g': 1.0 + nrm(ks[13], (L, HEAD_DIM), 0.1),
        'attn_sinks': nrm(ks[14], (L, N_HEADS), 0.5),
        'w_pool': nrm(ks[15], (L, POOL_GROUPS, POOL_GC, POOL_GC), POOL_GC ** -0.5),
        'pool_scale': 1.0 + nrm(ks[16], (L, POOL_W), 0.1),
        'w_branch_attn': nrm(ks[17], (L, ATT_W, D_MODEL), ATT_W ** -0.5),
        'w_branch_pool': nrm(ks[18], (L, POOL_W, D_MODEL), POOL_W ** -0.5),
        'w_out': nrm(ks[19], (L, D_MODEL, D_MODEL), D_MODEL ** -0.5),
        'peer_wq': nrm(ks[20], (L, D_MODEL, PEER_HEADS * PEER_DQ), D_MODEL ** -0.5),
        'peer_subkeys': nrm(ks[21], (L, PEER_HEADS, 2, PEER_NKEYS, PEER_DQ // 2), (PEER_DQ // 2) ** -0.5),
        'peer_u': nrm(ks[22], (L, PEER_EXPERTS, D_MODEL), D_MODEL ** -0.5),
        'peer_v': nrm(ks[23], (L, PEER_EXPERTS, D_MODEL), PEER_HEADS ** -0.5),
    }

def reference(x_prompt, x_sample, cache_k, cache_v, state_pool, c_prompt, c_sample,
              norm1_g, norm2_g, w_ada, b_ada, w_in, q_norm_g, k_norm_g, attn_sinks,
              w_pool, pool_scale, w_branch_attn, w_branch_pool, w_out,
              peer_wq, peer_subkeys, peer_u, peer_v):
    yp, ys = x_prompt, x_sample
    kp, vp, pp, ksm, vsm, psm = [], [], [], [], [], []
    n_hist = state_pool.shape[2]
    for l in range(DEPTH):
        q, k, v, p, ga, gb, mods = mixer_projections(yp, c_prompt, norm1_g[l], w_ada[l], b_ada[l],
                                                     w_in[l], q_norm_g[l], k_norm_g[l])
        ao = attn_prompt(q, k, v, attn_sinks[l])
        po = multiscale_pool(p, 0, w_pool[l], pool_scale[l])
        kp.append(k[:, -WINDOW:])
        vp.append(v[:, -WINDOW:])
        pp.append(p[:, -POOL_HIST:])
        yp = merge_and_channel_mix(yp, ao, po, ga, gb, mods, w_branch_attn[l], w_branch_pool[l], w_out[l],
                                   norm2_g[l], peer_wq[l], peer_subkeys[l], peer_u[l], peer_v[l])
        q, k, v, p, ga, gb, mods = mixer_projections(ys, c_sample, norm1_g[l], w_ada[l], b_ada[l],
                                                     w_in[l], q_norm_g[l], k_norm_g[l])
        ao, nk, nv = attn_sample(q, k, v, cache_k[l], cache_v[l], attn_sinks[l])
        p_ext = jnp.concatenate([state_pool[l], p], axis=1)
        po = multiscale_pool(p_ext, n_hist, w_pool[l], pool_scale[l])
        ksm.append(nk)
        vsm.append(nv)
        psm.append(p_ext[:, -n_hist:])
        ys = merge_and_channel_mix(ys, ao, po, ga, gb, mods, w_branch_attn[l], w_branch_pool[l], w_out[l],
                                   norm2_g[l], peer_wq[l], peer_subkeys[l], peer_u[l], peer_v[l])
    return (yp, ys, jnp.stack(kp), jnp.stack(vp), jnp.stack(pp), jnp.stack(ksm), jnp.stack(vsm), jnp.stack(psm))


_drawn_inputs = setup_inputs


def setup_inputs(seed=0):
    import zlib

    import numpy as np

    out = dict(_drawn_inputs(seed))
    spreads = {}
    factors = {'norm2_g': 2.747, 'q_norm_g': 8.0, 'attn_sinks': 28.285, 'pool_scale': 3.144}
    for name, (base, spread) in spreads.items():
        noise = np.random.default_rng([zlib.crc32(name.encode()), seed]).standard_normal(out[name].shape)
        drawn = base * np.exp(spread * noise) if base else spread * noise
        out[name] = __import__('jax').numpy.asarray(drawn.astype(out[name].dtype))
    for name, factor in factors.items():
        out[name] = (out[name] * factor).astype(out[name].dtype)
    return out
```

```python
import numpy as np

import concourse.bass as bass
from concourse import mybir

F32 = mybir.dt.float32
I32 = mybir.dt.int32
U32 = mybir.dt.uint32
ALU = mybir.AluOpType
ACT = mybir.ActivationFunctionType
X = mybir.AxisListType.X

P = 128
D = 1024
C = D // P
T = 512
NB = T // P
S = 8
TT = T + S
HEADS, KV, HD = 8, 2, 64
G = HEADS // KV
WIN = 128
PG = 4
POOL_WINDOWS = (2, 4, 8, 16)
HIST = 15
PW = PG * P
PH = 8
TOPK = 16
NK = 128
SLOTS = PH * TOPK
EPS = 1e-6
NEG = -1e30
BANKS = 8
CHUNK = 8 * 512
RING = 3
GS = 4
TURN = 4

K_ID = 0
K_BIAS = K_ID + P
K_OWN = K_BIAS + HEADS * 2 * P
K_FIRST = K_OWN + PG * P
K_PREV = K_FIRST + PG * P
K_POOLS = K_PREV + PG * P
K_IOTA = K_POOLS + PG * S
K_BIASS = K_IOTA + TOPK
K_END = K_BIASS + KV * (WIN + 1)


def constants():
    k = np.zeros((P, K_END), np.float32)
    k[:, K_ID:K_BIAS] = np.eye(P)
    q, s = np.arange(P)[:, None], np.arange(2 * P)[None, :]
    dist = q + P - s
    valid = (dist >= 0) & (dist <= WIN)
    for kv in range(KV):
        for j in range(G):
            slope = 2.0 ** -(kv * G + j + 1)
            o = K_BIAS + (kv * G + j) * 2 * P
            k[:, o:o + 2 * P] = np.where(valid, -slope * dist, NEG)
            o = K_BIASS + kv * (WIN + 1)
            k[j, o:o + WIN + 1] = -slope * (WIN - np.arange(WIN + 1))
    s, t = np.arange(P)[:, None], np.arange(P)[None, :]
    for g, w in enumerate(POOL_WINDOWS):
        near = (t - s >= 0) & (t - s < w)
        k[:, K_OWN + g * P:K_OWN + (g + 1) * P] = near / w - (s == t)
        k[:, K_FIRST + g * P:K_FIRST + (g + 1) * P] = near / np.minimum(t + 1, w) - (s == t)
        k[:, K_PREV + g * P:K_PREV + (g + 1) * P] = (t + P - s < w) / w
        for r in range(HIST + 1):
            for b in range(S):
                k[r * S + b, K_POOLS + g * S + b] = (r > HIST - w) / w - (r == HIST)
    k[:, K_IOTA:K_IOTA + TOPK] = np.arange(TOPK)
    return k


def bank_plan():
    plan = [(("vecT",), "A"), (("cT",), "A")]
    plan += [(("xT", c), "A") for c in range(C)] + [(("xTs",), "A")]
    plan += [(("ss", 1), "V"), (("sss", 1), "V")]
    plan += [(("ada", i), "V") for i in range(4)]
    plan += [((w, b), "A") for w in ("q", "kv", "p") for b in range(NB + 1)]
    for i in range(4):
        plan += [(("gate", 4 * i + n), "A") for n in range(4)] + [(("gates", i), "A")]
    for b in range(NB):
        plan += [(("qT", b), "A"), (("kT", b), "A")]
    plan += [(("qkTs",), "A")]

    def scores(b):
        return [(("s", b, j), "V") for j in range(G)]

    def values(b):
        halves = (1,) if b == 0 else (0, 1)
        return [k for kv in range(KV) for k in [(("pt", b, kv, h), "A") for h in halves] + [(("o", b, kv), "A")]]

    plan += scores(0) + [(("d", 0), "A")] + scores(1) + [(("d", 1), "A")] + values(0)
    plan += scores(2) + [(("d", 2), "A")] + values(1) + scores(3) + [(("d", 3), "A")] + values(2)
    plan += [(("ds",), "A")] + values(3)
    plan += [(("ada", i), "V") for i in (4, 5)]
    plan += [(("ktT", i), "A") for i in range(2)] + [(("k0T",), "A")]
    plan += [(("sc4", kv, h), "V") for kv in range(KV) for h in range(2)] + [(("sc0", kv), "V") for kv in range(KV)]
    plan += [(("y", g), "A") for g in range(PG)] + [(("ys",), "V")]
    plan += [((w, n), "V") for n in range(C) for w in ("A", "B")]
    plan += [(("pts",), "A"), (("os",), "A")] + [(("ABs",), "V")]
    plan += [(("o2", n), "V") for n in range(C)] + [(("o2s",), "V")]
    plan += [(("ada", i), "V") for i in range(6, 12)]
    plan += [(("skT", i), "A") for i in range(4)]
    plan += [(("ss", 2), "V"), (("sss", 2), "V")]
    plan += [(("g2b", i), "A") for i in range(2)]
    for m in range(16):
        if m % 4 == 0:
            plan += [(("pqs", m // 4), "A")]
        plan += [(("pq", m), "A")]
        if m % 4 == 0:
            plan += [(("scs", m // 4), "V")]
        if m:
            plan += [(("sc", m - 1), "V")]
    plan += [(("sc", 15), "V")]
    plan += [(("h2n", b, i), "A") for b in range(NB + 1) for i in range(2)]
    return plan


def weight_chunks():
    chunks = [(("ada", i), ("ada", i)) for i in range(4)]
    chunks += [((w,), (w, NB)) for w in ("q", "kv", "p")]
    chunks += [(("gate", i), ("gates", i)) for i in range(4)]
    chunks += [(("ada", i), ("ada", i)) for i in (4, 5)]
    chunks += [(("wa",), ("ABs",)), (("wb",), ("ABs",))]
    chunks += [(("wo", 0), ("o2s",)), (("wo", 1), ("o2s",))]
    chunks += [(("ada", i), ("ada", i)) for i in range(6, 12)]
    chunks += [(("wq", i), ("pq", 4 * i + 3)) for i in range(4)]
    return chunks


def decoder_layer(nc, x_prompt, x_sample, cache_k, cache_v, state_pool, c_prompt, c_sample, norm1_g,
                  norm2_g, w_ada, b_ada, w_in, q_norm_g, k_norm_g, attn_sinks, w_pool, pool_scale,
                  w_branch_attn, w_branch_pool, w_out, peer_wq, peer_subkeys, peer_u, peer_v, consts,
                  y_prompt, y_sample, k_win_p, v_win_p, pool_p, k_win_s, v_win_s, pool_s):
    plan = bank_plan()
    order = {key: i for i, (key, _) in enumerate(plan)}
    taker = dict(plan)
    turn = {}
    for who in "AV":
        for i, key in enumerate(k for k, w in plan if w == who):
            turn[key] = i + 1
    chunks = weight_chunks()
    chunk_at = {key: i for i, (key, _) in enumerate(chunks)}

    def sem(name):
        return nc.alloc_semaphore(name)

    bank_filled, emptied_by_act, emptied_by_dve = sem("bank_filled"), sem("emptied_by_act"), sem("emptied_by_dve")
    x_loaded, c_loaded, consts_loaded, small_loaded = sem("x_loaded"), sem("c_loaded"), sem("consts_loaded"), sem("small_loaded")
    subkeys_loaded, cache_loaded, oldest_v_loaded, tail_loaded = sem("subkeys_loaded"), sem("cache_loaded"), sem("oldest_v_loaded"), sem("tail_loaded")
    windows_stored, y_stored = sem("windows_stored"), sem("y_stored")
    w_loaded = [sem(f"w_loaded{i}") for i in range(RING)]
    act_step, dve_step = sem("act_step"), sem("dve_step")
    silu_ready, ones_ready, filler_ready = sem("silu_ready"), sem("ones_ready"), sem("filler_ready")
    squares_ready, root_ready, h_ready = sem("squares_ready"), sem("root_ready"), sem("h_ready")
    qk_mean_ready, qk_root_ready, qk_normed = sem("qk_mean_ready"), sem("qk_root_ready"), sem("qk_normed")
    max_ready, exps_ready, probs_ready = sem("max_ready"), sem("exps_ready"), sem("probs_ready")
    merged_ready, x1_ready = sem("merged_ready"), sem("x1_ready")
    best_ready, best_exp_ready, routed, gates_ready = sem("best_ready"), sem("best_exp_ready"), sem("routed"), sem("gates_ready")
    u_landed = [sem(f"u_landed_half{i}") for i in range(2)]
    v_landed = [sem(f"v_landed_half{i}") for i in range(2)]
    sample_routed, sample_u_landed, sample_v_landed = sem("sample_routed"), sem("sample_u_landed"), sem("sample_v_landed")
    sample_turned, sample_summed, sample_coef_ready, sample_out_ready = sem("sample_turned"), sem("sample_summed"), sem("sample_coef_ready"), sem("sample_out_ready")
    sample_h_ready, sample_h_used = sem("sample_h_ready"), sem("sample_h_used")
    pad_ready = sem("pad_ready")
    u_used, v_used, idx_copied = sem("u_used"), sem("v_used"), sem("idx_copied")
    gelu_done, coef_ready, diag_ready = sem("gelu_done"), sem("coef_ready"), sem("diag_ready")
    sum_read, x1_rows_ready, y_ready = sem("sum_read"), sem("x1_rows_ready"), sem("y_ready")

    AR = 53200
    arena = nc.alloc_sbuf_tensor("arena", [P, AR], F32)
    top = [0]

    def at(off, n, a=None):
        v = arena[:, off:off + n]
        return v if a is None else v.rearrange("p (a b) -> p a b", a=a)

    def take(n):
        top[0] += n
        assert top[0] <= AR, top[0]
        return top[0] - n

    kc = at(take(K_END), K_END)
    ident = kc[:, K_ID:K_ID + P]
    vecT = at(take(68), 68)
    ones = at(take(P), P)
    scT = at(take(C * 9), C * 9, C)
    gqk = at(take(2 * HD), 2 * HD, 2)
    mods = at(take(48 * 9), 48 * 9, 48)
    sinks = at(take(8), 8)
    sinks4 = at(take(2), 2)
    smod = at(take(9 * C), 9 * C, C)
    nmax, ssum, srec, ssink = (at(take(8), 8) for _ in range(4))
    xT = at(take(C * TT), C * TT, C)
    hT = at(take(C * TT), C * TT, C)
    o_ring = take(RING * CHUNK)
    ring = [at(o_ring + i * CHUNK, CHUNK) for i in range(RING)]
    o_shared = top[0]
    o_ga, o_gb = take(C * TT), take(C * TT)
    ga, gb = at(o_ga, C * TT, C), at(o_gb, C * TT, C)
    squares = at(o_gb, C * TT, C)
    o_att, o_d = take(G * TT), take(PG * TT)
    attT, dT = at(o_att, G * TT, G), at(o_d, PG * TT, PG)
    msq, root = at(o_att, TT), at(o_att + TT, TT)
    c9, silu9 = at(o_d, D), at(o_d + D, D)
    v0 = at(o_d, S * P, S)
    o_z = take(6400)
    zqk, zv, zp = at(o_z, 3200, 5), at(o_z + 3200, 640, 5), at(o_z + 3840, 2560, 5)
    xnat = at(o_z, 5 * D, 5)
    pext = zp[:, 0, :]
    mT = at(o_z, C * TT, C)
    o_qkT = take(5 * TT)
    qkT = at(o_qkT, 5 * TT, 5)
    bT = at(o_qkT, PG * TT, PG)
    vec68 = at(o_qkT, P)
    o_q = take(5184)
    zsq, qk_rms = at(o_q, 3200), at(o_q + 3200, 50)
    sS = [at(o_q, 2048, 8), at(o_q + 2048, 2048, 8)]
    pT = at(o_q + 4096, 1024, 2)
    ktile, vtile = at(o_q, 1024, S), at(o_q + 1024, 1024, S)
    kTs = at(o_q + 2048, 1024, S)
    sSs = at(o_q + 3072, 16 * 129, 16)
    k0, k0T = at(take(P), P), at(take(S), S)
    pTs, smisc = at(take(P), P), at(take(4 * 16), 64, 4)
    wpool = at(take(PG * P), PG * P, PG)
    top[0] = o_shared
    o_sk = take(4096)
    sk_rows, skT = at(o_sk, 2048, 16), at(o_sk + 2048, 2048, 16)
    sc = at(take(5 * 16 * NK), 5 * 16 * NK, 80)
    h2n = at(take(5 * D), 5 * D, 5)
    g2b = at(take(D), D)
    o_diag = take(2 * GS * P)
    diags = at(o_diag, 2 * GS * P, 2 * GS)
    pq, pqs = at(o_diag, 1024, 2), at(take(4 * S), 4 * S)
    eidx = at(take(5 * SLOTS), 5 * SLOTS, 5).bitcast(I32)
    best = at(take(5 * SLOTS), 5 * SLOTS, 5)
    r_in, r_cut = at(take(2 * NK), 2 * NK, 2), at(take(2 * NK), 2 * NK, 2)
    r_val = at(take(2 * TOPK), 2 * TOPK, 2)
    r_idx = at(take(2 * TOPK), 2 * TOPK, 2).bitcast(U32)
    r_idxf = at(take(2 * TOPK), 2 * TOPK, 2)
    r_cand, r_cand2 = at(take(TOPK * TOPK), TOPK * TOPK, TOPK), at(take(TOPK * TOPK), TOPK * TOPK)
    r_best = at(take(TOPK), TOPK)
    r_pos = at(take(TOPK), TOPK).bitcast(U32)
    r_half = at(take(2 * TOPK), 2 * TOPK, 2).bitcast(U32)
    r_halff = at(take(2 * TOPK), 2 * TOPK, 2)
    r_hot = at(take(2 * TOPK * TOPK), 2 * TOPK * TOPK, 2 * TOPK)
    r_pick = at(take(2 * TOPK), 2 * TOPK, 2)
    r_e = at(take(TOPK), TOPK)
    r_max, r_sum = at(take(PH), PH), at(take(PH), PH)
    zeros = at(take(P), P)
    y_rows = at(take(D), D)
    acts, gelus, coefs = (at(take(2 * GS), 2 * GS, 2) for _ in range(3))
    idx_s, gate_s, act_s, out_s = at(take(S), S).bitcast(I32), at(take(S), S), at(take(S), S), at(take(C * S), C * S, C)
    eidx_f = at(take(SLOTS), SLOTS)
    pool_pad = at(take(3), 3)
    idx_now = at(take(TURN * GS), TURN * GS, TURN).bitcast(I32)
    u_rows = [at(o_ring + i * D, D) for i in range(2 * GS)]
    v_rows = [at(o_ring + (2 * GS + i) * D, D) for i in range(2 * GS)]
    assert 4 * GS * D <= RING * CHUNK + 4096

    psum = nc.alloc_psum_tensor("psum", [P, BANKS, 512], F32)

    def bank(key):
        return psum[:, order[key] % BANKS, :]

    def wait_filled(eng, key):
        eng.wait_ge(bank_filled, order[key] + 1)

    def wait_emptied(eng, key):
        eng.wait_ge(emptied_by_act if taker[key] == "A" else emptied_by_dve, turn[key])

    def cols(b):
        return slice(b * P, (b + 1) * P) if b < NB else slice(T, TT)

    def rows(b):
        return P if b < NB else S

    last = plan[-1][0]
    N_SMALL = 11
    STEPS = SLOTS // GS
    AHEAD = 2

    block = nc.Block()
    block.__enter__()

    @block.sync
    def _(sp):
        for b in range(NB):
            sp.dma_start(xnat[:, b, :], x_prompt[0, b * P:(b + 1) * P, :]).then_inc(x_loaded, 16)
        sp.dma_start(xnat[0:S, NB, :], x_sample[:, 0, :]).then_inc(x_loaded, 16)
        win = w_in[0].rearrange("(k p) n -> p k n", p=P)
        wad = w_ada[0].rearrange("(k p) n -> p k n", p=P)
        wqd = peer_wq[0].rearrange("(k p) n -> p k n", p=P)
        starts = {"q": (0, 512), "kv": (512, 256), "p": (768, 512)}
        for i, (key, _) in enumerate(chunks):
            if i >= RING:
                wait_filled(sp, chunks[i - RING][1])
            r = ring[i % RING]
            wide = r.rearrange("p (k n) -> p k n", k=8)
            if key[0] == "ada":
                src, dst = wad[:, :, key[1] * 512:(key[1] + 1) * 512], wide
            elif key[0] in starts:
                c0, n = starts[key[0]]
                src, dst = win[:, :, c0:c0 + n], wide[:, :, 0:n]
            elif key[0] == "gate":
                c0 = 1280 + key[1] * 512
                src, dst = win[:, :, c0:c0 + 512], wide
            elif key[0] == "wq":
                src, dst = wqd[:, :, key[1] * 512:(key[1] + 1) * 512], wide
            elif key[0] == "wo":
                src, dst = w_out[0].rearrange("(k p) n -> p k n", p=P)[:, :, key[1] * 512:(key[1] + 1) * 512], wide
            elif key[0] == "wb":
                src, dst = w_branch_pool[0].rearrange("(k p) n -> p k n", p=P), r.rearrange("p (k n) -> p k n", k=4)
            else:
                dst = r.rearrange("p (k n) -> p k n", k=4)
                for kv in range(KV):
                    half = w_branch_attn[0, kv * G * HD:(kv + 1) * G * HD, :].rearrange("(j e) n -> e j n", j=G)
                    sp.dma_start(dst[kv * HD:(kv + 1) * HD], half).then_inc(w_loaded[i % RING], 8 * 2)
                continue
            sp.dma_start(dst, src).then_inc(w_loaded[i % RING], 16)
        for b in range(NB + 1):
            sp.wait_ge(y_ready, b + 1)
            dst = y_prompt[0, b * P:(b + 1) * P, :] if b < NB else y_sample[:, 0, :]
            sp.dma_start(dst, y_rows[0:rows(b), :]).then_inc(y_stored, 16)
        sp.wait_ge(y_stored, 16 * (NB + 1))

    def slot_rounds(i):
        n = 0
        for j in range(i % RING, i + 1, RING):
            n += 2 if chunks[j][0] == ("wa",) else 1
        return 16 * n

    @block.gpsimd
    def _(pool):
        pool.dma_start(c9[0:1, :], c_prompt).then_inc(c_loaded, 16)
        pool.dma_start(c9[1:9, :], c_sample).then_inc(c_loaded, 16)
        pool.dma_start(kc, consts).then_inc(consts_loaded, 16)
        pool.dma_start(vec68[0:48, :], b_ada[0].rearrange("(a b) -> a b", b=P)).then_inc(small_loaded, 16)
        pool.dma_start(vec68[48:56, :], norm1_g[0].rearrange("(a b) -> a b", b=P)).then_inc(small_loaded, 16)
        pool.dma_start(vec68[56:64, :], norm2_g[0].rearrange("(a b) -> a b", b=P)).then_inc(small_loaded, 16)
        pool.dma_start(vec68[64:68, :], pool_scale[0].rearrange("(a b) -> a b", b=P)).then_inc(small_loaded, 16)
        pool.dma_start(gqk[:, 0, :], q_norm_g[0:1, :].broadcast_to((P, HD))).then_inc(small_loaded, 16)
        pool.dma_start(gqk[:, 1, :], k_norm_g[0:1, :].broadcast_to((P, HD))).then_inc(small_loaded, 16)
        pool.dma_start(sinks, attn_sinks[0:1, :].broadcast_to((P, HEADS))).then_inc(small_loaded, 16)
        for kv in range(KV):
            pool.dma_start(sinks4[0:G, kv:kv + 1],
                           attn_sinks[0, kv * G:(kv + 1) * G].rearrange("(j o) -> j o", o=1), allow_slow_non_contiguous=True).then_inc(small_loaded, 16)
        pool.dma_start(wpool, w_pool[0].rearrange("g c e -> c g e")).then_inc(small_loaded, 16)
        pool.dma_start(k0[0:S, :], cache_k[0, :, 0].rearrange("b h e -> b (h e)")).then_inc(small_loaded, 16)
        pool.wait_ge(qk_normed, 1)
        pool.dma_start(k_win_p[0, 0].rearrange("t h e -> t (h e)"), zqk[:, NB - 1, 512:640]).then_inc(windows_stored, 16)
        pool.dma_start(v_win_p[0, 0].rearrange("t h e -> t (h e)"), zv[:, NB - 1, :]).then_inc(windows_stored, 16)
        pool.dma_start(pool_p[0, 0], zp[P - HIST:P, NB - 1, :]).then_inc(windows_stored, 16)
        wait_filled(pool, ("d", 1))
        pool.dma_start(pext[0:HIST * S, :], state_pool[0].rearrange("b r c -> r b c")).then_inc(tail_loaded, 16)
        pool.dma_start(pext[HIST * S:P, :], zp[0:S, NB, :]).then_inc(tail_loaded, 16)
        pool.wait_ge(tail_loaded, 32)
        pool.dma_start(pool_s[0].rearrange("b r c -> r b c"), pext[S:P, :]).then_inc(windows_stored, 16)
        wait_filled(pool, ("o", NB - 1, 1))
        for cache, tile, new in ((cache_k, ktile, zqk[0:S, NB, 512:640]), (cache_v, vtile, zv[0:S, NB, :])):
            pool.dma_start(tile[0:WIN - 1], cache[0, :, 1:WIN].rearrange("b s h e -> s b (h e)")).then_inc(cache_loaded, 16)
            pool.dma_start(tile[WIN - 1:WIN], new).then_inc(cache_loaded, 16)
        pool.wait_ge(cache_loaded, 64)
        pool.dma_start(k_win_s[0].rearrange("b s h e -> s b (h e)"), ktile).then_inc(windows_stored, 16)
        pool.dma_start(v_win_s[0].rearrange("b s h e -> s b (h e)"), vtile).then_inc(windows_stored, 16)
        wait_filled(pool, ("ys",))
        pool.dma_start(v0[0:1], cache_v[0:1, :, 0].rearrange("o b h e -> o b (h e)")).then_inc(oldest_v_loaded, 16)
        wait_emptied(pool, ("ABs",))
        pool.dma_start(sk_rows, peer_subkeys[0].rearrange("h c n e -> n (h c) e")).then_inc(subkeys_loaded, 16)
        wait_filled(pool, last)
        pool.memset(pool_pad, 0.0).then_inc(pad_ready, 1)
        pool.wait_ge(pad_ready, 1)
        for b in range(NB):
            pool.wait_ge(routed, b + 1)
            with pool.Fori(0, STEPS // TURN) as it:
                for k in range(TURN):
                    n, half = it * TURN + (b * STEPS + k), k % 2
                    pool.wait_ge(u_used, n + 1)
                    pool.tensor_copy(idx_now[:, k, :],
                                     eidx[:, b, bass.ds(it * (TURN * GS) + k * GS, GS)]).then_inc(idx_copied, 1)
                    pool.wait_ge(idx_copied, n + 1)
                    for table, buf, landed in ((peer_u, u_rows, u_landed), (peer_v, v_rows, v_landed)):
                        if table is peer_v:
                            pool.wait_ge(v_used, n + 1)
                        c = 2 if table is peer_v else 1
                        pool.tensor_tensor(pool_pad[:, c:c + 1], pool_pad[:, 0:1], pool_pad[:, 0:1], ALU.mult)
                        for i in range(GS):
                            pool.indirect_dma_start(
                                out=buf[half * GS + i], out_offset=None, in_=table[0],
                                in_offset=bass.IndirectOffsetOnAxis(ap=idx_now[:, k, i:i + 1], axis=0),
                            ).then_inc(landed[half], 16)
        pool.wait_ge(sample_routed, 1)
        pool.wait_ge(u_used, AHEAD + NB * STEPS)
        for s in range(S):
            pool.indirect_dma_start(out=u_rows[s], out_offset=None, in_=peer_u[0],
                                    in_offset=bass.IndirectOffsetOnAxis(ap=idx_s[:, s:s + 1], axis=0)).then_inc(sample_u_landed, 16)
        pool.wait_ge(v_used, AHEAD + NB * STEPS)
        for s in range(S):
            pool.indirect_dma_start(out=v_rows[s], out_offset=None, in_=peer_v[0],
                                    in_offset=bass.IndirectOffsetOnAxis(ap=idx_s[:, s:s + 1], axis=0)).then_inc(sample_v_landed, 16)
        pool.wait_ge(windows_stored, 16 * 6)

    @block.scalar
    def _(act):
        def empty(key, ops):
            wait_filled(act, key)
            for n, (out, in_, f, kw) in enumerate(ops):
                ins = act.activation(out, in_, f, **kw)
            ins.then_inc(emptied_by_act, 1)

        def copy(key, out, in_, f=ACT.Copy, **kw):
            empty(key, [(out, in_, f, kw)])

        act.wait_ge(c_loaded, 32)
        act.activation(silu9[0:9, :], c9[0:9, :], ACT.Silu).then_inc(silu_ready, 1)
        copy(("vecT",), vecT, bank(("vecT",))[:, 0:68])
        wait_filled(act, ("vecT",))
        copy(("cT",), scT, bank(("cT",))[:, 0:72].rearrange("p (a b) -> p a b", a=C))
        for c in range(C):
            copy(("xT", c), xT[:, c, 0:T], bank(("xT", c)))
        copy(("xTs",), xT[:, :, T:TT], bank(("xTs",))[:, 0:64].rearrange("p (a b) -> p a b", a=C))
        wait_emptied(act, ("xTs",))
        act.activation(squares, xT, ACT.Square).then_inc(squares_ready, 1)
        wait_emptied(act, ("sss", 1))
        act.activation(root, msq, ACT.Sqrt).then_inc(root_ready, 1)
        act.wait_ge(filler_ready, 1)
        for b in range(NB + 1):
            out = zqk[0:rows(b), b, 0:512].rearrange("p (j v e) -> p v j e", v=KV, e=HD)
            copy(("q", b), out, bank(("q", b))[0:rows(b)].rearrange("p (v j e) -> p v j e", v=KV, e=HD))
        for b in range(NB + 1):
            src = bank(("kv", b))[0:rows(b)]
            empty(("kv", b), [(zqk[0:rows(b), b, 512:640], src[:, 0:128], ACT.Copy, {}),
                              (zv[0:rows(b), b, :], src[:, 128:256], ACT.Copy, {})])
        for b in range(NB + 1):
            copy(("p", b), zp[0:rows(b), b, :], bank(("p", b))[0:rows(b)])
        for i in range(4):
            g = ga if i < 2 else gb
            for n in range(4):
                copy(("gate", 4 * i + n), g[:, (4 * i + n) % C, 0:T], bank(("gate", 4 * i + n)), ACT.Sigmoid)
            copy(("gates", i), g[:, 4 * (i % 2):4 * (i % 2) + 4, T:TT],
                 bank(("gates", i))[:, 0:32].rearrange("p (a b) -> p a b", a=4), ACT.Sigmoid)
        act.wait_ge(qk_mean_ready, 1)
        act.activation(qk_rms, qk_rms, ACT.Sqrt).then_inc(qk_root_ready, 1)
        for b in range(NB):
            copy(("qT", b), qkT[:, 0:4, cols(b)], bank(("qT", b)).rearrange("p (a b) -> p a b", a=4))
            copy(("kT", b), qkT[:, 4, cols(b)], bank(("kT", b))[:, 0:P])
        copy(("qkTs",), qkT[:, :, T:TT], bank(("qkTs",))[:, 0:40].rearrange("p (a b) -> p a b", a=5))

        def exps(b):
            lo = P if b == 0 else 0
            act.wait_ge(max_ready, b + 1)
            for h in range(HEADS):
                act.activation(sS[b % 2][:, h, lo:], sS[b % 2][:, h, lo:], ACT.Exp, bias=nmax[:, h:h + 1],
                               accum_out=ssum[:, h:h + 1])
            act.activation(ssink, ssink, ACT.Exp).then_inc(exps_ready, 1)

        def values(b):
            halves = (1,) if b == 0 else (0, 1)
            for kv in range(KV):
                if b or kv:
                    wait_filled(act, ("o", b, 0) if kv else ("o", b - 1, 1))
                for h in halves:
                    copy(("pt", b, kv, h), pT[:, h, :], bank(("pt", b, kv, h)))
                r = slice(kv * HD, (kv + 1) * HD)
                copy(("o", b, kv), attT[r, :, cols(b)], bank(("o", b, kv))[r].rearrange("p (a b) -> p a b", a=G))

        def pooled(b):
            copy(("d", b), dT[:, :, cols(b)], bank(("d", b)).rearrange("p (a b) -> p a b", a=PG))

        exps(0)
        pooled(0)
        exps(1)
        pooled(1)
        values(0)
        exps(2)
        pooled(2)
        values(1)
        exps(3)
        pooled(3)
        values(2)
        copy(("ds",), dT[:, :, T:TT], bank(("ds",))[:, 0:32].rearrange("p (a b) -> p a b", a=PG))
        values(3)
        for i in range(2):
            copy(("ktT", i), kTs[:, 4 * i:4 * i + 4, :], bank(("ktT", i)).rearrange("p (a b) -> p a b", a=4))
        copy(("k0T",), k0T, bank(("k0T",))[:, 0:S])
        act.wait_ge(max_ready, NB + 1)
        act.activation(smisc[0:G, 1, :], smisc[0:G, 1, :], ACT.Exp)
        act.activation(sSs[0:G], sSs[0:G], ACT.Exp).then_inc(exps_ready, 1)
        for g in range(PG):
            copy(("y", g), bT[:, g, 0:T], bank(("y", g)), scale=vecT[:, 64 + g:65 + g])
        src = bank(("pts",))
        empty(("pts",), [(pTs[:, 0:64], src[:, 0:64], ACT.Copy, {}), (pTs[0:1, 64:128], src[0:1, 64:128], ACT.Copy, {})])
        copy(("os",), attT[:, :, T:TT], bank(("os",))[:, 0:32].rearrange("p (b j) -> p j b", j=G))
        act.wait_ge(x1_ready, 1)
        act.activation(squares, xT, ACT.Square).then_inc(squares_ready, 1)
        for i in range(4):
            copy(("skT", i), skT[:, 4 * i:4 * i + 4, :], bank(("skT", i)).rearrange("p (a b) -> p a b", a=4))
        wait_emptied(act, ("sss", 2))
        act.activation(root, msq, ACT.Sqrt).then_inc(root_ready, 1)
        for i in range(2):
            copy(("g2b", i), g2b[:, i * 512:(i + 1) * 512], bank(("g2b", i)))
        for m in range(16):
            if m % 4 == 0:
                if m:
                    wait_filled(act, ("scs", m // 4 - 1))
                copy(("pqs", m // 4), pqs, bank(("pqs", m // 4))[:, 0:32])
            if m >= 2:
                wait_filled(act, ("sc", m - 2))
            copy(("pq", m), pq[:, m % 2, :], bank(("pq", m)))
        for b in range(NB + 1):
            for i in range(2):
                copy(("h2n", b, i), h2n[0:rows(b), b, i * 512:(i + 1) * 512], bank(("h2n", b, i))[0:rows(b)])

        def gate_exp(b):
            act.wait_ge(best_ready, b + 1)
            act.activation(best[0:rows(b), b, :], best[0:rows(b), b, :], ACT.Exp).then_inc(best_exp_ready, 1)

        gate_exp(0)
        for b in range(NB):
            R = rows(b)
            with act.Fori(0, STEPS // TURN) as it:
                for k in range(TURN):
                    n, half = it * TURN + (b * STEPS + k), k % 2
                    act.wait_ge(u_used, n + 1 + AHEAD)
                    act.activation(gelus[0:R, half, :], acts[0:R, half, :], ACT.Gelu_apprx_tanh).then_inc(gelu_done, 1)
                    act.wait_ge(coef_ready, n + 1)
                    act.wait_ge(v_used, n + 1)
                    for i in range(GS):
                        ins = act.activation(diags[0:R, half * GS + i, 0:R], ident[0:R, 0:R], ACT.Copy,
                                             scale=coefs[0:R, half, i:i + 1])
                    ins.then_inc(diag_ready, 1)
            gate_exp(b + 1)
        act.wait_ge(sample_summed, 1)
        act.activation(act_s, act_s, ACT.Gelu_apprx_tanh).then_inc(gelu_done, 1)

    @block.vector
    def _(dve):
        steps = [0, None]

        def link(ins):
            if steps[1] is not None:
                dve.drain()
                return
            ins.then_inc(dve_step, 1)
            steps[0] += 1
            dve.wait_ge(dve_step, steps[0])

        link(dve.memset(ones, 1.0))
        dve.wait_ge(dve_step, 1)
        dve.memset(nmax, 0.0).then_inc(ones_ready, 1)

        def mean_squares(n):
            wait_filled(dve, ("ss", n))
            dve.tensor_scalar(msq[:, 0:T], bank(("ss", n)), 1.0 / D, EPS, ALU.mult, ALU.add).then_inc(emptied_by_dve, 1)
            wait_filled(dve, ("sss", n))
            dve.tensor_scalar(msq[:, T:TT], bank(("sss", n))[:, 0:S], 1.0 / D, EPS, ALU.mult, ALU.add).then_inc(emptied_by_dve, 1)

        def ada(i):
            wait_filled(dve, ("ada", i))
            bias = vecT[:, 4 * i:4 * i + 4].unsqueeze(2).broadcast_to((P, 4, 9))
            dve.tensor_tensor(mods[:, 4 * i:4 * i + 4, :], bank(("ada", i))[:, 0:36].rearrange("p (a b) -> p a b", a=4),
                              bias, ALU.add).then_inc(emptied_by_dve, 1)

        def modulate(n, shift, scale, gain):
            wait_emptied(dve, ("ada", max(shift, scale) // 4 + 1))
            link(dve.scalar_tensor_tensor(smod, mods[:, scale:scale + C, :], 1.0,
                                          vecT[:, gain:gain + C].unsqueeze(2).broadcast_to((P, C, 9)), ALU.add, ALU.mult))
            dve.wait_ge(root_ready, n)
            link(dve.reciprocal(root, root))
            for c in range(C):
                link(dve.scalar_tensor_tensor(hT[:, c, 0:T], xT[:, c, 0:T], smod[:, c, 0:1], root[:, 0:T], ALU.mult, ALU.mult))
                link(dve.tensor_scalar(hT[:, c, 0:T], hT[:, c, 0:T], mods[:, shift + c, 0:1], None, ALU.add))
            hs = hT[:, :, T:TT]
            link(dve.tensor_tensor(hs, xT[:, :, T:TT], smod[:, :, 1:9], ALU.mult))
            link(dve.tensor_tensor(hs, hs, root[:, T:TT].unsqueeze(1).broadcast_to((P, C, S)), ALU.mult))
            dve.tensor_tensor(hs, hs, mods[:, shift:shift + C, 1:9], ALU.add).then_inc(h_ready, 1)

        mean_squares(1)
        for i in range(4):
            ada(i)
        modulate(1, 0, C, 48)
        wait_emptied(dve, ("xTs",))
        dve.memset(zqk[:, NB, :], 1.0).then_inc(filler_ready, 1)
        wait_emptied(dve, ("kv", NB))
        dve.wait_ge(small_loaded, 16 * N_SMALL)
        dve.wait_ge(filler_ready, 1)
        heads = zqk.rearrange("p b n -> p (b n)").rearrange("p (h e) -> p h e", e=HD)
        zsqh = zsq.rearrange("p (h e) -> p h e", e=HD)
        link(dve.tensor_tensor(zsqh, heads, heads, ALU.mult))
        link(dve.tensor_reduce(qk_rms, zsqh, X, ALU.add))
        dve.tensor_scalar(qk_rms, qk_rms, 1.0 / HD, EPS, ALU.mult, ALU.add).then_inc(qk_mean_ready, 1)
        dve.wait_ge(qk_root_ready, 1)
        link(dve.reciprocal(qk_rms, qk_rms))
        link(dve.tensor_tensor(heads, heads, qk_rms.unsqueeze(2).broadcast_to((P, 50, HD)), ALU.mult))
        for b in range(NB + 1):
            q, k = zqk[:, b, 0:512].rearrange("p (h e) -> p h e", e=HD), zqk[:, b, 512:640].rearrange("p (h e) -> p h e", e=HD)
            dve.tensor_tensor(q, q, gqk[:, 0:1, :].broadcast_to((P, HEADS, HD)), ALU.mult)
            ins = dve.tensor_tensor(k, k, gqk[:, 1:2, :].broadcast_to((P, KV, HD)), ALU.mult)
        ins.then_inc(qk_normed, 1)

        bias = kc[:, K_BIAS:K_OWN].rearrange("p (h s) -> p h s", h=HEADS)

        def scores(b):
            lo = P if b == 0 else 0
            if b >= 2:
                wait_filled(dve, ("pt", b - 2, 1, 1))
            for j in range(G):
                wait_filled(dve, ("s", b, j))
                dve.scalar_tensor_tensor(sS[b % 2][:, 2 * j:2 * j + 2, lo:], bank(("s", b, j)).rearrange("p (v s) -> p v s", v=KV)[:, :, lo:],
                                         HD ** -0.5, bias[:, 2 * j:2 * j + 2, lo:], ALU.mult, ALU.add).then_inc(emptied_by_dve, 1)

        def maxima(b):
            lo = P if b == 0 else 0
            wait_emptied(dve, ("s", b, G - 1))
            link(dve.tensor_reduce(nmax, sS[b % 2][:, :, lo:], X, ALU.max))
            link(dve.tensor_tensor(nmax, nmax, sinks, ALU.max))
            link(dve.tensor_scalar(nmax, nmax, -1.0, None, ALU.mult))
            dve.tensor_tensor(ssink, sinks, nmax, ALU.add).then_inc(max_ready, 1)

        def probabilities(b):
            lo = P if b == 0 else 0
            dve.wait_ge(exps_ready, b + 1)
            link(dve.tensor_tensor(srec, ssum, ssink, ALU.add))
            link(dve.reciprocal(srec, srec))
            s = sS[b % 2][:, :, lo:]
            dve.tensor_tensor(s, s, srec.unsqueeze(2).broadcast_to((P, HEADS, 2 * P - lo)), ALU.mult).then_inc(probs_ready, 1)

        scores(0)
        maxima(0)
        for b in range(1, NB):
            scores(b)
            probabilities(b - 1)
            maxima(b)
        probabilities(NB - 1)
        for i in (4, 5):
            ada(i)
        biass = kc[0:G, K_BIASS:K_END].rearrange("p (v s) -> p v s", v=KV)
        for kv in range(KV):
            for h in range(2):
                wait_filled(dve, ("sc4", kv, h))
                i = kv * S + h * 4
                dve.scalar_tensor_tensor(sSs[0:G, i:i + 4, 1:], bank(("sc4", kv, h))[0:G].rearrange("p (b s) -> p b s", b=4), HD ** -0.5,
                                         biass[:, kv:kv + 1, 1:].broadcast_to((G, 4, WIN)), ALU.mult, ALU.add).then_inc(emptied_by_dve, 1)
        for kv in range(KV):
            wait_filled(dve, ("sc0", kv))
            dve.scalar_tensor_tensor(sSs[0:G, kv * S:(kv + 1) * S, 0:1], bank(("sc0", kv))[0:G, 0:S].unsqueeze(2), HD ** -0.5,
                                           biass[:, kv:kv + 1, 0:1].broadcast_to((G, S, 1)), ALU.mult, ALU.add).then_inc(emptied_by_dve, 1)
        wait_emptied(dve, ("sc0", KV - 1))
        sk = sinks4[0:G, :].unsqueeze(2).broadcast_to((G, KV, S))
        m_max, m_sink, m_sum = (smisc[0:G, i, :] for i in range(3))
        link(dve.tensor_reduce(m_max, sSs[0:G], X, ALU.max))
        link(dve.tensor_tensor(m_max.rearrange("p (v b) -> p v b", v=KV), m_max.rearrange("p (v b) -> p v b", v=KV), sk, ALU.max))
        link(dve.tensor_tensor(m_sink.rearrange("p (v b) -> p v b", v=KV), sk, m_max.rearrange("p (v b) -> p v b", v=KV), ALU.subtract))
        dve.tensor_tensor(sSs[0:G], sSs[0:G], m_max.unsqueeze(2).broadcast_to((G, 16, WIN + 1)), ALU.subtract).then_inc(max_ready, 1)
        dve.wait_ge(exps_ready, NB + 1)
        link(dve.tensor_reduce(m_sum, sSs[0:G], X, ALU.add))
        link(dve.tensor_tensor(m_sum, m_sum, m_sink, ALU.add))
        link(dve.reciprocal(m_sum, m_sum))
        dve.tensor_tensor(sSs[0:G], sSs[0:G], m_sum.unsqueeze(2).broadcast_to((G, 16, WIN + 1)), ALU.mult).then_inc(probs_ready, 1)
        wait_filled(dve, ("ys",))
        dve.tensor_tensor(bT[:, :, T:TT], bank(("ys",))[:, 0:32].rearrange("p (a b) -> p a b", a=PG),
                          vecT[:, 64:68].unsqueeze(2).broadcast_to((P, PG, S)), ALU.mult).then_inc(emptied_by_dve, 1)
        dve.wait_ge(windows_stored, 16 * 6)
        for n in range(C):
            wait_filled(dve, ("A", n))
            dve.tensor_tensor(mT[:, n, 0:T], bank(("A", n)), ga[:, n, 0:T], ALU.mult).then_inc(emptied_by_dve, 1)
            wait_filled(dve, ("B", n))
            dve.tensor_tensor(gb[:, n, 0:T], bank(("B", n)), gb[:, n, 0:T], ALU.mult).then_inc(emptied_by_dve, 1)
            wait_emptied(dve, ("B", n))
            dve.tensor_tensor(mT[:, n, 0:T], mT[:, n, 0:T], gb[:, n, 0:T], ALU.add).then_inc(merged_ready, 1)
        wait_filled(dve, ("ABs",))
        ab = bank(("ABs",))[:, 0:128].rearrange("p (w n b) -> p w n b", w=2, n=C)
        link(dve.tensor_tensor(mT[:, :, T:TT], ab[:, 0], ga[:, :, T:TT], ALU.mult))
        dve.tensor_tensor(gb[:, :, T:TT], ab[:, 1], gb[:, :, T:TT], ALU.mult).then_inc(emptied_by_dve, 1)
        wait_emptied(dve, ("ABs",))
        dve.tensor_tensor(mT[:, :, T:TT], mT[:, :, T:TT], gb[:, :, T:TT], ALU.add).then_inc(merged_ready, 1)
        for n in range(C):
            wait_filled(dve, ("o2", n))
            dve.scalar_tensor_tensor(xT[:, n, 0:T], bank(("o2", n)), mods[:, 16 + n, 0:1], xT[:, n, 0:T],
                                     ALU.mult, ALU.add).then_inc(emptied_by_dve, 1)
        wait_filled(dve, ("o2s",))
        dve.tensor_tensor(gb[:, :, T:TT], bank(("o2s",))[:, 0:64].rearrange("p (a b) -> p a b", a=C),
                          mods[:, 16:24, 1:9], ALU.mult).then_inc(emptied_by_dve, 1)
        wait_emptied(dve, ("o2s",))
        dve.tensor_tensor(xT[:, :, T:TT], xT[:, :, T:TT], gb[:, :, T:TT], ALU.add).then_inc(x1_ready, 1)
        for i in range(6, 12):
            ada(i)
        mean_squares(2)
        modulate(2, 24, 32, 56)
        scv = sc.rearrange("p (b m) n -> p b m n", b=5)
        for m in range(16):
            if m % 4 == 0:
                wait_filled(dve, ("scs", m // 4))
                dve.tensor_copy(scv[0:S, NB, m:m + 4, :], bank(("scs", m // 4))[0:S].rearrange("p (a b) -> p a b", a=4)).then_inc(emptied_by_dve, 1)
            if m:
                wait_filled(dve, ("sc", m - 1))
                dve.tensor_copy(scv[:, 0:NB, m - 1, :], bank(("sc", m - 1)).rearrange("p (a b) -> p a b", a=NB)).then_inc(emptied_by_dve, 1)
        wait_filled(dve, ("sc", 15))
        dve.tensor_copy(scv[:, 0:NB, 15, :], bank(("sc", 15)).rearrange("p (a b) -> p a b", a=NB)).then_inc(emptied_by_dve, 1)
        wait_emptied(dve, ("sc", 15))
        link(dve.memset(zeros, 0.0))
        dve.memset(u_rows[0][:, 0:1], 0.0).then_inc(u_used, AHEAD)
        dve.wait_ge(u_used, AHEAD)

        iota = kc[:, K_IOTA:K_IOTA + TOPK]

        def first8(values, index, src, cut):
            for v, s in zip(values, src):
                dve.max(v[:, 0:8], s)
            dve.drain()
            for v, i, s, c in zip(values, index, src, cut):
                dve.max_index(i[:, 0:8], v[:, 0:8], s)
                dve.match_replace(c, v[:, 0:8], s, -3e38)
            dve.drain()

        def next8(values, index, cut):
            for v, c in zip(values, cut):
                dve.max(v[:, 8:16], c)
            dve.drain()
            for v, i, c in zip(values, index, cut):
                dve.max_index(i[:, 8:16], v[:, 8:16], c)
            dve.drain()

        def route(b, h, part):
            R = rows(b)
            halves = range(2)
            vals, idxs = [r_val[0:R, c, :] for c in halves], [r_idx[0:R, c, :] for c in halves]
            cuts = [r_cut[0:R, c, :] for c in halves]
            flat = r_cand[0:R].rearrange("p a b -> p (a b)")
            if part == 0:
                dve.tensor_copy(r_in[0:R], scv[0:R, b, bass.ds(h * 2, 2), :])
                dve.drain()
                first8(vals, idxs, [r_in[0:R, c, :] for c in halves], cuts)
            if part == 1:
                next8(vals, idxs, cuts)
                dve.tensor_copy(r_idxf[0:R], r_idx[0:R])
                dve.tensor_tensor(r_cand[0:R], r_val[0:R, 0, :].unsqueeze(2).broadcast_to((R, TOPK, TOPK)),
                                  r_val[0:R, 1, :].unsqueeze(1).broadcast_to((R, TOPK, TOPK)), ALU.add)
                dve.drain()
            if part == 2:
                first8([r_best[0:R]], [r_pos[0:R]], [flat], [r_cand2[0:R]])
                next8([r_best[0:R]], [r_pos[0:R]], [r_cand2[0:R]])
            if part == 3:
                dve.tensor_copy(best[0:R, b, bass.ds(h * TOPK, TOPK)], r_best[0:R])
                dve.tensor_scalar(r_half[0:R, 0, :], r_pos[0:R], 4, None, ALU.logical_shift_right)
                dve.tensor_scalar(r_half[0:R, 1, :], r_pos[0:R], 15, None, ALU.bitwise_and)
                dve.drain()
                dve.tensor_copy(r_halff[0:R], r_half[0:R])
                dve.drain()
                hot = r_hot[0:R].rearrange("p (c k) i -> p c k i", c=2)
                dve.tensor_tensor(r_hot[0:R], r_halff[0:R].rearrange("p c k -> p (c k)").unsqueeze(2).broadcast_to((R, 2 * TOPK, TOPK)),
                                  iota[0:R].unsqueeze(1).broadcast_to((R, 2 * TOPK, TOPK)), ALU.is_equal)
                dve.drain()
                dve.tensor_tensor(hot, hot, r_idxf[0:R].unsqueeze(2).broadcast_to((R, 2, TOPK, TOPK)), ALU.mult)
                dve.drain()
                dve.tensor_reduce(r_pick[0:R].rearrange("p c k -> p (c k)"), r_hot[0:R], X, ALU.add)
                dve.drain()
                dve.scalar_tensor_tensor(r_e[0:R], r_pick[0:R, 0, :], float(NK), r_pick[0:R, 1, :], ALU.mult, ALU.add)
                dve.drain()
                dve.tensor_copy(eidx[0:R, b, bass.ds(h * TOPK, TOPK)], r_e[0:R])
                dve.drain()

        def softmax_begin(b):
            R = rows(b)
            v = best[0:R, b, :].rearrange("p (h k) -> p h k", h=PH)
            link(dve.tensor_copy(r_max[0:R].unsqueeze(2), v[:, :, 0:1]))
            dve.tensor_tensor(v, v, r_max[0:R].unsqueeze(2).broadcast_to((R, PH, TOPK)), ALU.subtract).then_inc(best_ready, 1)
            dve.nop().then_inc(routed, 1)

        def softmax_end(b):
            R = rows(b)
            v = best[0:R, b, :].rearrange("p (h k) -> p h k", h=PH)
            dve.wait_ge(best_exp_ready, b + 1)
            link(dve.tensor_reduce(r_sum[0:R], v, X, ALU.add))
            link(dve.reciprocal(r_sum[0:R], r_sum[0:R]))
            link(dve.tensor_tensor(v, v, r_sum[0:R].unsqueeze(2).broadcast_to((R, PH, TOPK)), ALU.mult))

        def loop(count, body):
            with dve.Fori(0, count) as it:
                steps[1] = it
                body(it)
            steps[1] = None

        loop(PH, lambda it: [route(0, it, part) for part in range(4)])
        softmax_begin(0)
        softmax_end(0)
        for b in range(NB):
            R = rows(b)

            def one_turn(it):
                for k in range(TURN):
                    n, half = it * TURN + (b * STEPS + k), k % 2
                    dve.wait_ge(u_landed[half], it * (TURN // 2 * GS * 16) + (b * STEPS // 2 + k // 2 + 1) * GS * 16)
                    for i in range(GS):
                        rows_i = u_rows[half * GS + i]
                        ins = dve.tensor_tensor_reduce(rows_i, rows_i, h2n[:, b, :], 1.0, 0.0,
                                                       ALU.mult, ALU.add, acts[:, half, i:i + 1])
                    ins.then_inc(u_used, 1)
                    route(b + 1, it, k)
                    dve.wait_ge(gelu_done, n + 1)
                    dve.tensor_tensor(coefs[:, half, :], gelus[:, half, :],
                                      best[:, b, bass.ds(it * (TURN * GS) + k * GS, GS)], ALU.mult).then_inc(coef_ready, 1)

            loop(STEPS // TURN, one_turn)
            softmax_begin(b + 1)
            softmax_end(b + 1)
            dve.wait_ge(v_used, AHEAD + (b + 1) * STEPS)
            if b:
                dve.wait_ge(y_stored, 16 * b)
            for i in range(2):
                h = slice(i * 512, (i + 1) * 512)
                ins = dve.tensor_tensor(y_rows[:, h], psum[:, 2 * (b % 2) + i, :], g2b[:, h], ALU.mult)
            ins.then_inc(sum_read, 1)
            dve.wait_ge(sum_read, b + 1)
            dve.wait_ge(x1_rows_ready, b + 1)
            for i in range(2):
                h = slice(i * 512, (i + 1) * 512)
                ins = dve.tensor_tensor(y_rows[:, h], y_rows[:, h], psum[:, 4 + i, :], ALU.add)
            ins.then_inc(y_ready, 1)
        dve.tensor_copy(eidx_f[0:S, :], eidx[0:S, NB, :]).then_inc(sample_turned, 1)
        dve.wait_ge(sample_turned, 2)
        dve.tensor_copy(idx_s, psum[:, 6, 0:S]).then_inc(sample_routed, 1)
        dve.tensor_copy(gate_s, psum[:, 6, S:2 * S])
        dve.wait_ge(sample_u_landed, 16 * S)
        for s in range(S):
            dve.wait_ge(sample_h_ready, s + 1)
            dve.tensor_tensor_reduce(u_rows[s].rearrange("p (a b) -> p a b", a=2), u_rows[s].rearrange("p (a b) -> p a b", a=2),
                                     psum[:, 2 * (s % 2):2 * (s % 2) + 2, :], 1.0, 0.0,
                                     ALU.mult, ALU.add, act_s[:, s:s + 1]).then_inc(sample_h_used, 1)
        dve.wait_ge(sample_h_used, S)
        dve.nop().then_inc(sample_summed, 1)
        dve.wait_ge(gelu_done, NB * STEPS + 1)
        dve.tensor_tensor(act_s, act_s, gate_s, ALU.mult).then_inc(sample_coef_ready, 1)
        dve.wait_ge(sample_out_ready, 1)
        link(dve.tensor_tensor(out_s, psum[:, 7, 0:C * S].rearrange("p (a b) -> p a b", a=C), mods[:, 40:48, 1:9], ALU.mult))
        dve.tensor_tensor(out_s, out_s, xT[:, :, T:TT], ALU.add).then_inc(sample_coef_ready, 1)
        dve.wait_ge(sample_out_ready, 2)
        dve.wait_ge(y_stored, 16 * NB)
        dve.tensor_copy(y_rows[0:S, :].rearrange("p (a b) -> p a b", a=2), psum[0:S, 4:6, :]).then_inc(y_ready, 1)

    @block.tensor
    def _(pe):
        def begin(key):
            i = order[key]
            if i >= BANKS:
                wait_emptied(pe, plan[i - BANKS][0])
            return bank(key)

        def end(ins):
            ins.then_inc(bank_filled, 1)

        def chunk(key):
            i = chunk_at[key]
            pe.wait_ge(w_loaded[i % RING], slot_rounds(i))
            k = 4 if key[0] in ("wa", "wb") else 8
            return ring[i % RING].rearrange("p (k n) -> p k n", k=k)

        def product(out, pairs):
            for n, (a, b) in enumerate(pairs):
                ins = pe.matmul(out, a, b, start=(n == 0), stop=(n == len(pairs) - 1))
            return ins

        def mean_squares(n):
            pe.wait_ge(squares_ready, n)
            end(product(begin(("ss", n)), [(ones, squares[:, c, 0:T]) for c in range(C)]))
            end(product(begin(("sss", n))[:, 0:S], [(ones, squares[:, c, T:TT]) for c in range(C)]))

        def ada(i):
            w = chunk(("ada", i))
            o = begin(("ada", i))
            for n in range(4):
                ins = product(o[:, n * 9:(n + 1) * 9], [(w[:, k, n * P:(n + 1) * P], scT[:, k, :]) for k in range(8)])
            end(ins)

        pe.wait_ge(consts_loaded, 16)
        pe.wait_ge(small_loaded, 16 * N_SMALL)
        end(pe.transpose(begin(("vecT",))[:, 0:68], vec68[0:68, :], ident[0:68, 0:68]))
        pe.wait_ge(silu_ready, 1)
        o = begin(("cT",))
        for c in range(C):
            ins = pe.transpose(o[:, c * 9:(c + 1) * 9], silu9[0:9, c * P:(c + 1) * P], ident[0:9, 0:9])
        end(ins)
        pe.wait_ge(x_loaded, 16 * 5)
        for c in range(C):
            o = begin(("xT", c))
            for b in range(NB):
                ins = pe.transpose(o[:, b * P:(b + 1) * P], xnat[:, b, c * P:(c + 1) * P], ident)
            end(ins)
        o = begin(("xTs",))
        for c in range(C):
            ins = pe.transpose(o[:, c * S:(c + 1) * S], xnat[0:S, NB, c * P:(c + 1) * P], ident[0:S, 0:S])
        end(ins)
        pe.wait_ge(ones_ready, 1)
        mean_squares(1)
        wait_emptied(pe, ("cT",))
        for i in range(4):
            ada(i)
        pe.wait_ge(h_ready, 1)
        for w, n in (("q", 512), ("kv", 256), ("p", 512)):
            wt = chunk((w,))
            for b in range(NB + 1):
                end(product(begin((w, b))[0:rows(b), 0:n], [(hT[:, k, cols(b)], wt[:, k, 0:n]) for k in range(C)]))
        for i in range(4):
            w = chunk(("gate", i))
            for n in range(4):
                end(product(begin(("gate", 4 * i + n)), [(w[:, k, n * P:(n + 1) * P], hT[:, k, 0:T]) for k in range(C)]))
            o = begin(("gates", i))
            for n in range(4):
                ins = product(o[:, n * S:(n + 1) * S], [(w[:, k, n * P:(n + 1) * P], hT[:, k, T:TT]) for k in range(C)])
            end(ins)
        pe.wait_ge(qk_normed, 1)
        for b in range(NB):
            o = begin(("qT", b))
            for j in range(G):
                ins = pe.transpose(o[:, j * P:(j + 1) * P], zqk[:, b, j * P:(j + 1) * P], ident)
            end(ins)
            end(pe.transpose(begin(("kT", b))[:, 0:P], zqk[:, b, 512:640], ident))
        o = begin(("qkTs",))
        for j in range(G + 1):
            ins = pe.transpose(o[:, j * S:(j + 1) * S], zqk[0:S, NB, j * P:(j + 1) * P], ident[0:S, 0:S])
        end(ins)

        def scores(b):
            wait_emptied(pe, ("kT", b))
            lo = P if b == 0 else 0
            for j in range(G):
                o = begin(("s", b, j))
                r = slice(j // 2 * HD, (j // 2 + 1) * HD)
                for i in range(2):
                    ins = pe.matmul(o[:, i * 2 * P + lo:(i + 1) * 2 * P], qkT[r, j % 2 * 2 + i, cols(b)],
                                    qkT[r, 4, (b - 1) * P + lo:(b + 1) * P], start=True, stop=True)
                end(ins)

        def pooled(b):
            own = K_OWN if b else K_FIRST
            o = begin(("d", b))
            for g in range(PG):
                gs = slice(g * P, (g + 1) * P)
                pairs = [(zp[:, b, gs], kc[:, own + g * P:own + (g + 1) * P])]
                if b:
                    pairs += [(zp[:, b - 1, gs], kc[:, K_PREV + g * P:K_PREV + (g + 1) * P])]
                ins = product(o[:, gs], pairs)
            end(ins)

        def values(b):
            halves = (1,) if b == 0 else (0, 1)
            pe.wait_ge(probs_ready, b + 1)
            for kv in range(KV):
                for h in halves:
                    o = begin(("pt", b, kv, h))
                    for j in range(G):
                        ins = pe.transpose(o[:, j * P:(j + 1) * P], sS[b % 2][:, kv * G + j, h * P:(h + 1) * P], ident)
                    end(ins)
                o = begin(("o", b, kv))
                wait_emptied(pe, ("pt", b, kv, 1))
                end(product(o[kv * HD:(kv + 1) * HD, :], [(zv[:, b - 1 + h, kv * HD:(kv + 1) * HD], pT[:, h, :]) for h in halves]))

        scores(0)
        pooled(0)
        scores(1)
        pooled(1)
        values(0)
        scores(2)
        pooled(2)
        values(1)
        scores(3)
        pooled(3)
        values(2)
        pe.wait_ge(tail_loaded, 32)
        o = begin(("ds",))
        for g in range(PG):
            ins = pe.matmul(o[:, g * S:(g + 1) * S], pext[:, g * P:(g + 1) * P], kc[:, K_POOLS + g * S:K_POOLS + (g + 1) * S],
                            start=True, stop=True)
        end(ins)
        values(3)
        for i in (4, 5):
            ada(i)
        pe.wait_ge(cache_loaded, 64)
        for i in range(2):
            o = begin(("ktT", i))
            for b in range(4):
                ins = pe.transpose(o[:, b * P:(b + 1) * P], ktile[:, 4 * i + b, :], ident)
            end(ins)
        end(pe.transpose(begin(("k0T",))[:, 0:S], k0[0:S, :], ident[0:S, 0:S]))
        wait_emptied(pe, ("k0T",))
        for kv in range(KV):
            r = slice(kv * HD, (kv + 1) * HD)
            for h in range(2):
                o = begin(("sc4", kv, h))
                for b in range(4):
                    s = 4 * h + b
                    ins = pe.matmul(o[0:G, b * P:(b + 1) * P], qkT[r, 0:G, T + s], kTs[r, s, :], start=True, stop=True)
                end(ins)
        for kv in range(KV):
            o = begin(("sc0", kv))
            r = slice(kv * HD, (kv + 1) * HD)
            for s in range(S):
                ins = pe.matmul(o[0:G, s:s + 1], qkT[r, 0:G, T + s], k0T[r, s:s + 1], start=True, stop=True)
            end(ins)
        wait_emptied(pe, ("ds",))
        for g in range(PG):
            end(pe.matmul(begin(("y", g)), wpool[:, g, :], dT[:, g, 0:T], start=True, stop=True))
        o = begin(("ys",))
        for g in range(PG):
            ins = pe.matmul(o[:, g * S:(g + 1) * S], wpool[:, g, :], dT[:, g, T:TT], start=True, stop=True)
        end(ins)
        wa, wb = chunk(("wa",)), chunk(("wb",))
        wait_emptied(pe, ("y", PG - 1))
        for n in range(C):
            ns = slice(n * P, (n + 1) * P)
            end(product(begin(("A", n)), [(wa[:, k, ns], attT[:, k, 0:T]) for k in range(4)]))
            end(product(begin(("B", n)), [(wb[:, k, ns], bT[:, k, 0:T]) for k in range(4)]))
        pe.wait_ge(probs_ready, NB + 1)
        o = begin(("pts",))
        for i in range(16):
            pe.transpose(o[:, i * G:(i + 1) * G], sSs[0:G, i, 1:], ident[0:G, 0:G])
        for i in range(16):
            ins = pe.transpose(o[0:1, 64 + i * G:64 + (i + 1) * G], sSs[0:G, i, 0:1], ident[0:G, 0:G])
        end(ins)
        pe.wait_ge(oldest_v_loaded, 16)
        o = begin(("os",))
        wait_emptied(pe, ("pts",))
        for kv in range(KV):
            r = slice(kv * HD, (kv + 1) * HD)
            for s in range(S):
                i = (kv * S + s) * G
                out = o[r, s * G:(s + 1) * G]
                pe.matmul(out, vtile[:, s, r], pTs[:, i:i + G], start=True, stop=False)
                ins = pe.matmul(out, v0[0:1, s, r], pTs[0:1, 64 + i:64 + i + G], start=False, stop=True)
        end(ins)
        o = begin(("ABs",))
        wait_emptied(pe, ("os",))
        wait_emptied(pe, ("ys",))
        for n in range(C):
            ns = slice(n * P, (n + 1) * P)
            product(o[:, n * S:(n + 1) * S], [(wa[:, k, ns], attT[:, k, T:TT]) for k in range(4)])
            ins = product(o[:, 64 + n * S:64 + (n + 1) * S], [(wb[:, k, ns], bT[:, k, T:TT]) for k in range(4)])
        end(ins)
        pe.wait_ge(merged_ready, C + 1)
        for n in range(C):
            w = chunk(("wo", n // 4))
            ns = slice(n % 4 * P, (n % 4 + 1) * P)
            end(product(begin(("o2", n)), [(w[:, k, ns], mT[:, k, 0:T]) for k in range(C)]))
        o = begin(("o2s",))
        for n in range(C):
            w = chunk(("wo", n // 4))
            ns = slice(n % 4 * P, (n % 4 + 1) * P)
            ins = product(o[:, n * S:(n + 1) * S], [(w[:, k, ns], mT[:, k, T:TT]) for k in range(C)])
        end(ins)
        for i in range(6, 12):
            ada(i)
        pe.wait_ge(subkeys_loaded, 16)
        for i in range(4):
            o = begin(("skT", i))
            for m in range(4):
                ins = pe.transpose(o[:, m * P:(m + 1) * P], sk_rows[:, 4 * i + m, :], ident)
            end(ins)
        mean_squares(2)
        wait_emptied(pe, ("ada", 11))
        for i in range(2):
            o = begin(("g2b", i))
            for c in range(4):
                ins = pe.matmul(o[:, c * P:(c + 1) * P], mods[:, 40 + 4 * i + c, 0:1].broadcast_to((P, P)), ident, start=True, stop=True)
            end(ins)
        pe.wait_ge(h_ready, 2)

        def subkey_scores(m):
            o = begin(("sc", m))
            wait_emptied(pe, ("pq", m))
            for b in range(NB):
                ins = pe.matmul(o[:, b * P:(b + 1) * P], pq[:, m % 2, b * P:(b + 1) * P], skT[:, m, :], start=True, stop=True)
            end(ins)

        for m in range(16):
            w = chunk(("wq", m // 4))
            if m % 4 == 0:
                o = begin(("pqs", m // 4))
                for n in range(4):
                    ins = product(o[:, n * S:(n + 1) * S], [(w[:, k, n * P:(n + 1) * P], hT[:, k, T:TT]) for k in range(C)])
                end(ins)
            ns = slice(m % 4 * P, (m % 4 + 1) * P)
            end(product(begin(("pq", m)), [(w[:, k, ns], hT[:, k, 0:T]) for k in range(C)]))
            if m % 4 == 0:
                o = begin(("scs", m // 4))
                wait_emptied(pe, ("pqs", m // 4))
                for n in range(4):
                    ins = pe.matmul(o[0:S, n * P:(n + 1) * P], pqs[:, n * S:(n + 1) * S], skT[:, m + n, :], start=True, stop=True)
                end(ins)
            if m:
                subkey_scores(m - 1)
        subkey_scores(15)
        for b in range(NB + 1):
            for i in range(2):
                o = begin(("h2n", b, i))
                for c in range(4):
                    ins = pe.transpose(o[0:rows(b), c * P:(c + 1) * P], hT[:, 4 * i + c, cols(b)], ident)
                end(ins)
        for key, _ in plan[-BANKS:]:
            wait_emptied(pe, key)
        pe.nop().then_inc(v_used, AHEAD)
        for b in range(NB):
            pe.wait_ge(u_used, AHEAD)
            if b >= 2:
                pe.wait_ge(sum_read, b - 1)
            for i in range(2):
                pe.matmul(psum[:, 2 * (b % 2) + i, :], zeros, zeros[:, 0:1].broadcast_to((P, 512)),
                          start=True, stop=False, skip_group_check=True)
            if b:
                pe.wait_ge(y_ready, b)
            for i in range(2):
                for c in range(4):
                    ins = pe.transpose(psum[:, 4 + i, c * P:(c + 1) * P], xT[:, 4 * i + c, cols(b)], ident)
            ins.then_inc(x1_rows_ready, 1)
            with pe.Fori(0, STEPS // TURN) as it:
                for k in range(TURN):
                    n, half = it * TURN + (b * STEPS + k), k % 2
                    pe.wait_ge(v_landed[half], it * (TURN // 2 * GS * 16) + (b * STEPS // 2 + k // 2 + 1) * GS * 16)
                    pe.wait_ge(diag_ready, n + 1)
                    for i in range(GS):
                        for h in range(2):
                            ins = pe.matmul(psum[:, 2 * (b % 2) + h, :], diags[:, half * GS + i, :],
                                            v_rows[half * GS + i][:, h * 512:(h + 1) * 512],
                                            start=False, stop=False, skip_group_check=True)
                    ins.then_inc(v_used, 1)
        pe.wait_ge(sample_turned, 1)
        pe.transpose(psum[:, 6, 0:S], eidx_f[0:S, :], ident[0:S, 0:S])
        pe.transpose(psum[:, 6, S:2 * S], best[0:S, NB, :], ident[0:S, 0:S]).then_inc(sample_turned, 1)
        pe.wait_ge(sum_read, NB)
        for s in range(S):
            if s >= 2:
                pe.wait_ge(sample_h_used, s - 1)
            for h in range(2):
                ins = pe.matmul(psum[:, 2 * (s % 2) + h, :], ident[0:S, s:s + 1].broadcast_to((S, P)),
                                h2n[0:S, NB, h * 512:(h + 1) * 512], start=True, stop=True)
            ins.then_inc(sample_h_ready, 1)
        pe.wait_ge(sample_v_landed, 16 * S)
        pe.wait_ge(sample_coef_ready, 1)
        for s in range(S):
            for c in range(C):
                ins = pe.matmul(psum[:, 7, c * S + s:c * S + s + 1], v_rows[s][:, c * P:(c + 1) * P], act_s[:, s:s + 1],
                                start=True, stop=True)
        ins.then_inc(sample_out_ready, 1)
        pe.wait_ge(sample_coef_ready, 2)
        pe.wait_ge(y_ready, NB)
        for c in range(C):
            ins = pe.transpose(psum[0:S, 4 + c // 4, c % 4 * P:(c % 4 + 1) * P], out_s[:, c, :], ident)
        ins.then_inc(sample_out_ready, 1)

    block.__exit__(None, None, None)


_INS = ['x_prompt', 'x_sample', 'cache_k', 'cache_v', 'state_pool', 'c_prompt', 'c_sample', 'norm1_g', 'norm2_g', 'w_ada',
        'b_ada', 'w_in', 'q_norm_g', 'k_norm_g', 'attn_sinks', 'w_pool', 'pool_scale', 'w_branch_attn', 'w_branch_pool',
        'w_out', 'peer_wq', 'peer_subkeys', 'peer_u', 'peer_v']
_OUTS = [(1, T, D), (S, 1, D), (1, 1, WIN, KV, HD), (1, 1, WIN, KV, HD), (1, 1, HIST, PW),
         (1, S, WIN, KV, HD), (1, S, WIN, KV, HD), (1, S, HIST, PW)]


def kernel(**inputs):
    import concourse.bacc as bacc
    from concourse.bass_utils import run_bass_kernel_spmd

    nc = bacc.Bacc("TRN2", target_bir_lowering=False, num_devices=1)
    arrays, args = {}, []
    for name in _INS:
        a = np.ascontiguousarray(inputs[name])
        arrays[f"in_{name}"] = a
        args.append(nc.dram_tensor(f"in_{name}", a.shape, mybir.dt.from_np(a.dtype), kind="ExternalInput").ap())
    arrays["in_consts"] = constants()
    args.append(nc.dram_tensor("in_consts", arrays["in_consts"].shape, F32, kind="ExternalInput").ap())
    for i, shape in enumerate(_OUTS):
        args.append(nc.dram_tensor(f"out_{i}", shape, F32, kind="ExternalOutput").ap())
    decoder_layer(nc, *args)
    r = run_bass_kernel_spmd(nc, [arrays], core_ids=[0])
    return tuple(r.results[0][f"out_{i}"] for i in range(len(_OUTS)))
```

```python
import numpy as np

import concourse.bass as bass
from concourse import mybir

F32 = mybir.dt.float32
I32 = mybir.dt.int32
U32 = mybir.dt.uint32
ALU = mybir.AluOpType
ACT = mybir.ActivationFunctionType
X = mybir.AxisListType.X

P = 128
D = 1024
C = D // P
T = 512
NB = T // P
S = 8
TT = T + S
HT = TT // 2
HEADS, KV, HD = 8, 2, 64
G = HEADS // KV
WIN = 128
PG = 4
POOL_WINDOWS = (2, 4, 8, 16)
HIST = 15
PW = PG * P
PH = 8
TOPK = 16
NK = 128
SLOTS = PH * TOPK
EPS = 1e-6
NEG = -1e30
BANKS = 8
CHUNK = 8 * 512
RING = 3
GS = 4
TURN = 4

K_ID = 0
K_BIAS = K_ID + P
K_OWN = K_BIAS + HEADS * 2 * P
K_FIRST = K_OWN + PG * P
K_PREV = K_FIRST + PG * P
K_POOLS = K_PREV + PG * P
K_IOTA = K_POOLS + PG * S
K_BIASS = K_IOTA + TOPK
K_END = K_BIASS + KV * (WIN + 1)


def constants():
    k = np.zeros((P, K_END), np.float32)
    k[:, K_ID:K_BIAS] = np.eye(P)
    q, s = np.arange(P)[:, None], np.arange(2 * P)[None, :]
    dist = q + P - s
    valid = (dist >= 0) & (dist <= WIN)
    for kv in range(KV):
        for j in range(G):
            slope = 2.0 ** -(kv * G + j + 1)
            o = K_BIAS + (kv * G + j) * 2 * P
            k[:, o:o + 2 * P] = np.where(valid, -slope * dist, NEG)
            o = K_BIASS + kv * (WIN + 1)
            k[j, o:o + WIN + 1] = -slope * (WIN - np.arange(WIN + 1))
    s, t = np.arange(P)[:, None], np.arange(P)[None, :]
    for g, w in enumerate(POOL_WINDOWS):
        near = (t - s >= 0) & (t - s < w)
        k[:, K_OWN + g * P:K_OWN + (g + 1) * P] = near / w - (s == t)
        k[:, K_FIRST + g * P:K_FIRST + (g + 1) * P] = near / np.minimum(t + 1, w) - (s == t)
        k[:, K_PREV + g * P:K_PREV + (g + 1) * P] = (t + P - s < w) / w
        for r in range(HIST + 1):
            for b in range(S):
                k[r * S + b, K_POOLS + g * S + b] = (r > HIST - w) / w - (r == HIST)
    k[:, K_IOTA:K_IOTA + TOPK] = np.arange(TOPK)
    return k


def bank_plan():
    both = range(2)
    def ada_rows(i):
        return [(("ada_rows", i), "A")]

    def ada(i):
        return [(("ada", i), "V")]

    plan = [(("vecT",), "A"), (("cT",), "A")]
    plan += [(("xT", c), "A") for c in range(C)] + [(("xTs",), "A")]
    plan += [(("ss", 1, h), "V") for h in both]
    plan += ada_rows(0) + ada_rows(1) + ada(0) + ada_rows(2) + ada(1) + ada_rows(3) + ada(2) + ada(3)
    plan += [((w, b), "A") for w in ("q", "kv", "p") for b in range(NB + 1)]

    def gates(ms):
        return [(("gate", m, h), "A") for m in ms for h in both]

    def scores(b):
        return [(("s", b, j), "V") for j in range(G)]

    def values(b):
        halves = (1,) if b == 0 else (0, 1)
        return [k for kv in range(KV) for k in [(("pt", b, kv, h), "A") for h in halves] + [(("o", b, kv), "A")]]

    plan += gates(range(8))
    for b in range(NB):
        plan += [(("qT", b), "A"), (("kT", b), "A")]
    plan += [(("qkTs",), "A")]
    plan += scores(0) + [(("d", 0), "A")] + gates((8, 9)) + scores(1) + [(("d", 1), "A")] + gates((10, 11)) + values(0)
    plan += scores(2) + [(("d", 2), "A")] + gates((12, 13)) + values(1) + scores(3) + [(("d", 3), "A")] + gates((14, 15)) + values(2)
    plan += [(("ds",), "A")] + ada_rows(4) + values(3) + ada(4) + ada_rows(5) + ada_rows(6) + ada(5) + ada(6)
    plan += [(("ktT", i), "A") for i in range(2)] + [(("k0T",), "A")]
    plan += [(("sc4", kv, h), "V") for kv in range(KV) for h in range(2)] + [(("sc0", kv), "V") for kv in range(KV)]
    plan += [(("y", g, h), "A") for h in both for g in range(PG)]
    plan += [((w, n, 0), "V") for n in range(C) for w in ("A", "B")]
    plan += [(("pts",), "A"), (("os",), "A")]
    plan += [((w, n, 1), "V") for n in range(C) for w in ("A", "B")] + ada_rows(7) + ada(7)
    plan += [(("o2", n, h), "V") for n in range(C) for h in both]
    plan += [(("skT", i), "A") for i in range(4)]
    plan += [(("ss", 2, h), "V") for h in both]
    plan += ada_rows(8) + ada_rows(9) + ada(8) + ada(9) + ada_rows(10) + ada_rows(11) + ada(10) + ada(11)
    plan += [(("g2b", i), "A") for i in range(2)]
    plan += [(("h2n", b, i), "A") for b in range(NB + 1) for i in range(2)]
    for m in range(16):
        plan += [(("pq", m, h), "A") for h in both]
        if m:
            plan += [(("sc", m - 1), "V"), (("scs", m - 1), "A")]
    plan += [(("sc", 15), "V"), (("scs", 15), "A")]
    return plan


def weight_chunks():
    chunks = [(("ada", i), ("ada_rows", i)) for i in range(4)]
    chunks += [((w,), (w, NB)) for w in ("q", "kv", "p")]
    chunks += [(("gate", i), ("gate", 4 * i + 3, 1)) for i in range(4)]
    chunks += [(("ada", i), ("ada_rows", i)) for i in (4, 5, 6)]
    chunks += [(("wa",), ("B", C - 1, 1)), (("wb",), ("B", C - 1, 1))]
    chunks += [(("ada", 7), ("ada_rows", 7))]
    chunks += [(("wo", 0), ("o2", 3, 1)), (("wo", 1), ("o2", 7, 1))]
    chunks += [(("ada", i), ("ada_rows", i)) for i in (8, 9, 10, 11)]
    chunks += [(("wq", i), ("pq", 4 * i + 3, 1)) for i in range(4)]
    return chunks


def decoder_layer(nc, x_prompt, x_sample, cache_k, cache_v, state_pool, c_prompt, c_sample, norm1_g,
                  norm2_g, w_ada, b_ada, w_in, q_norm_g, k_norm_g, attn_sinks, w_pool, pool_scale,
                  w_branch_attn, w_branch_pool, w_out, peer_wq, peer_subkeys, peer_u, peer_v, consts,
                  y_prompt, y_sample, k_win_p, v_win_p, pool_p, k_win_s, v_win_s, pool_s):
    plan = bank_plan()
    order = {key: i for i, (key, _) in enumerate(plan)}
    taker = dict(plan)
    turn = {}
    for who in "AV":
        for i, key in enumerate(k for k, w in plan if w == who):
            turn[key] = i + 1
    chunks = weight_chunks()
    chunk_at = {key: i for i, (key, _) in enumerate(chunks)}

    def sem(name):
        return nc.alloc_semaphore(name)

    bank_filled, emptied_by_act, emptied_by_dve = sem("bank_filled"), sem("emptied_by_act"), sem("emptied_by_dve")
    x_loaded, c_loaded, consts_loaded, small_loaded = sem("x_loaded"), sem("c_loaded"), sem("consts_loaded"), sem("small_loaded")
    ident_loaded, vecs_loaded = sem("ident_loaded"), sem("vecs_loaded")
    subkeys_loaded, cache_loaded, oldest_v_loaded, tail_loaded = sem("subkeys_loaded"), sem("cache_loaded"), sem("oldest_v_loaded"), sem("tail_loaded")
    windows_stored, y_stored = sem("windows_stored"), sem("y_stored")
    w_loaded = [sem(f"w_loaded{i}") for i in range(RING)]
    act_step, dve_step = sem("act_step"), sem("dve_step")
    silu_ready, ones_ready, filler_ready = sem("silu_ready"), sem("ones_ready"), sem("filler_ready")
    squares_ready, root_ready, h_ready = sem("squares_ready"), sem("root_ready"), sem("h_ready")
    qk_mean_ready, qk_root_ready, qk_normed = sem("qk_mean_ready"), sem("qk_root_ready"), sem("qk_normed")
    max_ready, exps_ready, probs_ready = sem("max_ready"), sem("exps_ready"), sem("probs_ready")
    merged_ready, x1_ready = sem("merged_ready"), sem("x1_ready")
    best_ready, best_exp_ready, routed, gates_ready = sem("best_ready"), sem("best_exp_ready"), sem("routed"), sem("gates_ready")
    u_landed = [sem(f"u_landed_half{i}") for i in range(2)]
    v_landed = [sem(f"v_landed_half{i}") for i in range(2)]
    sample_routed, sample_u_landed, sample_v_landed = sem("sample_routed"), [sem(f"sample_u_landed{q}") for q in range(2)], [sem(f"sample_v_landed{q}") for q in range(2)]
    sample_turned, sample_summed, sample_coef_ready, sample_out_ready = sem("sample_turned"), sem("sample_summed"), sem("sample_coef_ready"), sem("sample_out_ready")
    sample_h_ready, sample_h_used = sem("sample_h_ready"), sem("sample_h_used")
    sample_y_ready, sample_h_free = sem("sample_y_ready"), sem("sample_h_free")
    pad_ready = sem("pad_ready")
    u_used, v_used, idx_copied = sem("u_used"), sem("v_used"), sem("idx_copied")
    gelu_done, coef_ready, diag_ready = sem("gelu_done"), sem("coef_ready"), sem("diag_ready")
    sum_read, x1_rows_ready, y_ready = sem("sum_read"), sem("x1_rows_ready"), sem("y_ready")

    AR = 53200
    arena = nc.alloc_sbuf_tensor("arena", [P, AR], F32)
    top = [0]

    def at(off, n, a=None):
        v = arena[:, off:off + n]
        return v if a is None else v.rearrange("p (a b) -> p a b", a=a)

    def take(n):
        top[0] += n
        assert top[0] <= AR, top[0]
        return top[0] - n

    kc = at(take(K_END), K_END)
    ident = kc[:, K_ID:K_ID + P]
    vecT = at(take(68), 68)
    ones = at(take(P), P)
    scT = at(take(C * 9), C * 9, C)
    gqk = at(take(2 * HD), 2 * HD, 2)
    mods = at(take(48 * 9), 48 * 9, 48)
    sinks = at(take(8), 8)
    sinks4 = at(take(2), 2)
    smod = at(take(9 * C), 9 * C, C)
    res_s = at(take(S), S)
    nmax, ssum, srec, ssink = (at(take(8), 8) for _ in range(4))
    xT = at(take(C * TT), C * TT, C)
    hT = at(take(C * TT), C * TT, C)
    o_ring = take(RING * CHUNK)
    ring = [at(o_ring + i * CHUNK, CHUNK) for i in range(RING)]
    o_shared = top[0]
    o_ga, o_gb = take(C * TT), take(C * TT)
    ga, gb = at(o_ga, C * TT, C), at(o_gb, C * TT, C)
    squares = at(o_gb, C * TT, C)
    o_att, o_d = take(G * TT), take(PG * TT)
    attT, dT = at(o_att, G * TT, G), at(o_d, PG * TT, PG)
    msq, root = at(o_att, TT), at(o_att + TT, TT)
    c9, silu9 = at(o_d, D), at(o_d + D, D)
    v0 = at(o_d, S * P, S)
    o_z = take(6400)
    zqk, zv, zp = at(o_z, 3200, 5), at(o_z + 3200, 640, 5), at(o_z + 3840, 2560, 5)
    xnat = at(o_z, 5 * D, 5)
    pext = zp[:, 0, :]
    mT = at(o_z, C * TT, C)
    o_qkT = take(5 * TT)
    qkT = at(o_qkT, 5 * TT, 5)
    bT = at(o_qkT, PG * TT, PG)
    vec68 = at(o_qkT, P)
    o_q = take(5184)
    zsq, qk_rms = at(o_q, 3200), at(o_q + 3200, 50)
    sS = [at(o_q, 2048, 8), at(o_q + 2048, 2048, 8)]
    pT = at(o_q + 4096, 1024, 2)
    o_h = o_ring - C * TT
    ktile, vtile = at(o_h, 1024, S), at(o_h + 1024, 1024, S)
    ada_places = [o_q + i * 512 for i in range(4)] + [o_h + 2048 + i * 512 for i in range(3)] + [o_q + i * 512 for i in range(5)]
    ada_rows = [at(o, 512) for o in ada_places]
    kTs = at(o_q + 2048, 1024, S)
    sSs = at(o_q + 3072, 16 * 129, 16)
    k0, k0T = at(take(P), P), at(take(S), S)
    pTs, smisc = at(take(P), P), at(take(4 * 16), 64, 4)
    wpool = at(take(PG * P), PG * P, PG)
    top[0] = o_shared
    o_sk = take(4096)
    sk_rows, skT = at(o_sk, 2048, 16), at(o_sk + 2048, 2048, 16)
    sc = at(take(5 * 16 * NK), 5 * 16 * NK, 80)
    h_all = at(o_sk + 4096, S * D, S)
    h2n = at(take(5 * D), 5 * D, 5)
    g2b = at(take(D), D)
    o_diag = take(2 * GS * P)
    diags = at(o_diag, 2 * GS * P, 2 * GS)
    pq = at(take(2 * TT), 2 * TT, 2)
    eidx = at(take(5 * SLOTS), 5 * SLOTS, 5).bitcast(I32)
    best = at(take(5 * SLOTS), 5 * SLOTS, 5)
    r_in, r_cut = at(take(2 * NK), 2 * NK, 2), at(take(2 * NK), 2 * NK, 2)
    r_val = at(take(2 * TOPK), 2 * TOPK, 2)
    r_idx = at(take(2 * TOPK), 2 * TOPK, 2).bitcast(U32)
    r_idxf = at(take(2 * TOPK), 2 * TOPK, 2)
    r_cand, r_cand2 = at(take(TOPK * TOPK), TOPK * TOPK, TOPK), at(take(TOPK * TOPK), TOPK * TOPK)
    r_best = at(take(TOPK), TOPK)
    r_pos = at(take(TOPK), TOPK).bitcast(U32)
    r_half = at(take(2 * TOPK), 2 * TOPK, 2).bitcast(U32)
    r_halff = at(take(2 * TOPK), 2 * TOPK, 2)
    r_hot = at(take(2 * TOPK * TOPK), 2 * TOPK * TOPK, 2 * TOPK)
    r_pick = at(take(2 * TOPK), 2 * TOPK, 2)
    r_e = at(take(TOPK), TOPK)
    r_max, r_sum = at(take(PH), PH), at(take(PH), PH)
    zeros = at(take(P), P)
    y_rows = at(take(D), D)
    acts, gelus, coefs = (at(take(2 * GS), 2 * GS, 2) for _ in range(3))
    idx_s, gate_s, act_s, out_s = at(take(S), S).bitcast(I32), at(take(S), S), at(take(S), S), at(take(C * S), C * S, C)
    eidx_f = at(take(SLOTS), SLOTS)
    pool_pad = at(take(3), 3)
    idx_now = at(take(TURN * GS), TURN * GS, TURN).bitcast(I32)
    u_rows = [at(o_ring + i * D, D) for i in range(2 * GS)]
    v_rows = [at(o_ring + (2 * GS + i) * D, D) for i in range(2 * GS)]
    assert 4 * GS * D <= RING * CHUNK + 4096

    psum = nc.alloc_psum_tensor("psum", [P, BANKS, 512], F32)

    def bank(key):
        return psum[:, order[key] % BANKS, :]

    def wait_filled(eng, key):
        eng.wait_ge(bank_filled, order[key] + 1)

    def wait_emptied(eng, key):
        eng.wait_ge(emptied_by_act if taker[key] == "A" else emptied_by_dve, turn[key])

    def cols(b):
        return slice(b * P, (b + 1) * P) if b < NB else slice(T, TT)

    def rows(b):
        return P if b < NB else S

    def half(h):
        return slice(h * HT, (h + 1) * HT)

    last = plan[-1][0]
    N_SMALL = 7
    STEPS = SLOTS // GS
    EARLY = 4
    AHEAD = 2

    block = nc.Block()
    block.__enter__()

    @block.sync
    def _(sp):
        sp.dma_start(c9[0:1, :], c_prompt).then_inc(c_loaded, 16)
        sp.dma_start(c9[1:9, :], c_sample).then_inc(c_loaded, 16)
        sp.dma_start(ident, consts[:, 0:P]).then_inc(ident_loaded, 16)
        sp.dma_start(vec68[0:48, :], b_ada[0].rearrange("(a b) -> a b", b=P)).then_inc(vecs_loaded, 16)
        sp.dma_start(vec68[48:56, :], norm1_g[0].rearrange("(a b) -> a b", b=P)).then_inc(vecs_loaded, 16)
        sp.dma_start(vec68[56:64, :], norm2_g[0].rearrange("(a b) -> a b", b=P)).then_inc(vecs_loaded, 16)
        sp.dma_start(vec68[64:68, :], pool_scale[0].rearrange("(a b) -> a b", b=P)).then_inc(vecs_loaded, 16)
        for b in range(NB):
            sp.dma_start(xnat[:, b, :], x_prompt[0, b * P:(b + 1) * P, :]).then_inc(x_loaded, 16)
        sp.dma_start(xnat[0:S, NB, :], x_sample[:, 0, :]).then_inc(x_loaded, 16)
        win = w_in[0].rearrange("(k p) n -> p k n", p=P)
        wad = w_ada[0].rearrange("(k p) n -> p k n", p=P)
        wqd = peer_wq[0].rearrange("(k p) n -> p k n", p=P)
        starts = {"q": (0, 512), "kv": (512, 256), "p": (768, 512)}
        for i, (key, _) in enumerate(chunks):
            if i >= RING:
                wait_filled(sp, chunks[i - RING][1])
            r = ring[i % RING]
            wide = r.rearrange("p (k n) -> p k n", k=8)
            if key[0] == "ada":
                src, dst = wad[:, :, key[1] * 512:(key[1] + 1) * 512], wide
            elif key[0] in starts:
                c0, n = starts[key[0]]
                src, dst = win[:, :, c0:c0 + n], wide[:, :, 0:n]
            elif key[0] == "gate":
                c0 = 1280 + key[1] * 512
                src, dst = win[:, :, c0:c0 + 512], wide
            elif key[0] == "wq":
                src, dst = wqd[:, :, key[1] * 512:(key[1] + 1) * 512], wide
            elif key[0] == "wo":
                src, dst = w_out[0].rearrange("(k p) n -> p k n", p=P)[:, :, key[1] * 512:(key[1] + 1) * 512], wide
            elif key[0] == "wb":
                src, dst = w_branch_pool[0].rearrange("(k p) n -> p k n", p=P), r.rearrange("p (k n) -> p k n", k=4)
            else:
                dst = r.rearrange("p (k n) -> p k n", k=4)
                for kv in range(KV):
                    half = w_branch_attn[0, kv * G * HD:(kv + 1) * G * HD, :].rearrange("(j e) n -> e j n", j=G)
                    sp.dma_start(dst[kv * HD:(kv + 1) * HD], half).then_inc(w_loaded[i % RING], 8 * 2)
                continue
            sp.dma_start(dst, src).then_inc(w_loaded[i % RING], 16)
        for b in range(NB + 1):
            sp.wait_ge(y_ready, b + 1)
            dst = y_prompt[0, b * P:(b + 1) * P, :] if b < NB else y_sample[:, 0, :]
            sp.dma_start(dst, y_rows[0:rows(b), :]).then_inc(y_stored, 16)
        sp.wait_ge(y_stored, 16 * (NB + 1))

    def slot_rounds(i):
        n = 0
        for j in range(i % RING, i + 1, RING):
            n += 2 if chunks[j][0] == ("wa",) else 1
        return 16 * n

    @block.gpsimd
    def _(pool):
        pool.dma_start(gqk[:, 0, :], q_norm_g[0:1, :].broadcast_to((P, HD))).then_inc(small_loaded, 16)
        pool.dma_start(gqk[:, 1, :], k_norm_g[0:1, :].broadcast_to((P, HD))).then_inc(small_loaded, 16)
        pool.dma_start(sinks, attn_sinks[0:1, :].broadcast_to((P, HEADS))).then_inc(small_loaded, 16)
        for kv in range(KV):
            pool.dma_start(sinks4[0:G, kv:kv + 1],
                           attn_sinks[0, kv * G:(kv + 1) * G].rearrange("(j o) -> j o", o=1), allow_slow_non_contiguous=True).then_inc(small_loaded, 16)
        pool.dma_start(wpool, w_pool[0].rearrange("g c e -> c g e")).then_inc(small_loaded, 16)
        pool.dma_start(k0[0:S, :], cache_k[0, :, 0].rearrange("b h e -> b (h e)")).then_inc(small_loaded, 16)
        pool.dma_start(kc[:, P:], consts[:, P:]).then_inc(consts_loaded, 16)
        pool.wait_ge(qk_normed, 1)
        pool.dma_start(k_win_p[0, 0].rearrange("t h e -> t (h e)"), zqk[:, NB - 1, 512:640]).then_inc(windows_stored, 16)
        pool.dma_start(v_win_p[0, 0].rearrange("t h e -> t (h e)"), zv[:, NB - 1, :]).then_inc(windows_stored, 16)
        pool.dma_start(pool_p[0, 0], zp[P - HIST:P, NB - 1, :]).then_inc(windows_stored, 16)
        wait_filled(pool, ("d", 1))
        pool.dma_start(pext[0:HIST * S, :], state_pool[0].rearrange("b r c -> r b c")).then_inc(tail_loaded, 16)
        pool.dma_start(pext[HIST * S:P, :], zp[0:S, NB, :]).then_inc(tail_loaded, 16)
        pool.wait_ge(tail_loaded, 32)
        pool.dma_start(pool_s[0].rearrange("b r c -> r b c"), pext[S:P, :]).then_inc(windows_stored, 16)
        wait_filled(pool, ("gate", 2 * C - 1, 1))
        for cache, tile, new in ((cache_k, ktile, zqk[0:S, NB, 512:640]), (cache_v, vtile, zv[0:S, NB, :])):
            pool.dma_start(tile[0:WIN - 1], cache[0, :, 1:WIN].rearrange("b s h e -> s b (h e)")).then_inc(cache_loaded, 16)
            pool.dma_start(tile[WIN - 1:WIN], new).then_inc(cache_loaded, 16)
        pool.wait_ge(cache_loaded, 64)
        pool.dma_start(k_win_s[0].rearrange("b s h e -> s b (h e)"), ktile).then_inc(windows_stored, 16)
        pool.dma_start(v_win_s[0].rearrange("b s h e -> s b (h e)"), vtile).then_inc(windows_stored, 16)
        wait_filled(pool, ("y", PG - 1, 1))
        pool.dma_start(v0[0:1], cache_v[0:1, :, 0].rearrange("o b h e -> o b (h e)")).then_inc(oldest_v_loaded, 16)
        pool.wait_ge(merged_ready, 2 * C)
        pool.dma_start(sk_rows, peer_subkeys[0].rearrange("h c n e -> n (h c) e")).then_inc(subkeys_loaded, 16)
        wait_filled(pool, last)
        pool.memset(pool_pad, 0.0).then_inc(pad_ready, 1)
        pool.wait_ge(pad_ready, 1)
        def gather_turns(b, first, count):
            with pool.Fori(first, first + count) as it:
                for k in range(TURN):
                    n, side = it * TURN + (b * STEPS + k), k % 2
                    pool.wait_ge(u_used, n + 1)
                    pool.tensor_copy(idx_now[:, k, :],
                                     eidx[:, b, bass.ds(it * (TURN * GS) + k * GS, GS)]).then_inc(idx_copied, 1)
                    pool.wait_ge(idx_copied, n + 1)
                    for table, buf, landed in ((peer_u, u_rows, u_landed), (peer_v, v_rows, v_landed)):
                        if table is peer_v:
                            pool.wait_ge(v_used, n + 1)
                        c = 2 if table is peer_v else 1
                        pool.tensor_tensor(pool_pad[:, c:c + 1], pool_pad[:, 0:1], pool_pad[:, 0:1], ALU.mult)
                        for i in range(GS):
                            pool.indirect_dma_start(
                                out=buf[side * GS + i], out_offset=None, in_=table[0],
                                in_offset=bass.IndirectOffsetOnAxis(ap=idx_now[:, k, i:i + 1], axis=0),
                            ).then_inc(landed[side], 16)
        pool.wait_ge(routed, 1)
        gather_turns(0, 0, EARLY)
        for b in range(NB):
            pool.wait_ge(routed, b + 2)
            gather_turns(b, 0 if b else EARLY, STEPS // TURN - (0 if b else EARLY))
        pool.wait_ge(sample_routed, 1)
        for table, buf, used, landed in ((peer_u, u_rows, u_used, sample_u_landed), (peer_v, v_rows, v_used, sample_v_landed)):
            for q in range(2):
                pool.wait_ge(used, AHEAD + NB * STEPS - 1 + q)
                for t in range(q * GS, (q + 1) * GS):
                    pool.indirect_dma_start(out=buf[t], out_offset=None, in_=table[0],
                                            in_offset=bass.IndirectOffsetOnAxis(ap=idx_s[:, t:t + 1], axis=0)).then_inc(landed[q], 16)
        pool.wait_ge(windows_stored, 16 * 6)

    @block.scalar
    def _(act):
        def empty(key, ops):
            wait_filled(act, key)
            for n, (out, in_, f, kw) in enumerate(ops):
                ins = act.activation(out, in_, f, **kw)
            ins.then_inc(emptied_by_act, 1)

        def copy(key, out, in_, f=ACT.Copy, **kw):
            empty(key, [(out, in_, f, kw)])

        act.wait_ge(c_loaded, 32)
        act.activation(silu9[0:9, :], c9[0:9, :], ACT.Silu).then_inc(silu_ready, 1)
        copy(("vecT",), vecT, bank(("vecT",))[:, 0:68])
        wait_filled(act, ("vecT",))
        copy(("cT",), scT, bank(("cT",))[:, 0:72].rearrange("p (a b) -> p a b", a=C))
        for c in range(C):
            copy(("xT", c), xT[:, c, 0:T], bank(("xT", c)))
        copy(("xTs",), xT[:, :, T:TT], bank(("xTs",))[:, 0:64].rearrange("p (a b) -> p a b", a=C))
        wait_emptied(act, ("ss", 1, 1))
        act.activation(root, msq, ACT.Sqrt).then_inc(root_ready, 1)

        def ada(i):
            copy(("ada_rows", i), ada_rows[i][0:9, :], bank(("ada_rows", i))[0:9, :])

        for i in range(4):
            ada(i)
        act.wait_ge(filler_ready, 1)
        for b in range(NB + 1):
            out = zqk[0:rows(b), b, 0:512].rearrange("p (j v e) -> p v j e", v=KV, e=HD)
            copy(("q", b), out, bank(("q", b))[0:rows(b)].rearrange("p (v j e) -> p v j e", v=KV, e=HD))
        for b in range(NB + 1):
            src = bank(("kv", b))[0:rows(b)]
            empty(("kv", b), [(zqk[0:rows(b), b, 512:640], src[:, 0:128], ACT.Copy, {}),
                              (zv[0:rows(b), b, :], src[:, 128:256], ACT.Copy, {})])
        for b in range(NB + 1):
            copy(("p", b), zp[0:rows(b), b, :], bank(("p", b))[0:rows(b)])
        def gates(ms):
            for m in ms:
                for h in range(2):
                    copy(("gate", m, h), (ga if m < C else gb)[:, m % C, half(h)], bank(("gate", m, h))[:, 0:HT], ACT.Sigmoid)

        gates(range(4))
        act.wait_ge(qk_mean_ready, 1)
        act.activation(qk_rms, qk_rms, ACT.Sqrt).then_inc(qk_root_ready, 1)
        gates(range(4, 8))
        for b in range(NB):
            copy(("qT", b), qkT[:, 0:4, cols(b)], bank(("qT", b)).rearrange("p (a b) -> p a b", a=4))
            copy(("kT", b), qkT[:, 4, cols(b)], bank(("kT", b))[:, 0:P])
        copy(("qkTs",), qkT[:, :, T:TT], bank(("qkTs",))[:, 0:40].rearrange("p (a b) -> p a b", a=5))

        def exps(b):
            lo = P if b == 0 else 0
            act.wait_ge(max_ready, b + 1)
            for h in range(HEADS):
                act.activation(sS[b % 2][:, h, lo:], sS[b % 2][:, h, lo:], ACT.Exp, bias=nmax[:, h:h + 1],
                               accum_out=ssum[:, h:h + 1])
            act.activation(ssink, ssink, ACT.Exp).then_inc(exps_ready, 1)

        def values(b):
            halves = (1,) if b == 0 else (0, 1)
            for kv in range(KV):
                if b or kv:
                    wait_filled(act, ("o", b, 0) if kv else ("o", b - 1, 1))
                for h in halves:
                    copy(("pt", b, kv, h), pT[:, h, :], bank(("pt", b, kv, h)))
                r = slice(kv * HD, (kv + 1) * HD)
                copy(("o", b, kv), attT[r, :, cols(b)], bank(("o", b, kv))[r].rearrange("p (a b) -> p a b", a=G))

        def pooled(b):
            copy(("d", b), dT[:, :, cols(b)], bank(("d", b)).rearrange("p (a b) -> p a b", a=PG))

        exps(0)
        pooled(0)
        gates((8, 9))
        exps(1)
        pooled(1)
        gates((10, 11))
        values(0)
        exps(2)
        pooled(2)
        gates((12, 13))
        values(1)
        exps(3)
        pooled(3)
        gates((14, 15))
        values(2)
        copy(("ds",), dT[:, :, T:TT], bank(("ds",))[:, 0:32].rearrange("p (a b) -> p a b", a=PG))
        ada(4)
        values(3)
        ada(5)
        ada(6)
        for i in range(2):
            copy(("ktT", i), kTs[:, 4 * i:4 * i + 4, :], bank(("ktT", i)).rearrange("p (a b) -> p a b", a=4))
        copy(("k0T",), k0T, bank(("k0T",))[:, 0:S])
        act.wait_ge(max_ready, NB + 1)
        act.activation(smisc[0:G, 1, :], smisc[0:G, 1, :], ACT.Exp)
        act.activation(sSs[0:G], sSs[0:G], ACT.Exp).then_inc(exps_ready, 1)
        for h in range(2):
            for g in range(PG):
                copy(("y", g, h), bT[:, g, half(h)], bank(("y", g, h))[:, 0:HT], scale=vecT[:, 64 + g:65 + g])
        src = bank(("pts",))
        empty(("pts",), [(pTs[:, 0:64], src[:, 0:64], ACT.Copy, {}), (pTs[0:1, 64:128], src[0:1, 64:128], ACT.Copy, {})])
        copy(("os",), attT[:, :, T:TT], bank(("os",))[:, 0:32].rearrange("p (b j) -> p j b", j=G))
        ada(7)
        for n in range(C):
            act.wait_ge(x1_ready, n + 1)
            act.activation(squares[:, n, :], xT[:, n, :], ACT.Square).then_inc(squares_ready, 1)
        for i in range(4):
            copy(("skT", i), skT[:, 4 * i:4 * i + 4, :], bank(("skT", i)).rearrange("p (a b) -> p a b", a=4))
        wait_emptied(act, ("ss", 2, 1))
        act.activation(root, msq, ACT.Sqrt).then_inc(root_ready, 1)
        for i in range(8, 12):
            ada(i)
        for i in range(2):
            copy(("g2b", i), g2b[:, i * 512:(i + 1) * 512], bank(("g2b", i)))
        for b in range(NB + 1):
            for i in range(2):
                copy(("h2n", b, i), h2n[0:rows(b), b, i * 512:(i + 1) * 512], bank(("h2n", b, i))[0:rows(b)])
        scv = sc.rearrange("p (b m) n -> p b m n", b=5)
        for m in range(16):
            if m >= 2:
                wait_filled(act, ("scs", m - 2))
            for h in range(2):
                copy(("pq", m, h), pq[:, m % 2, half(h)], bank(("pq", m, h))[:, 0:HT])
            if m:
                copy(("scs", m - 1), scv[0:S, NB, m - 1, :], bank(("scs", m - 1))[0:S, 0:NK])
        copy(("scs", 15), scv[0:S, NB, 15, :], bank(("scs", 15))[0:S, 0:NK])

        def gate_exp(b):
            act.wait_ge(best_ready, b + 1)
            act.activation(best[0:rows(b), b, :], best[0:rows(b), b, :], ACT.Exp).then_inc(best_exp_ready, 1)

        gate_exp(0)
        for b in range(NB):
            if b == NB - 1:
                for t in range(S):
                    act.wait_ge(sample_h_ready, t + 1)
                    act.activation(h_all[:, t, :].rearrange("p (a b) -> p a b", a=2), psum[:, 4 + 2 * (t % 2):6 + 2 * (t % 2), :],
                                   ACT.Copy).then_inc(sample_h_used, 1)
            with act.Fori(0, STEPS // TURN) as it:
                for k in range(TURN):
                    n, side = it * TURN + (b * STEPS + k), k % 2
                    act.wait_ge(u_used, n + 1 + AHEAD)
                    act.activation(gelus[:, side, :], acts[:, side, :], ACT.Gelu_apprx_tanh).then_inc(gelu_done, 1)
                    act.wait_ge(coef_ready, n + 1)
                    act.wait_ge(v_used, n + 1)
                    for i in range(GS):
                        ins = act.activation(diags[:, side * GS + i, :], ident, ACT.Copy, scale=coefs[:, side, i:i + 1])
                    ins.then_inc(diag_ready, 1)
            gate_exp(b + 1)
        for q in range(2):
            act.wait_ge(sample_summed, (q + 1) * GS)
            act.activation(act_s[:, q * GS:(q + 1) * GS], act_s[:, q * GS:(q + 1) * GS], ACT.Gelu_apprx_tanh).then_inc(gelu_done, 1)

    @block.vector
    def _(dve):
        steps = [0, None]

        def link(ins):
            if steps[1] is not None:
                dve.drain()
                return
            ins.then_inc(dve_step, 1)
            steps[0] += 1
            dve.wait_ge(dve_step, steps[0])

        link(dve.memset(ones, 1.0))
        dve.wait_ge(dve_step, 1)
        dve.memset(nmax, 0.0).then_inc(ones_ready, 1)

        def mean_squares(n):
            for h in range(2):
                wait_filled(dve, ("ss", n, h))
                dve.tensor_scalar(msq[:, half(h)], bank(("ss", n, h))[:, 0:HT], 1.0 / D, EPS, ALU.mult, ALU.add).then_inc(emptied_by_dve, 1)

        def ada(i):
            wait_filled(dve, ("ada", i))
            bias = vecT[:, 4 * i:4 * i + 4].unsqueeze(2).broadcast_to((P, 4, 9))
            dve.tensor_tensor(mods[:, 4 * i:4 * i + 4, :], bank(("ada", i))[:, 0:36].rearrange("p (a b) -> p a b", a=4),
                              bias, ALU.add).then_inc(emptied_by_dve, 1)

        def normalize(n):
            dve.wait_ge(root_ready, n)
            link(dve.reciprocal(root, root))
            for c in range(C):
                ins = dve.tensor_tensor(hT[:, c, :], xT[:, c, :], root, ALU.mult)
            link(ins)

        def modulate(shift, scale, gain):
            wait_emptied(dve, ("ada", max(shift, scale) // 4 + 1))
            link(dve.scalar_tensor_tensor(smod, mods[:, scale:scale + C, :], 1.0,
                                          vecT[:, gain:gain + C].unsqueeze(2).broadcast_to((P, C, 9)), ALU.add, ALU.mult))
            hs = hT[:, :, T:TT]
            link(dve.tensor_tensor(hs, hs, smod[:, :, 1:9], ALU.mult))
            dve.tensor_tensor(hs, hs, mods[:, shift:shift + C, 1:9], ALU.add)
            for c in range(C):
                dve.tensor_scalar(hT[:, c, 0:T], hT[:, c, 0:T], smod[:, c, 0:1], mods[:, shift + c, 0:1], ALU.mult, ALU.add).then_inc(h_ready, 1)

        for c in range(C):
            wait_emptied(dve, ("xT", c))
            dve.tensor_tensor(squares[:, c, 0:T], xT[:, c, 0:T], xT[:, c, 0:T], ALU.mult).then_inc(squares_ready, 1)
        wait_emptied(dve, ("xTs",))
        dve.tensor_tensor(squares[:, :, T:TT], xT[:, :, T:TT], xT[:, :, T:TT], ALU.mult).then_inc(squares_ready, 1)
        mean_squares(1)
        normalize(1)
        for i in range(4):
            ada(i)
        modulate(0, C, 48)
        wait_emptied(dve, ("xTs",))
        dve.memset(zqk[:, NB, :], 1.0).then_inc(filler_ready, 1)
        wait_emptied(dve, ("kv", NB))
        dve.wait_ge(small_loaded, 16 * N_SMALL)
        dve.wait_ge(filler_ready, 1)
        heads = zqk.rearrange("p b n -> p (b n)").rearrange("p (h e) -> p h e", e=HD)
        zsqh = zsq.rearrange("p (h e) -> p h e", e=HD)
        link(dve.tensor_tensor(zsqh, heads, heads, ALU.mult))
        link(dve.tensor_reduce(qk_rms, zsqh, X, ALU.add))
        dve.tensor_scalar(qk_rms, qk_rms, 1.0 / HD, EPS, ALU.mult, ALU.add).then_inc(qk_mean_ready, 1)
        dve.wait_ge(qk_root_ready, 1)
        link(dve.reciprocal(qk_rms, qk_rms))
        link(dve.tensor_tensor(heads, heads, qk_rms.unsqueeze(2).broadcast_to((P, 50, HD)), ALU.mult))
        for b in range(NB + 1):
            q, k = zqk[:, b, 0:512].rearrange("p (h e) -> p h e", e=HD), zqk[:, b, 512:640].rearrange("p (h e) -> p h e", e=HD)
            dve.tensor_tensor(q, q, gqk[:, 0:1, :].broadcast_to((P, HEADS, HD)), ALU.mult)
            ins = dve.tensor_tensor(k, k, gqk[:, 1:2, :].broadcast_to((P, KV, HD)), ALU.mult)
        ins.then_inc(qk_normed, 1)

        bias = kc[:, K_BIAS:K_OWN].rearrange("p (h s) -> p h s", h=HEADS)

        def scores(b):
            lo = P if b == 0 else 0
            if b >= 2:
                wait_filled(dve, ("pt", b - 2, 1, 1))
            for j in range(G):
                wait_filled(dve, ("s", b, j))
                dve.scalar_tensor_tensor(sS[b % 2][:, 2 * j:2 * j + 2, lo:], bank(("s", b, j)).rearrange("p (v s) -> p v s", v=KV)[:, :, lo:],
                                         HD ** -0.5, bias[:, 2 * j:2 * j + 2, lo:], ALU.mult, ALU.add).then_inc(emptied_by_dve, 1)

        def maxima(b):
            lo = P if b == 0 else 0
            wait_emptied(dve, ("s", b, G - 1))
            link(dve.tensor_reduce(nmax, sS[b % 2][:, :, lo:], X, ALU.max))
            link(dve.tensor_tensor(nmax, nmax, sinks, ALU.max))
            link(dve.tensor_scalar(nmax, nmax, -1.0, None, ALU.mult))
            dve.tensor_tensor(ssink, sinks, nmax, ALU.add).then_inc(max_ready, 1)

        def probabilities(b):
            lo = P if b == 0 else 0
            dve.wait_ge(exps_ready, b + 1)
            link(dve.tensor_tensor(srec, ssum, ssink, ALU.add))
            link(dve.reciprocal(srec, srec))
            s = sS[b % 2][:, :, lo:]
            dve.tensor_tensor(s, s, srec.unsqueeze(2).broadcast_to((P, HEADS, 2 * P - lo)), ALU.mult).then_inc(probs_ready, 1)

        scores(0)
        maxima(0)
        for b in range(1, NB):
            scores(b)
            probabilities(b - 1)
            maxima(b)
        probabilities(NB - 1)
        for i in (4, 5, 6):
            ada(i)
        biass = kc[0:G, K_BIASS:K_END].rearrange("p (v s) -> p v s", v=KV)
        for kv in range(KV):
            for h in range(2):
                wait_filled(dve, ("sc4", kv, h))
                i = kv * S + h * 4
                dve.scalar_tensor_tensor(sSs[0:G, i:i + 4, 1:], bank(("sc4", kv, h))[0:G].rearrange("p (b s) -> p b s", b=4), HD ** -0.5,
                                         biass[:, kv:kv + 1, 1:].broadcast_to((G, 4, WIN)), ALU.mult, ALU.add).then_inc(emptied_by_dve, 1)
        for kv in range(KV):
            wait_filled(dve, ("sc0", kv))
            dve.scalar_tensor_tensor(sSs[0:G, kv * S:(kv + 1) * S, 0:1], bank(("sc0", kv))[0:G, 0:S].unsqueeze(2), HD ** -0.5,
                                           biass[:, kv:kv + 1, 0:1].broadcast_to((G, S, 1)), ALU.mult, ALU.add).then_inc(emptied_by_dve, 1)
        wait_emptied(dve, ("sc0", KV - 1))
        sk = sinks4[0:G, :].unsqueeze(2).broadcast_to((G, KV, S))
        m_max, m_sink, m_sum = (smisc[0:G, i, :] for i in range(3))
        link(dve.tensor_reduce(m_max, sSs[0:G], X, ALU.max))
        link(dve.tensor_tensor(m_max.rearrange("p (v b) -> p v b", v=KV), m_max.rearrange("p (v b) -> p v b", v=KV), sk, ALU.max))
        link(dve.tensor_tensor(m_sink.rearrange("p (v b) -> p v b", v=KV), sk, m_max.rearrange("p (v b) -> p v b", v=KV), ALU.subtract))
        dve.tensor_tensor(sSs[0:G], sSs[0:G], m_max.unsqueeze(2).broadcast_to((G, 16, WIN + 1)), ALU.subtract).then_inc(max_ready, 1)
        dve.wait_ge(exps_ready, NB + 1)
        link(dve.tensor_reduce(m_sum, sSs[0:G], X, ALU.add))
        link(dve.tensor_tensor(m_sum, m_sum, m_sink, ALU.add))
        link(dve.reciprocal(m_sum, m_sum))
        dve.tensor_tensor(sSs[0:G], sSs[0:G], m_sum.unsqueeze(2).broadcast_to((G, 16, WIN + 1)), ALU.mult).then_inc(probs_ready, 1)
        dve.wait_ge(windows_stored, 16 * 6)
        for h in range(2):
            hs = half(h)
            for n in range(C):
                wait_filled(dve, ("A", n, h))
                dve.tensor_tensor(mT[:, n, hs], bank(("A", n, h))[:, 0:HT], ga[:, n, hs], ALU.mult).then_inc(emptied_by_dve, 1)
                wait_filled(dve, ("B", n, h))
                dve.tensor_tensor(gb[:, n, hs], bank(("B", n, h))[:, 0:HT], gb[:, n, hs], ALU.mult).then_inc(emptied_by_dve, 1)
                wait_emptied(dve, ("B", n, h))
                dve.tensor_tensor(mT[:, n, hs], mT[:, n, hs], gb[:, n, hs], ALU.add).then_inc(merged_ready, 1)
        ada(7)
        for n in range(C):
            wait_filled(dve, ("o2", n, 0))
            dve.scalar_tensor_tensor(xT[:, n, half(0)], bank(("o2", n, 0))[:, 0:HT], mods[:, 16 + n, 0:1], xT[:, n, half(0)],
                                     ALU.mult, ALU.add).then_inc(emptied_by_dve, 1)
            wait_filled(dve, ("o2", n, 1))
            o = bank(("o2", n, 1))
            dve.scalar_tensor_tensor(xT[:, n, HT:T], o[:, 0:T - HT], mods[:, 16 + n, 0:1], xT[:, n, HT:T], ALU.mult, ALU.add)
            dve.tensor_tensor(res_s, o[:, T - HT:HT], mods[:, 16 + n, 1:9], ALU.mult).then_inc(emptied_by_dve, 1)
            wait_emptied(dve, ("o2", n, 1))
            dve.tensor_tensor(xT[:, n, T:TT], xT[:, n, T:TT], res_s, ALU.add).then_inc(x1_ready, 1)
            dve.wait_ge(x1_ready, n + 1)
        mean_squares(2)
        normalize(2)
        ada(8)
        ada(9)
        modulate(24, 32, 56)
        ada(10)
        ada(11)
        scv = sc.rearrange("p (b m) n -> p b m n", b=5)
        link(dve.memset(zeros, 0.0))
        dve.memset(gelus, 0.0).then_inc(u_used, AHEAD)
        dve.wait_ge(u_used, AHEAD)

        iota = kc[:, K_IOTA:K_IOTA + TOPK]

        def first8(values, index, src, cut):
            for v, s in zip(values, src):
                dve.max(v[:, 0:8], s)
            dve.drain()
            for v, i, s, c in zip(values, index, src, cut):
                dve.max_index(i[:, 0:8], v[:, 0:8], s)
                dve.match_replace(c, v[:, 0:8], s, -3e38)
            dve.drain()

        def next8(values, index, cut):
            for v, c in zip(values, cut):
                dve.max(v[:, 8:16], c)
            dve.drain()
            for v, i, c in zip(values, index, cut):
                dve.max_index(i[:, 8:16], v[:, 8:16], c)
            dve.drain()

        def route(b, h, part):
            R = rows(b)
            halves = range(2)
            vals, idxs = [r_val[0:R, c, :] for c in halves], [r_idx[0:R, c, :] for c in halves]
            cuts = [r_cut[0:R, c, :] for c in halves]
            flat = r_cand[0:R].rearrange("p a b -> p (a b)")
            if part == 0:
                dve.tensor_copy(r_in[0:R], scv[0:R, b, bass.ds(h * 2, 2), :])
                dve.drain()
                first8(vals, idxs, [r_in[0:R, c, :] for c in halves], cuts)
            if part == 1:
                next8(vals, idxs, cuts)
                dve.tensor_copy(r_idxf[0:R], r_idx[0:R])
                dve.tensor_tensor(r_cand[0:R], r_val[0:R, 0, :].unsqueeze(2).broadcast_to((R, TOPK, TOPK)),
                                  r_val[0:R, 1, :].unsqueeze(1).broadcast_to((R, TOPK, TOPK)), ALU.add)
                dve.drain()
            if part == 2:
                first8([r_best[0:R]], [r_pos[0:R]], [flat], [r_cand2[0:R]])
                next8([r_best[0:R]], [r_pos[0:R]], [r_cand2[0:R]])
            if part == 3:
                dve.tensor_copy(best[0:R, b, bass.ds(h * TOPK, TOPK)], r_best[0:R])
                dve.tensor_scalar(r_half[0:R, 0, :], r_pos[0:R], 4, None, ALU.logical_shift_right)
                dve.tensor_scalar(r_half[0:R, 1, :], r_pos[0:R], 15, None, ALU.bitwise_and)
                dve.drain()
                dve.tensor_copy(r_halff[0:R], r_half[0:R])
                dve.drain()
                hot = r_hot[0:R].rearrange("p (c k) i -> p c k i", c=2)
                dve.tensor_tensor(r_hot[0:R], r_halff[0:R].rearrange("p c k -> p (c k)").unsqueeze(2).broadcast_to((R, 2 * TOPK, TOPK)),
                                  iota[0:R].unsqueeze(1).broadcast_to((R, 2 * TOPK, TOPK)), ALU.is_equal)
                dve.drain()
                dve.tensor_tensor(hot, hot, r_idxf[0:R].unsqueeze(2).broadcast_to((R, 2, TOPK, TOPK)), ALU.mult)
                dve.drain()
                dve.tensor_reduce(r_pick[0:R].rearrange("p c k -> p (c k)"), r_hot[0:R], X, ALU.add)
                dve.drain()
                dve.scalar_tensor_tensor(r_e[0:R], r_pick[0:R, 0, :], float(NK), r_pick[0:R, 1, :], ALU.mult, ALU.add)
                dve.drain()
                dve.tensor_copy(eidx[0:R, b, bass.ds(h * TOPK, TOPK)], r_e[0:R])
                dve.drain()

        def softmax_begin(b):
            R = rows(b)
            v = best[0:R, b, :].rearrange("p (h k) -> p h k", h=PH)
            link(dve.tensor_copy(r_max[0:R].unsqueeze(2), v[:, :, 0:1]))
            dve.tensor_tensor(v, v, r_max[0:R].unsqueeze(2).broadcast_to((R, PH, TOPK)), ALU.subtract).then_inc(best_ready, 1)
            dve.nop().then_inc(routed, 1)

        def softmax_end(b):
            R = rows(b)
            v = best[0:R, b, :].rearrange("p (h k) -> p h k", h=PH)
            dve.wait_ge(best_exp_ready, b + 1)
            link(dve.tensor_reduce(r_sum[0:R], v, X, ALU.add))
            link(dve.reciprocal(r_sum[0:R], r_sum[0:R]))
            link(dve.tensor_tensor(v, v, r_sum[0:R].unsqueeze(2).broadcast_to((R, PH, TOPK)), ALU.mult))

        def loop(count, body):
            with dve.Fori(0, count) as it:
                steps[1] = it
                body(it)
            steps[1] = None

        for m in range(16):
            wait_filled(dve, ("sc", m))
            dve.tensor_copy(scv[:, 0:NB, m, :], bank(("sc", m)).rearrange("p (a b) -> p a b", a=NB)).then_inc(emptied_by_dve, 1)
            if m % 2:
                wait_emptied(dve, ("sc", m))
                for part in range(4):
                    route(0, m // 2, part)
                if m // 2 == EARLY - 1:
                    dve.nop().then_inc(routed, 1)
        wait_emptied(dve, ("scs", 15))
        wait_emptied(dve, ("h2n", NB, 1))
        softmax_begin(0)
        softmax_end(0)
        for b in range(NB):
            R = rows(b)

            def one_turn(it):
                for k in range(TURN):
                    n, side = it * TURN + (b * STEPS + k), k % 2
                    dve.wait_ge(u_landed[side], it * (TURN // 2 * GS * 16) + (b * STEPS // 2 + k // 2 + 1) * GS * 16)
                    for i in range(GS):
                        rows_i = u_rows[side * GS + i]
                        ins = dve.tensor_tensor_reduce(rows_i, rows_i, h2n[:, b, :], 1.0, 0.0,
                                                       ALU.mult, ALU.add, acts[:, side, i:i + 1])
                    ins.then_inc(u_used, 1)
                    route(b + 1, it, k)
                    dve.wait_ge(gelu_done, n + 1)
                    dve.tensor_tensor(coefs[:, side, :], gelus[:, side, :],
                                      best[:, b, bass.ds(it * (TURN * GS) + k * GS, GS)], ALU.mult).then_inc(coef_ready, 1)

            loop(STEPS // TURN, one_turn)
            softmax_begin(b + 1)
            if b == NB - 2:
                dve.nop().then_inc(sample_h_free, 1)
            softmax_end(b + 1)
            dve.wait_ge(v_used, AHEAD + (b + 1) * STEPS)
            if b:
                dve.wait_ge(y_stored, 16 * b)
            for i in range(2):
                h = slice(i * 512, (i + 1) * 512)
                ins = dve.tensor_tensor(y_rows[:, h], psum[:, 2 * (b % 2) + i, :], g2b[:, h], ALU.mult)
            ins.then_inc(sum_read, 1)
            dve.wait_ge(sum_read, b + 1)
            dve.wait_ge(x1_rows_ready, b + 1)
            for i in range(2):
                h = slice(i * 512, (i + 1) * 512)
                ins = dve.tensor_tensor(y_rows[:, h], y_rows[:, h], psum[:, 4 + i, :], ALU.add)
            ins.then_inc(y_ready, 1)
        dve.tensor_copy(eidx_f[0:S, :], eidx[0:S, NB, :]).then_inc(sample_turned, 1)
        dve.wait_ge(sample_turned, 2)
        dve.tensor_copy(idx_s, psum[:, 6, 0:S]).then_inc(sample_routed, 1)
        dve.tensor_copy(gate_s, psum[:, 6, S:2 * S])
        dve.wait_ge(sample_h_used, S)
        for q in range(2):
            dve.wait_ge(sample_u_landed[q], 16 * GS)
            for t in range(q * GS, (q + 1) * GS):
                dve.tensor_tensor_reduce(u_rows[t], u_rows[t], h_all[:, t, :], 1.0, 0.0,
                                         ALU.mult, ALU.add, act_s[:, t:t + 1]).then_inc(sample_summed, 1)
        for q in range(2):
            dve.wait_ge(gelu_done, NB * STEPS + q + 1)
            qs = slice(q * GS, (q + 1) * GS)
            dve.tensor_tensor(act_s[:, qs], act_s[:, qs], gate_s[:, qs], ALU.mult).then_inc(sample_coef_ready, 1)
        dve.wait_ge(sample_out_ready, 1)
        link(dve.tensor_tensor(out_s, psum[:, 7, 0:C * S].rearrange("p (a b) -> p a b", a=C), mods[:, 40:48, 1:9], ALU.mult))
        dve.tensor_tensor(out_s, out_s, xT[:, :, T:TT], ALU.add).then_inc(sample_y_ready, 1)
        dve.wait_ge(sample_out_ready, 2)
        dve.wait_ge(y_stored, 16 * NB)
        dve.tensor_copy(y_rows[0:S, :].rearrange("p (a b) -> p a b", a=2), psum[0:S, 4:6, :]).then_inc(y_ready, 1)

    @block.tensor
    def _(pe):
        def begin(key):
            i = order[key]
            if i >= BANKS:
                wait_emptied(pe, plan[i - BANKS][0])
            return bank(key)

        def end(ins):
            ins.then_inc(bank_filled, 1)

        def chunk(key):
            i = chunk_at[key]
            pe.wait_ge(w_loaded[i % RING], slot_rounds(i))
            k = 4 if key[0] in ("wa", "wb") else 8
            return ring[i % RING].rearrange("p (k n) -> p k n", k=k)

        def product(out, pairs):
            for n, (a, b) in enumerate(pairs):
                ins = pe.matmul(out, a, b, start=(n == 0), stop=(n == len(pairs) - 1))
            return ins

        def mean_squares(n):
            for h in range(2):
                o = begin(("ss", n, h))[:, 0:HT]
                for c in range(C):
                    if h == 0:
                        pe.wait_ge(squares_ready, c + 1 if n == 1 else C + 2 + c)
                    if (n, h, c) == (1, 1, 0):
                        pe.wait_ge(squares_ready, C + 1)
                    ins = pe.matmul(o, ones, squares[:, c, half(h)], start=(c == 0), stop=(c == C - 1))
                end(ins)

        def halves(key, w, n, x, ks):
            ns = slice(n * P, (n + 1) * P)
            for h in range(2):
                end(product(begin((*key, h))[:, 0:HT], [(w[:, k, ns], x[:, k, half(h)]) for k in range(ks)]))

        def ada_products(i):
            w = chunk(("ada", i))
            end(product(begin(("ada_rows", i))[0:9, :], [(scT[:, k, :], w[:, k, :]) for k in range(8)]))

        def ada(i):
            o = begin(("ada", i))
            wait_emptied(pe, ("ada_rows", i))
            for n in range(4):
                ins = pe.transpose(o[:, n * 9:(n + 1) * 9], ada_rows[i][0:9, n * P:(n + 1) * P], ident[0:9, 0:9])
            end(ins)

        pe.wait_ge(ident_loaded, 16)
        pe.wait_ge(vecs_loaded, 16 * 4)
        end(pe.transpose(begin(("vecT",))[:, 0:68], vec68[0:68, :], ident[0:68, 0:68]))
        pe.wait_ge(silu_ready, 1)
        o = begin(("cT",))
        for c in range(C):
            ins = pe.transpose(o[:, c * 9:(c + 1) * 9], silu9[0:9, c * P:(c + 1) * P], ident[0:9, 0:9])
        end(ins)
        pe.wait_ge(x_loaded, 16 * 5)
        for c in range(C):
            o = begin(("xT", c))
            for b in range(NB):
                ins = pe.transpose(o[:, b * P:(b + 1) * P], xnat[:, b, c * P:(c + 1) * P], ident)
            end(ins)
        o = begin(("xTs",))
        for c in range(C):
            ins = pe.transpose(o[:, c * S:(c + 1) * S], xnat[0:S, NB, c * P:(c + 1) * P], ident[0:S, 0:S])
        end(ins)
        pe.wait_ge(ones_ready, 1)
        mean_squares(1)
        wait_emptied(pe, ("cT",))
        ada_products(0)
        for i in range(1, 4):
            ada_products(i)
            ada(i - 1)
        ada(3)
        for w, n in (("q", 512), ("kv", 256), ("p", 512)):
            wt = chunk((w,))
            for b in range(NB + 1):
                o = begin((w, b))[0:rows(b), 0:n]
                for k in range(C):
                    if (w, b) == ("q", 0):
                        pe.wait_ge(h_ready, k + 1)
                    ins = pe.matmul(o, hT[:, k, cols(b)], wt[:, k, 0:n], start=(k == 0), stop=(k == C - 1))
                end(ins)

        def gates(ms):
            for m in ms:
                halves(("gate", m), chunk(("gate", m // 4)), m % 4, hT, C)

        gates(range(8))
        pe.wait_ge(qk_normed, 1)
        for b in range(NB):
            o = begin(("qT", b))
            for j in range(G):
                ins = pe.transpose(o[:, j * P:(j + 1) * P], zqk[:, b, j * P:(j + 1) * P], ident)
            end(ins)
            end(pe.transpose(begin(("kT", b))[:, 0:P], zqk[:, b, 512:640], ident))
        o = begin(("qkTs",))
        for j in range(G + 1):
            ins = pe.transpose(o[:, j * S:(j + 1) * S], zqk[0:S, NB, j * P:(j + 1) * P], ident[0:S, 0:S])
        end(ins)

        def scores(b):
            wait_emptied(pe, ("kT", b))
            lo = P if b == 0 else 0
            for j in range(G):
                o = begin(("s", b, j))
                r = slice(j // 2 * HD, (j // 2 + 1) * HD)
                for i in range(2):
                    ins = pe.matmul(o[:, i * 2 * P + lo:(i + 1) * 2 * P], qkT[r, j % 2 * 2 + i, cols(b)],
                                    qkT[r, 4, (b - 1) * P + lo:(b + 1) * P], start=True, stop=True)
                end(ins)

        def pooled(b):
            own = K_OWN if b else K_FIRST
            o = begin(("d", b))
            for g in range(PG):
                gs = slice(g * P, (g + 1) * P)
                pairs = [(zp[:, b, gs], kc[:, own + g * P:own + (g + 1) * P])]
                if b:
                    pairs += [(zp[:, b - 1, gs], kc[:, K_PREV + g * P:K_PREV + (g + 1) * P])]
                ins = product(o[:, gs], pairs)
            end(ins)

        def values(b):
            halves = (1,) if b == 0 else (0, 1)
            pe.wait_ge(probs_ready, b + 1)
            for kv in range(KV):
                for h in halves:
                    o = begin(("pt", b, kv, h))
                    for j in range(G):
                        ins = pe.transpose(o[:, j * P:(j + 1) * P], sS[b % 2][:, kv * G + j, h * P:(h + 1) * P], ident)
                    end(ins)
                o = begin(("o", b, kv))
                wait_emptied(pe, ("pt", b, kv, 1))
                end(product(o[kv * HD:(kv + 1) * HD, :], [(zv[:, b - 1 + h, kv * HD:(kv + 1) * HD], pT[:, h, :]) for h in halves]))

        pe.wait_ge(consts_loaded, 16)
        scores(0)
        pooled(0)
        gates((8, 9))
        scores(1)
        pooled(1)
        gates((10, 11))
        values(0)
        scores(2)
        pooled(2)
        gates((12, 13))
        values(1)
        scores(3)
        pooled(3)
        gates((14, 15))
        values(2)
        pe.wait_ge(tail_loaded, 32)
        o = begin(("ds",))
        for g in range(PG):
            ins = pe.matmul(o[:, g * S:(g + 1) * S], pext[:, g * P:(g + 1) * P], kc[:, K_POOLS + g * S:K_POOLS + (g + 1) * S],
                            start=True, stop=True)
        end(ins)
        ada_products(4)
        values(3)
        ada(4)
        ada_products(5)
        ada_products(6)
        ada(5)
        ada(6)
        pe.wait_ge(cache_loaded, 64)
        for i in range(2):
            o = begin(("ktT", i))
            for b in range(4):
                ins = pe.transpose(o[:, b * P:(b + 1) * P], ktile[:, 4 * i + b, :], ident)
            end(ins)
        end(pe.transpose(begin(("k0T",))[:, 0:S], k0[0:S, :], ident[0:S, 0:S]))
        wait_emptied(pe, ("k0T",))
        for kv in range(KV):
            r = slice(kv * HD, (kv + 1) * HD)
            for h in range(2):
                o = begin(("sc4", kv, h))
                for b in range(4):
                    s = 4 * h + b
                    ins = pe.matmul(o[0:G, b * P:(b + 1) * P], qkT[r, 0:G, T + s], kTs[r, s, :], start=True, stop=True)
                end(ins)
        for kv in range(KV):
            o = begin(("sc0", kv))
            r = slice(kv * HD, (kv + 1) * HD)
            for s in range(S):
                ins = pe.matmul(o[0:G, s:s + 1], qkT[r, 0:G, T + s], k0T[r, s:s + 1], start=True, stop=True)
            end(ins)
        wait_emptied(pe, ("ds",))
        for h in range(2):
            for g in range(PG):
                end(pe.matmul(begin(("y", g, h))[:, 0:HT], wpool[:, g, :], dT[:, g, half(h)], start=True, stop=True))
        wa, wb = chunk(("wa",)), chunk(("wb",))

        def branches(h):
            for n in range(C):
                ns = slice(n * P, (n + 1) * P)
                for key, w, x in (("A", wa, attT), ("B", wb, bT)):
                    end(product(begin((key, n, h))[:, 0:HT], [(w[:, k, ns], x[:, k, half(h)]) for k in range(4)]))

        wait_emptied(pe, ("y", PG - 1, 1))
        branches(0)
        pe.wait_ge(probs_ready, NB + 1)
        o = begin(("pts",))
        for i in range(16):
            pe.transpose(o[:, i * G:(i + 1) * G], sSs[0:G, i, 1:], ident[0:G, 0:G])
        for i in range(16):
            ins = pe.transpose(o[0:1, 64 + i * G:64 + (i + 1) * G], sSs[0:G, i, 0:1], ident[0:G, 0:G])
        end(ins)
        pe.wait_ge(oldest_v_loaded, 16)
        o = begin(("os",))
        wait_emptied(pe, ("pts",))
        for kv in range(KV):
            r = slice(kv * HD, (kv + 1) * HD)
            for s in range(S):
                i = (kv * S + s) * G
                out = o[r, s * G:(s + 1) * G]
                pe.matmul(out, vtile[:, s, r], pTs[:, i:i + G], start=True, stop=False)
                ins = pe.matmul(out, v0[0:1, s, r], pTs[0:1, 64 + i:64 + i + G], start=False, stop=True)
        end(ins)
        wait_emptied(pe, ("os",))
        branches(1)
        ada_products(7)
        ada(7)
        pe.wait_ge(merged_ready, 2 * C)
        for n in range(C):
            halves(("o2", n), chunk(("wo", n // 4)), n % 4, mT, C)
        pe.wait_ge(subkeys_loaded, 16)
        for i in range(4):
            o = begin(("skT", i))
            for m in range(4):
                ins = pe.transpose(o[:, m * P:(m + 1) * P], sk_rows[:, 4 * i + m, :], ident)
            end(ins)
        mean_squares(2)
        for i in (8, 10):
            ada_products(i)
            ada_products(i + 1)
            ada(i)
            ada(i + 1)
        wait_emptied(pe, ("ada", 11))
        for i in range(2):
            o = begin(("g2b", i))
            for c in range(4):
                ins = pe.matmul(o[:, c * P:(c + 1) * P], mods[:, 40 + 4 * i + c, 0:1].broadcast_to((P, P)), ident, start=True, stop=True)
            end(ins)
        pe.wait_ge(h_ready, 2 * C)
        for b in range(NB + 1):
            for i in range(2):
                o = begin(("h2n", b, i))
                for c in range(4):
                    ins = pe.transpose(o[0:rows(b), c * P:(c + 1) * P], hT[:, 4 * i + c, cols(b)], ident)
                end(ins)

        def subkey_scores(m):
            o = begin(("sc", m))
            wait_emptied(pe, ("pq", m, 1))
            for b in range(NB):
                ins = pe.matmul(o[:, b * P:(b + 1) * P], pq[:, m % 2, b * P:(b + 1) * P], skT[:, m, :], start=True, stop=True)
            end(ins)
            end(pe.matmul(begin(("scs", m))[0:S, 0:NK], pq[:, m % 2, T:TT], skT[:, m, :], start=True, stop=True))

        for m in range(16):
            halves(("pq", m), chunk(("wq", m // 4)), m % 4, hT, C)
            if m:
                subkey_scores(m - 1)
        subkey_scores(15)
        pe.nop().then_inc(v_used, AHEAD)
        for key, _ in plan[-BANKS:]:
            wait_emptied(pe, key)
        for b in range(NB):
            pe.wait_ge(u_used, AHEAD)
            if b >= 2:
                pe.wait_ge(sum_read, b - 1)
            for i in range(2):
                pe.matmul(psum[:, 2 * (b % 2) + i, :], zeros, zeros[:, 0:1].broadcast_to((P, 512)),
                          start=True, stop=False, skip_group_check=True)
            if b:
                pe.wait_ge(y_ready, b)
            if b == NB - 1:
                pe.wait_ge(sample_h_free, 1)
                for t in range(S):
                    if t >= 2:
                        pe.wait_ge(sample_h_used, t - 1)
                    for h in range(2):
                        ins = pe.matmul(psum[:, 4 + 2 * (t % 2) + h, :], ident[0:S, t:t + 1].broadcast_to((S, P)),
                                        h2n[0:S, NB, h * 512:(h + 1) * 512], start=True, stop=True)
                    ins.then_inc(sample_h_ready, 1)
                pe.wait_ge(sample_h_used, S)
            for i in range(2):
                for c in range(4):
                    ins = pe.transpose(psum[:, 4 + i, c * P:(c + 1) * P], xT[:, 4 * i + c, cols(b)], ident)
            ins.then_inc(x1_rows_ready, 1)
            with pe.Fori(0, STEPS // TURN) as it:
                for k in range(TURN):
                    n, side = it * TURN + (b * STEPS + k), k % 2
                    pe.wait_ge(v_landed[side], it * (TURN // 2 * GS * 16) + (b * STEPS // 2 + k // 2 + 1) * GS * 16)
                    pe.wait_ge(diag_ready, n + 1)
                    for i in range(GS):
                        for h in range(2):
                            ins = pe.matmul(psum[:, 2 * (b % 2) + h, :], diags[:, side * GS + i, :],
                                            v_rows[side * GS + i][:, h * 512:(h + 1) * 512],
                                            start=False, stop=False, skip_group_check=True)
                    ins.then_inc(v_used, 1)
        pe.wait_ge(sample_turned, 1)
        pe.transpose(psum[:, 6, 0:S], eidx_f[0:S, :], ident[0:S, 0:S])
        pe.transpose(psum[:, 6, S:2 * S], best[0:S, NB, :], ident[0:S, 0:S]).then_inc(sample_turned, 1)
        for q in range(2):
            pe.wait_ge(sample_v_landed[q], 16 * GS)
            pe.wait_ge(sample_coef_ready, q + 1)
            for t in range(q * GS, (q + 1) * GS):
                for c in range(C):
                    ins = pe.matmul(psum[:, 7, c * S + t:c * S + t + 1], v_rows[t][:, c * P:(c + 1) * P], act_s[:, t:t + 1],
                                    start=True, stop=True)
        ins.then_inc(sample_out_ready, 1)
        pe.wait_ge(sample_y_ready, 1)
        pe.wait_ge(y_ready, NB)
        for c in range(C):
            ins = pe.transpose(psum[0:S, 4 + c // 4, c % 4 * P:(c % 4 + 1) * P], out_s[:, c, :], ident)
        ins.then_inc(sample_out_ready, 1)

    block.__exit__(None, None, None)


_INS = ['x_prompt', 'x_sample', 'cache_k', 'cache_v', 'state_pool', 'c_prompt', 'c_sample', 'norm1_g', 'norm2_g', 'w_ada',
        'b_ada', 'w_in', 'q_norm_g', 'k_norm_g', 'attn_sinks', 'w_pool', 'pool_scale', 'w_branch_attn', 'w_branch_pool',
        'w_out', 'peer_wq', 'peer_subkeys', 'peer_u', 'peer_v']
_OUTS = [(1, T, D), (S, 1, D), (1, 1, WIN, KV, HD), (1, 1, WIN, KV, HD), (1, 1, HIST, PW),
         (1, S, WIN, KV, HD), (1, S, WIN, KV, HD), (1, S, HIST, PW)]


def kernel(**inputs):
    import concourse.bacc as bacc
    from concourse.bass_utils import run_bass_kernel_spmd

    nc = bacc.Bacc("TRN2", target_bir_lowering=False, num_devices=1)
    arrays, args = {}, []
    for name in _INS:
        a = np.ascontiguousarray(inputs[name])
        arrays[f"in_{name}"] = a
        args.append(nc.dram_tensor(f"in_{name}", a.shape, mybir.dt.from_np(a.dtype), kind="ExternalInput").ap())
    arrays["in_consts"] = constants()
    args.append(nc.dram_tensor("in_consts", arrays["in_consts"].shape, F32, kind="ExternalInput").ap())
    for i, shape in enumerate(_OUTS):
        args.append(nc.dram_tensor(f"out_{i}", shape, F32, kind="ExternalOutput").ap())
    decoder_layer(nc, *args)
    r = run_bass_kernel_spmd(nc, [arrays], core_ids=[0])
    return tuple(r.results[0][f"out_{i}"] for i in range(len(_OUTS)))
```

```python
import numpy as np

import concourse.bass as bass
from concourse import mybir

F32 = mybir.dt.float32
I32 = mybir.dt.int32
U32 = mybir.dt.uint32
ALU = mybir.AluOpType
ACT = mybir.ActivationFunctionType
X = mybir.AxisListType.X

P = 128
D = 1024
C = D // P
T = 512
NB = T // P
S = 8
TT = T + S
HT = TT // 2
HEADS, KV, HD = 8, 2, 64
G = HEADS // KV
WIN = 128
PG = 4
POOL_WINDOWS = (2, 4, 8, 16)
HIST = 15
PW = PG * P
PH = 8
TOPK = 16
NK = 128
SLOTS = PH * TOPK
EPS = 1e-6
NEG = -1e30
BANKS = 8
CHUNK = 8 * 512
RING = 3
WQ_RING = 3
GS = 4
OVER = 4
OVER_FROM = 3
TURN = 4

K_ID = 0
K_BIAS = K_ID + P
K_OWN = K_BIAS + HEADS * 2 * P
K_FIRST = K_OWN + PG * P
K_PREV = K_FIRST + PG * P
K_POOLS = K_PREV + PG * P
K_IOTA = K_POOLS + PG * S
K_BIASS = K_IOTA + TOPK
K_HEAD = K_BIASS + KV * (WIN + 1)
K_SEQ = K_HEAD + PH
K_END = K_SEQ + S


def constants():
    k = np.zeros((P, K_END), np.float32)
    k[:, K_ID:K_BIAS] = np.eye(P)
    q, s = np.arange(P)[:, None], np.arange(2 * P)[None, :]
    dist = q + P - s
    valid = (dist >= 0) & (dist <= WIN)
    for kv in range(KV):
        for j in range(G):
            slope = 2.0 ** -(kv * G + j + 1)
            o = K_BIAS + (kv * G + j) * 2 * P
            k[:, o:o + 2 * P] = np.where(valid, -slope * dist, NEG)
            o = K_BIASS + kv * (WIN + 1)
            k[j, o:o + WIN + 1] = -slope * (WIN - np.arange(WIN + 1))
    s, t = np.arange(P)[:, None], np.arange(P)[None, :]
    for g, w in enumerate(POOL_WINDOWS):
        near = (t - s >= 0) & (t - s < w)
        k[:, K_OWN + g * P:K_OWN + (g + 1) * P] = near / w - (s == t)
        k[:, K_FIRST + g * P:K_FIRST + (g + 1) * P] = near / np.minimum(t + 1, w) - (s == t)
        k[:, K_PREV + g * P:K_PREV + (g + 1) * P] = (t + P - s < w) / w
        for r in range(HIST + 1):
            for b in range(S):
                k[r * S + b, K_POOLS + g * S + b] = (r > HIST - w) / w - (r == HIST)
    k[:, K_IOTA:K_IOTA + TOPK] = np.arange(TOPK)
    for h in range(PH):
        k[h * S:(h + 1) * S, K_HEAD + h] = 1
        k[h * S:(h + 1) * S, K_SEQ:K_SEQ + S] = np.eye(S)
    return k


def score_tiles(m):
    return {0: (), 1: (0, 1), 2: ()}.get(m, (m - 1,))


def bank_plan():
    both = range(2)
    def ada_rows(i):
        return [(("ada_rows", i), "A")]

    def ada(i):
        return [(("ada", i), "V")]

    plan = [(("vecT",), "A"), (("cT",), "A")]
    plan += [(("xT", c), "A") for c in range(C)] + [(("xTs",), "A")]
    plan += ada_rows(0) + [(("ss", 1, h), "V") for h in both]
    plan += ada_rows(1) + ada(0) + ada_rows(2) + ada(1) + ada_rows(3) + ada(2) + ada(3)
    plan += [((w, b), "A") for w in ("q", "kv", "p") for b in range(NB + 1)]

    def gates(ms):
        return [(("gate", m, h), "A") for m in ms for h in both]

    def scores(b):
        return [(("s", b, j), "V") for j in range(G)]

    def values(b):
        halves = (1,) if b == 0 else (0, 1)
        return [k for kv in range(KV) for k in [(("pt", b, kv, h), "A") for h in halves] + [(("o", b, kv), "A")]]

    plan += gates(range(8))
    for b in range(NB):
        plan += [(("qT", b), "A"), (("kT", b), "A")]
    plan += [(("qkTs",), "A")]
    plan += scores(0) + [(("d", 0), "A")] + gates((8, 9)) + scores(1) + [(("d", 1), "A")] + gates((10, 11)) + values(0)
    plan += scores(2) + [(("d", 2), "A")] + gates((12, 13)) + values(1) + scores(3) + [(("d", 3), "A")] + gates((14, 15)) + values(2)
    plan += [(("ds",), "A")] + ada_rows(4) + values(3) + ada(4) + ada_rows(5) + ada_rows(6) + ada(5) + ada(6)
    plan += [(("ktT", i), "A") for i in range(2)] + [(("k0T",), "A")]
    plan += [(("sc4", kv, h), "V") for kv in range(KV) for h in range(2)] + [(("sc0", kv), "V") for kv in range(KV)]
    plan += [(("y", g, h), "A") for h in both for g in range(PG)]
    plan += [((w, n, 0), "V") for n in range(C) for w in ("A", "B")]
    plan += [(("pts",), "A"), (("os",), "A")]
    plan += [((w, n, 1), "V") for n in range(C) for w in ("A", "B")] + ada_rows(7) + ada(7)
    plan += [(("o2", n, h), "V") for n in range(C) for h in both]
    plan += [(("skT", i), "A") for i in range(4)]
    plan += [(("ss", 2, h), "V") for h in both]
    plan += ada_rows(8) + ada_rows(9) + ada(8) + ada(9) + ada_rows(10) + ada_rows(11) + ada(10) + ada(11)
    plan += [(("h2n", b, i), "A") for b in range(NB + 1) for i in range(2)]
    for m in range(16):
        plan += [(("pq", m, h), "A") for h in both]
        for i in score_tiles(m):
            plan += [(("sc", i), "V"), (("scs", i), "A")]
    plan += [(("sc", 15), "V"), (("scs", 15), "A")]
    plan += [(("g2b", i), "A") for i in range(2)]
    return plan


def weight_chunks():
    chunks = [(("ada", i), ("ada_rows", i)) for i in range(4)]
    chunks += [((w,), (w, NB)) for w in ("q", "kv", "p")]
    chunks += [(("gate", i), ("gate", 4 * i + 3, 1)) for i in range(4)]
    chunks += [(("ada", i), ("ada_rows", i)) for i in (4, 5, 6)]
    chunks += [(("wa",), ("B", C - 1, 1)), (("wb",), ("B", C - 1, 1))]
    chunks += [(("ada", 7), ("ada_rows", 7))]
    chunks += [(("wo", 0), ("o2", 3, 1)), (("wo", 1), ("o2", 7, 1))]
    chunks += [(("ada", i), ("ada_rows", i)) for i in (8, 9, 10, 11)]
    return chunks


def decoder_layer(nc, x_prompt, x_sample, cache_k, cache_v, state_pool, c_prompt, c_sample, norm1_g,
                  norm2_g, w_ada, b_ada, w_in, q_norm_g, k_norm_g, attn_sinks, w_pool, pool_scale,
                  w_branch_attn, w_branch_pool, w_out, peer_wq, peer_subkeys, peer_u, peer_v, consts,
                  y_prompt, y_sample, k_win_p, v_win_p, pool_p, k_win_s, v_win_s, pool_s):
    plan = bank_plan()
    order = {key: i for i, (key, _) in enumerate(plan)}
    taker = dict(plan)
    turn = {}
    for who in "AV":
        for i, key in enumerate(k for k, w in plan if w == who):
            turn[key] = i + 1
    sums_from = order[("pq", OVER_FROM - 2, 0)]
    bank_of = [i % BANKS if i < sums_from else 2 + (i - sums_from) % (BANKS - 2) for i in range(len(plan))]
    content_before = [max((j for j in range(i) if bank_of[j] == bank_of[i]), default=None) for i in range(len(plan))]
    chunks = weight_chunks()
    chunk_at = {key: i for i, (key, _) in enumerate(chunks)}

    def sem(name):
        return nc.alloc_semaphore(name)

    bank_filled, emptied_by_act, emptied_by_dve = sem("bank_filled"), sem("emptied_by_act"), sem("emptied_by_dve")
    x_loaded, c_loaded, consts_loaded, small_loaded = sem("x_loaded"), sem("c_loaded"), sem("consts_loaded"), sem("small_loaded")
    ident_loaded, vecs_loaded = sem("ident_loaded"), sem("vecs_loaded")
    subkeys_loaded, cache_loaded, oldest_v_loaded, tail_loaded = sem("subkeys_loaded"), sem("cache_loaded"), sem("oldest_v_loaded"), sem("tail_loaded")
    windows_stored, y_stored = sem("windows_stored"), sem("y_stored")
    w_loaded = [sem(f"w_loaded{i}") for i in range(RING)]
    wq_loaded = [sem(f"wq_loaded{i}") for i in range(WQ_RING)]
    act_step, dve_step = sem("act_step"), sem("dve_step")
    silu_ready, ones_ready, filler_ready = sem("silu_ready"), sem("ones_ready"), sem("filler_ready")
    squares_ready, square_sum_ready, root_ready, h_ready = sem("squares_ready"), sem("square_sum_ready"), sem("root_ready"), sem("h_ready")
    qk_mean_ready, qk_root_ready, qk_normed = sem("qk_mean_ready"), sem("qk_root_ready"), sem("qk_normed")
    max_ready, exps_ready, probs_ready = sem("max_ready"), sem("exps_ready"), sem("probs_ready")
    merged_ready, x1_ready = sem("merged_ready"), sem("x1_ready")
    best_ready, best_exp_ready, routed, gates_ready = sem("best_ready"), sem("best_exp_ready"), sem("routed"), sem("gates_ready")
    u_landed = [sem(f"u_landed_half{i}") for i in range(2)]
    v_landed = [sem(f"v_landed_half{i}") for i in range(2)]
    sample_rows_loaded, sample_routed, sample_u_landed, sample_v_landed = sem("sample_rows_loaded"), sem("sample_routed"), [sem(f"sample_u_landed{q}") for q in range(2)], [sem(f"sample_v_landed{t}") for t in range(S)]
    sample_spread, sample_turned, sample_summed, sample_coef_ready, sample_out_ready = sem("sample_spread"), sem("sample_turned"), sem("sample_summed"), sem("sample_coef_ready"), sem("sample_out_ready")
    sample_h_ready, sample_h_used = sem("sample_h_ready"), sem("sample_h_used")
    sample_x_ready, sample_x_used = sem("sample_x_ready"), sem("sample_x_used")
    pad_ready = sem("pad_ready")
    u_used, v_used, idx_copied = sem("u_used"), sem("v_used"), sem("idx_copied")
    gelu_done, coef_ready, diag_ready = sem("gelu_done"), sem("coef_ready"), sem("diag_ready")
    sum_read, x1_rows_ready, y_ready = sem("sum_read"), sem("x1_rows_ready"), sem("y_ready")

    AR = 53200
    arena = nc.alloc_sbuf_tensor("arena", [P, AR], F32)
    top = [0]

    def at(off, n, a=None):
        v = arena[:, off:off + n]
        return v if a is None else v.rearrange("p (a b) -> p a b", a=a)

    def take(n):
        top[0] += n
        assert top[0] <= AR, top[0]
        return top[0] - n

    kc = at(take(K_END), K_END)
    ident = kc[:, K_ID:K_ID + P]
    vecT = at(take(68), 68)
    ones = at(take(P), P)
    scT = at(take(C * 9), C * 9, C)
    gqk = at(take(2 * HD), 2 * HD, 2)
    mods = at(take(48 * 9), 48 * 9, 48)
    sinks = at(take(8), 8)
    sinks4 = at(take(2), 2)
    smod = at(take(9 * C), 9 * C, C)
    res_s = at(take(S), S)
    nmax, ssum, srec, ssink = (at(take(8), 8) for _ in range(4))
    xT = at(take(C * TT), C * TT, C)
    hT = at(take(C * TT), C * TT, C)
    o_ring = take(RING * CHUNK)
    ring = [at(o_ring + i * CHUNK, CHUNK) for i in range(RING)]
    o_shared = top[0]
    o_ga, o_gb = take(C * TT), take(C * TT)
    ga, gb = at(o_ga, C * TT, C), at(o_gb, C * TT, C)
    squares = at(o_gb, C * TT, C)
    o_att, o_d = take(G * TT), take(PG * TT)
    attT, dT = at(o_att, G * TT, G), at(o_d, PG * TT, PG)
    msq, root = at(o_att, TT), at(o_att + TT, TT)
    c9, silu9 = at(o_d, D), at(o_d + D, D)
    v0 = at(o_d, S * P, S)
    o_z = take(6400)
    zqk, zv, zp = at(o_z, 3200, 5), at(o_z + 3200, 640, 5), at(o_z + 3840, 2560, 5)
    xnat = at(o_z, 5 * D, 5)
    pext = zp[:, 0, :]
    mT = at(o_z, C * TT, C)
    o_qkT = take(5 * TT)
    qkT = at(o_qkT, 5 * TT, 5)
    bT = at(o_qkT, PG * TT, PG)
    vec68 = at(o_qkT, P)
    o_q = take(5184)
    zsq, qk_rms = at(o_q, 3200), at(o_q + 3200, 50)
    sS = [at(o_q, 2048, 8), at(o_q + 2048, 2048, 8)]
    pT = at(o_q + 4096, 1024, 2)
    o_h = o_ring - C * TT
    ktile, vtile = at(o_h, 1024, S), at(o_h + 1024, 1024, S)
    ada_places = [o_q + i * 512 for i in range(4)] + [o_h + 2048 + i * 512 for i in range(3)] + [o_q + i * 512 for i in range(5)]
    ada_rows = [at(o, 512) for o in ada_places]
    kTs = at(o_q + 2048, 1024, S)
    sSs = at(o_q + 3072, 16 * 129, 16)
    k0, k0T = at(take(P), P), at(take(S), S)
    pTs, smisc = at(take(P), P), at(take(4 * 16), 64, 4)
    wpool = at(take(PG * P), PG * P, PG)
    top[0] = o_shared
    o_sk = take(4096)
    sk_rows = at(o_sk, 2048, 16)
    sc = at(take(5 * 16 * NK), 5 * 16 * NK, 80)
    h_all = at(o_sk + 4096, S * D, S)
    xs_rows, g2s_rows = at(o_sk + 4096 + S * D, D), at(o_sk + 4096 + (S + 1) * D, D)
    h2n = at(take(5 * D), 5 * D, 5)
    o_g2b = take(D)
    g2b = at(o_g2b, D)
    o_diag = take(2 * GS * P)
    diags = at(o_diag, 2 * GS * P, 2 * GS)
    pq = at(take(2 * TT), 2 * TT, 2)
    pick_s = pq.rearrange("p a b -> p (a b)")[:, 0:S * P].rearrange("p (s n) -> p s n", s=S)
    eidx = at(take(NB * SLOTS), NB * SLOTS, NB).bitcast(I32)
    best = at(take(NB * SLOTS), NB * SLOTS, NB)
    r_in, r_cut = at(take(2 * NK), 2 * NK, 2), at(take(2 * NK), 2 * NK, 2)
    r_val = at(take(2 * TOPK), 2 * TOPK, 2)
    r_idx = at(take(2 * TOPK), 2 * TOPK, 2).bitcast(U32)
    r_idxf = at(take(2 * TOPK), 2 * TOPK, 2)
    r_cand, r_cand2 = at(take(TOPK * TOPK), TOPK * TOPK, TOPK), at(take(TOPK * TOPK), TOPK * TOPK)
    r_best = at(take(TOPK), TOPK)
    r_pos = at(take(TOPK), TOPK).bitcast(U32)
    r_half = at(take(2 * TOPK), 2 * TOPK, 2).bitcast(U32)
    r_halff = at(take(2 * TOPK), 2 * TOPK, 2)
    r_hot = at(take(2 * TOPK * TOPK), 2 * TOPK * TOPK, 2 * TOPK)
    r_pick = at(take(2 * TOPK), 2 * TOPK, 2)
    r_e = at(take(TOPK), TOPK)
    r_max, r_sum = at(take(PH), PH), at(take(PH), PH)
    zeros = at(take(P), P)
    o_y = take(D)
    y_rows = at(o_y, D)
    skT = [at(o, 1024, 8)[:, m, :] for o in (o_g2b, o_y) for m in range(8)]
    wq_ring = [at(K_BIAS + i * D, D, C) for i in range(WQ_RING)]
    acts, gelus, coefs = (at(take(2 * GS), 2 * GS, 2) for _ in range(3))
    hs_in, hs_best, hs_expert = at(take(2 * NK), 2 * NK, 2), at(take(TOPK), TOPK), at(take(TOPK), TOPK)
    hs_max, hs_sum = at(take(1), 1), at(take(1), 1)
    hs_spread = at(take(2 * SLOTS), 2 * SLOTS, 2)
    idx_s, gate_s, act_s = at(take(S), S).bitcast(I32), at(take(S), S), at(take(S), S)
    coef_s = at(take(S * S), S * S)
    pool_pad = at(take(3), 3)
    idx_now = at(take(TURN * GS), TURN * GS, TURN).bitcast(I32)
    u_rows = [at(o_ring + i * D, D) for i in range(2 * GS)]
    v_rows = [at(o_ring + (2 * GS + i) * D, D) for i in range(2 * GS)]
    assert 4 * GS * D <= RING * CHUNK + 4096

    psum = nc.alloc_psum_tensor("psum", [P, BANKS, 512], F32)

    def bank(key):
        return psum[:, bank_of[order[key]], :]

    def wait_filled(eng, key):
        eng.wait_ge(bank_filled, order[key] + 1)

    def wait_emptied(eng, key):
        eng.wait_ge(emptied_by_act if taker[key] == "A" else emptied_by_dve, turn[key])

    def cols(b):
        return slice(b * P, (b + 1) * P) if b < NB else slice(T, TT)

    def rows(b):
        return P if b < NB else S

    def half(h):
        return slice(h * HT, (h + 1) * HT)

    N_SMALL = 7
    STEPS = SLOTS // GS
    TURNS = STEPS // TURN
    EARLY = 6
    AHEAD = 2

    block = nc.Block()
    block.__enter__()

    @block.sync
    def _(sp):
        sp.dma_start(c9[0:1, :], c_prompt).then_inc(c_loaded, 16)
        sp.dma_start(c9[1:9, :], c_sample).then_inc(c_loaded, 16)
        sp.dma_start(ident, consts[:, 0:P]).then_inc(ident_loaded, 16)
        sp.dma_start(vec68[0:48, :], b_ada[0].rearrange("(a b) -> a b", b=P)).then_inc(vecs_loaded, 16)
        sp.dma_start(vec68[48:56, :], norm1_g[0].rearrange("(a b) -> a b", b=P)).then_inc(vecs_loaded, 16)
        sp.dma_start(vec68[56:64, :], norm2_g[0].rearrange("(a b) -> a b", b=P)).then_inc(vecs_loaded, 16)
        sp.dma_start(vec68[64:68, :], pool_scale[0].rearrange("(a b) -> a b", b=P)).then_inc(vecs_loaded, 16)
        for b in range(NB):
            sp.dma_start(xnat[:, b, :], x_prompt[0, b * P:(b + 1) * P, :]).then_inc(x_loaded, 16)
        sp.dma_start(xnat[0:S, NB, :], x_sample[:, 0, :]).then_inc(x_loaded, 16)
        win = w_in[0].rearrange("(k p) n -> p k n", p=P)
        wad = w_ada[0].rearrange("(k p) n -> p k n", p=P)
        wqd = peer_wq[0].rearrange("(k p) n -> p k n", p=P)
        starts = {"q": (0, 512), "kv": (512, 256), "p": (768, 512)}
        for i, (key, _) in enumerate(chunks):
            if i >= RING:
                wait_filled(sp, chunks[i - RING][1])
            r = ring[i % RING]
            wide = r.rearrange("p (k n) -> p k n", k=8)
            if key[0] == "ada":
                src, dst = wad[:, :, key[1] * 512:(key[1] + 1) * 512], wide
            elif key[0] in starts:
                c0, n = starts[key[0]]
                src, dst = win[:, :, c0:c0 + n], wide[:, :, 0:n]
            elif key[0] == "gate":
                c0 = 1280 + key[1] * 512
                src, dst = win[:, :, c0:c0 + 512], wide
            elif key[0] == "wo":
                src, dst = w_out[0].rearrange("(k p) n -> p k n", p=P)[:, :, key[1] * 512:(key[1] + 1) * 512], wide
            elif key[0] == "wb":
                src, dst = w_branch_pool[0].rearrange("(k p) n -> p k n", p=P), r.rearrange("p (k n) -> p k n", k=4)
            else:
                dst = r.rearrange("p (k n) -> p k n", k=4)
                for kv in range(KV):
                    half = w_branch_attn[0, kv * G * HD:(kv + 1) * G * HD, :].rearrange("(j e) n -> e j n", j=G)
                    sp.dma_start(dst[kv * HD:(kv + 1) * HD], half).then_inc(w_loaded[i % RING], 8 * 2)
                continue
            sp.dma_start(dst, src).then_inc(w_loaded[i % RING], 16)
        for m in range(16):
            wait_filled(sp, ("pq", m - WQ_RING, 1) if m >= WQ_RING else ("o2", 0, 0))
            sp.dma_start(wq_ring[m % WQ_RING], wqd[:, :, m * P:(m + 1) * P]).then_inc(wq_loaded[m % WQ_RING], 16)
        wait_emptied(sp, ("scs", 15))
        for h in range(PH):
            sp.dma_start(hs_in[h * S:(h + 1) * S], sc[0:S, NB * 16 + 2 * h:NB * 16 + 2 * h + 2, :]).then_inc(sample_rows_loaded, 16)
        for b in range(NB + 1):
            sp.wait_ge(y_ready, b + 1)
            dst = y_prompt[0, b * P:(b + 1) * P, :] if b < NB else y_sample[:, 0, :]
            sp.dma_start(dst, y_rows[0:rows(b), :]).then_inc(y_stored, 16)
        sp.wait_ge(y_stored, 16 * (NB + 1))

    def slot_rounds(i):
        n = 0
        for j in range(i % RING, i + 1, RING):
            n += 2 if chunks[j][0] == ("wa",) else 1
        return 16 * n

    @block.gpsimd
    def _(pool):
        pool.dma_start(gqk[:, 0, :], q_norm_g[0:1, :].broadcast_to((P, HD))).then_inc(small_loaded, 16)
        pool.dma_start(gqk[:, 1, :], k_norm_g[0:1, :].broadcast_to((P, HD))).then_inc(small_loaded, 16)
        pool.dma_start(sinks, attn_sinks[0:1, :].broadcast_to((P, HEADS))).then_inc(small_loaded, 16)
        for kv in range(KV):
            pool.dma_start(sinks4[0:G, kv:kv + 1],
                           attn_sinks[0, kv * G:(kv + 1) * G].rearrange("(j o) -> j o", o=1), allow_slow_non_contiguous=True).then_inc(small_loaded, 16)
        pool.dma_start(wpool, w_pool[0].rearrange("g c e -> c g e")).then_inc(small_loaded, 16)
        pool.dma_start(k0[0:S, :], cache_k[0, :, 0].rearrange("b h e -> b (h e)")).then_inc(small_loaded, 16)
        pool.dma_start(kc[:, P:], consts[:, P:]).then_inc(consts_loaded, 16)
        pool.wait_ge(qk_normed, 1)
        pool.dma_start(k_win_p[0, 0].rearrange("t h e -> t (h e)"), zqk[:, NB - 1, 512:640]).then_inc(windows_stored, 16)
        pool.dma_start(v_win_p[0, 0].rearrange("t h e -> t (h e)"), zv[:, NB - 1, :]).then_inc(windows_stored, 16)
        pool.dma_start(pool_p[0, 0], zp[P - HIST:P, NB - 1, :]).then_inc(windows_stored, 16)
        wait_filled(pool, ("d", 1))
        pool.dma_start(pext[0:HIST * S, :], state_pool[0].rearrange("b r c -> r b c")).then_inc(tail_loaded, 16)
        pool.dma_start(pext[HIST * S:P, :], zp[0:S, NB, :]).then_inc(tail_loaded, 16)
        pool.wait_ge(tail_loaded, 32)
        pool.dma_start(pool_s[0].rearrange("b r c -> r b c"), pext[S:P, :]).then_inc(windows_stored, 16)
        wait_filled(pool, ("gate", 2 * C - 1, 1))
        for cache, tile, new in ((cache_k, ktile, zqk[0:S, NB, 512:640]), (cache_v, vtile, zv[0:S, NB, :])):
            pool.dma_start(tile[0:WIN - 1], cache[0, :, 1:WIN].rearrange("b s h e -> s b (h e)")).then_inc(cache_loaded, 16)
            pool.dma_start(tile[WIN - 1:WIN], new).then_inc(cache_loaded, 16)
        pool.wait_ge(cache_loaded, 64)
        pool.dma_start(k_win_s[0].rearrange("b s h e -> s b (h e)"), ktile).then_inc(windows_stored, 16)
        pool.dma_start(v_win_s[0].rearrange("b s h e -> s b (h e)"), vtile).then_inc(windows_stored, 16)
        wait_filled(pool, ("y", PG - 1, 1))
        pool.dma_start(v0[0:1], cache_v[0:1, :, 0].rearrange("o b h e -> o b (h e)")).then_inc(oldest_v_loaded, 16)
        pool.wait_ge(merged_ready, 2 * C)
        pool.dma_start(sk_rows, peer_subkeys[0].rearrange("h c n e -> n (h c) e")).then_inc(subkeys_loaded, 16)
        wait_filled(pool, ("ada", 11))
        pool.memset(pool_pad, 0.0).then_inc(pad_ready, 1)
        pool.wait_ge(pad_ready, 1)
        def gather_turns(b, first, count):
            with pool.Fori(first, first + count) as it:
                for k in range(TURN):
                    n, side = it * TURN + (b * STEPS + k), k % 2
                    pool.wait_ge(u_used, n + 1)
                    pool.tensor_copy(idx_now[:, k, :],
                                     eidx[:, b, bass.ds(it * (TURN * GS) + k * GS, GS)]).then_inc(idx_copied, 1)
                    pool.wait_ge(idx_copied, n + 1)
                    for table, buf, landed in ((peer_u, u_rows, u_landed), (peer_v, v_rows, v_landed)):
                        if table is peer_v:
                            pool.wait_ge(v_used, n + 1)
                        c = 2 if table is peer_v else 1
                        pool.tensor_tensor(pool_pad[:, c:c + 1], pool_pad[:, 0:1], pool_pad[:, 0:1], ALU.mult)
                        for i in range(GS):
                            pool.indirect_dma_start(
                                out=buf[side * GS + i], out_offset=None, in_=table[0],
                                in_offset=bass.IndirectOffsetOnAxis(ap=idx_now[:, k, i:i + 1], axis=0),
                            ).then_inc(landed[side], 16)
        for t in range(OVER):
            pool.wait_ge(routed, t + 1)
            gather_turns(0, t, 1)
        pool.wait_ge(routed, OVER + 1)
        gather_turns(0, OVER, EARLY - OVER)
        pool.wait_ge(routed, OVER + 2)
        gather_turns(0, EARLY, TURNS - EARLY)
        for b in range(1, NB):
            gather_turns(b, 0, TURNS)
        pool.wait_ge(sample_routed, 1)
        for table, buf, used, landed in ((peer_u, u_rows, u_used, [sample_u_landed[t // GS] for t in range(S)]), (peer_v, v_rows, v_used, sample_v_landed)):
            for q in range(2):
                pool.wait_ge(used, AHEAD + NB * STEPS - 1 + q)
                for t in range(q * GS, (q + 1) * GS):
                    pool.indirect_dma_start(out=buf[t], out_offset=None, in_=table[0],
                                            in_offset=bass.IndirectOffsetOnAxis(ap=idx_s[:, t:t + 1], axis=0)).then_inc(landed[t], 16)
        pool.wait_ge(windows_stored, 16 * 6)

    @block.scalar
    def _(act):
        def empty(key, ops):
            wait_filled(act, key)
            for n, (out, in_, f, kw) in enumerate(ops):
                ins = act.activation(out, in_, f, **kw)
            ins.then_inc(emptied_by_act, 1)

        def copy(key, out, in_, f=ACT.Copy, **kw):
            empty(key, [(out, in_, f, kw)])

        act.wait_ge(c_loaded, 32)
        act.activation(silu9[0:9, :], c9[0:9, :], ACT.Silu).then_inc(silu_ready, 1)
        copy(("vecT",), vecT, bank(("vecT",))[:, 0:68])
        wait_filled(act, ("vecT",))
        copy(("cT",), scT, bank(("cT",))[:, 0:72].rearrange("p (a b) -> p a b", a=C))
        for c in range(C):
            copy(("xT", c), xT[:, c, 0:T], bank(("xT", c)))
        copy(("xTs",), xT[:, :, T:TT], bank(("xTs",))[:, 0:64].rearrange("p (a b) -> p a b", a=C))
        def ada(i):
            copy(("ada_rows", i), ada_rows[i][0:9, :], bank(("ada_rows", i))[0:9, :])

        ada(0)
        wait_emptied(act, ("ss", 1, 1))
        act.activation(root, msq, ACT.Sqrt).then_inc(root_ready, 1)
        for i in range(1, 4):
            ada(i)
        act.wait_ge(filler_ready, 1)
        for b in range(NB + 1):
            out = zqk[0:rows(b), b, 0:512].rearrange("p (j v e) -> p v j e", v=KV, e=HD)
            copy(("q", b), out, bank(("q", b))[0:rows(b)].rearrange("p (v j e) -> p v j e", v=KV, e=HD))
        for b in range(NB + 1):
            src = bank(("kv", b))[0:rows(b)]
            empty(("kv", b), [(zqk[0:rows(b), b, 512:640], src[:, 0:128], ACT.Copy, {}),
                              (zv[0:rows(b), b, :], src[:, 128:256], ACT.Copy, {})])
        for b in range(NB + 1):
            copy(("p", b), zp[0:rows(b), b, :], bank(("p", b))[0:rows(b)])
        def gates(ms):
            for m in ms:
                for h in range(2):
                    copy(("gate", m, h), (ga if m < C else gb)[:, m % C, half(h)], bank(("gate", m, h))[:, 0:HT], ACT.Sigmoid)

        gates(range(4))
        act.wait_ge(qk_mean_ready, 1)
        act.activation(qk_rms, qk_rms, ACT.Sqrt).then_inc(qk_root_ready, 1)
        gates(range(4, 8))
        for b in range(NB):
            copy(("qT", b), qkT[:, 0:4, cols(b)], bank(("qT", b)).rearrange("p (a b) -> p a b", a=4))
            copy(("kT", b), qkT[:, 4, cols(b)], bank(("kT", b))[:, 0:P])
        copy(("qkTs",), qkT[:, :, T:TT], bank(("qkTs",))[:, 0:40].rearrange("p (a b) -> p a b", a=5))

        def exps(b):
            lo = P if b == 0 else 0
            act.wait_ge(max_ready, b + 1)
            for h in range(HEADS):
                act.activation(sS[b % 2][:, h, lo:], sS[b % 2][:, h, lo:], ACT.Exp, bias=nmax[:, h:h + 1],
                               accum_out=ssum[:, h:h + 1])
            act.activation(ssink, ssink, ACT.Exp).then_inc(exps_ready, 1)

        def values(b):
            halves = (1,) if b == 0 else (0, 1)
            for kv in range(KV):
                if b or kv:
                    wait_filled(act, ("o", b, 0) if kv else ("o", b - 1, 1))
                for h in halves:
                    copy(("pt", b, kv, h), pT[:, h, :], bank(("pt", b, kv, h)))
                r = slice(kv * HD, (kv + 1) * HD)
                copy(("o", b, kv), attT[r, :, cols(b)], bank(("o", b, kv))[r].rearrange("p (a b) -> p a b", a=G))

        def pooled(b):
            copy(("d", b), dT[:, :, cols(b)], bank(("d", b)).rearrange("p (a b) -> p a b", a=PG))

        exps(0)
        pooled(0)
        gates((8, 9))
        exps(1)
        pooled(1)
        gates((10, 11))
        values(0)
        exps(2)
        pooled(2)
        gates((12, 13))
        values(1)
        exps(3)
        pooled(3)
        gates((14, 15))
        values(2)
        copy(("ds",), dT[:, :, T:TT], bank(("ds",))[:, 0:32].rearrange("p (a b) -> p a b", a=PG))
        ada(4)
        values(3)
        ada(5)
        ada(6)
        for i in range(2):
            copy(("ktT", i), kTs[:, 4 * i:4 * i + 4, :], bank(("ktT", i)).rearrange("p (a b) -> p a b", a=4))
        copy(("k0T",), k0T, bank(("k0T",))[:, 0:S])
        for h in range(2):
            for g in range(PG):
                copy(("y", g, h), bT[:, g, half(h)], bank(("y", g, h))[:, 0:HT], scale=vecT[:, 64 + g:65 + g])
        act.wait_ge(max_ready, NB + 1)
        act.activation(smisc[0:G, 1, :], smisc[0:G, 1, :], ACT.Exp)
        act.activation(sSs[0:G], sSs[0:G], ACT.Exp).then_inc(exps_ready, 1)
        src = bank(("pts",))
        empty(("pts",), [(pTs[:, 0:64], src[:, 0:64], ACT.Copy, {}), (pTs[0:1, 64:128], src[0:1, 64:128], ACT.Copy, {})])
        copy(("os",), attT[:, :, T:TT], bank(("os",))[:, 0:32].rearrange("p (b j) -> p j b", j=G))
        ada(7)
        for n in range(C):
            act.wait_ge(x1_ready, n + 1)
            act.activation(squares[:, n, :], xT[:, n, :], ACT.Square).then_inc(squares_ready, 1)
        for i in range(4):
            copy(("skT", i), at((o_g2b, o_y)[i // 2] + i % 2 * 512, 512), bank(("skT", i)))
        wait_emptied(act, ("ss", 2, 1))
        act.activation(root, msq, ACT.Sqrt).then_inc(root_ready, 1)
        for i in range(8, 12):
            ada(i)
        for b in range(NB + 1):
            for i in range(2):
                copy(("h2n", b, i), h2n[0:rows(b), b, i * 512:(i + 1) * 512], bank(("h2n", b, i))[0:rows(b)])
        def expert_step(n, side):
            act.wait_ge(u_used, n + 1 + AHEAD)
            act.activation(gelus[:, side, :], acts[:, side, :], ACT.Gelu_apprx_tanh).then_inc(gelu_done, 1)
            act.wait_ge(coef_ready, n + 1)
            act.wait_ge(v_used, n + 1)
            for i in range(GS):
                ins = act.activation(diags[:, side * GS + i, :], ident, ACT.Copy, scale=coefs[:, side, i:i + 1])
            ins.then_inc(diag_ready, 1)

        softmaxes = [0]

        def gate_exp(v):
            softmaxes[0] += 1
            act.wait_ge(best_ready, softmaxes[0])
            act.activation(v, v, ACT.Exp).then_inc(best_exp_ready, 1)

        scv = sc.rearrange("p (b m) n -> p b m n", b=5)
        for m in range(OVER_FROM + OVER * TURN):
            if 2 <= m < 16:
                wait_filled(act, ("scs", m - 2))
            for h in range(2 if m < 16 else 0):
                copy(("pq", m, h), pq[:, m % 2, half(h)], bank(("pq", m, h))[:, 0:HT])
            for i in score_tiles(m) if m <= 16 else ():
                copy(("scs", i), scv[0:S, NB, i, :], bank(("scs", i))[0:S, 0:NK])
            if m % 2 and 0 <= m // 2 - 1 < OVER:
                gate_exp(best[:, 0, (m // 2 - 1) * TOPK:m // 2 * TOPK])
            if m == 17:
                gate_exp(best[:, 0, OVER * TOPK:])
            if 0 <= m - OVER_FROM < OVER * TURN:
                expert_step(m - OVER_FROM, (m - OVER_FROM) % 2)
        for i in range(2):
            copy(("g2b", i), g2b[:, i * 512:(i + 1) * 512], bank(("g2b", i)))

        def expert_turns(b, first, count):
            with act.Fori(first, first + count) as it:
                for k in range(TURN):
                    expert_step(it * TURN + (b * STEPS + k), k % 2)

        for b in range(NB - 1):
            expert_turns(b, 0 if b else OVER, TURNS - (0 if b else OVER))
            gate_exp(best[:, b + 1, :])
        expert_turns(NB - 1, 0, 1)
        gate_exp(hs_best[0:PH * S])
        expert_turns(NB - 1, 1, 2)
        for i, dst in enumerate((xs_rows, g2s_rows)):
            act.wait_ge(sample_x_ready, i + 1)
            act.activation(dst[0:S, :].rearrange("p (a b) -> p a b", a=2), psum[0:S, 0:2, :], ACT.Copy).then_inc(sample_x_used, 1)
            expert_turns(NB - 1, 3 + i, 1)
        for t in range(S):
            for h in range(2):
                act.wait_ge(sample_h_ready, 2 * t + h + 1)
                act.activation(h_all[:, t, h * 512:(h + 1) * 512], psum[:, h, :], ACT.Copy).then_inc(sample_h_used, 1)
            if 5 + t < TURNS:
                expert_turns(NB - 1, 5 + t, 1)
        for q in range(2):
            act.wait_ge(sample_summed, (q + 1) * GS)
            act.activation(act_s[:, q * GS:(q + 1) * GS], act_s[:, q * GS:(q + 1) * GS], ACT.Gelu_apprx_tanh).then_inc(gelu_done, 1)

    @block.vector
    def _(dve):
        steps = [0, None]

        def link(ins):
            if steps[1] is not None:
                dve.drain()
                return
            ins.then_inc(dve_step, 1)
            steps[0] += 1
            dve.wait_ge(dve_step, steps[0])

        link(dve.memset(ones, 1.0))
        dve.wait_ge(dve_step, 1)
        dve.memset(nmax, 0.0).then_inc(ones_ready, 1)

        def mean_squares(n):
            for h in range(2):
                wait_filled(dve, ("ss", n, h))
                dve.tensor_scalar(msq[:, half(h)], bank(("ss", n, h))[:, 0:HT], 1.0 / D, EPS, ALU.mult, ALU.add).then_inc(emptied_by_dve, 1)

        def ada(i):
            wait_filled(dve, ("ada", i))
            bias = vecT[:, 4 * i:4 * i + 4].unsqueeze(2).broadcast_to((P, 4, 9))
            dve.tensor_tensor(mods[:, 4 * i:4 * i + 4, :], bank(("ada", i))[:, 0:36].rearrange("p (a b) -> p a b", a=4),
                              bias, ALU.add).then_inc(emptied_by_dve, 1)

        def normalize(n):
            dve.wait_ge(root_ready, n)
            link(dve.reciprocal(root, root))
            for c in range(C):
                ins = dve.tensor_tensor(hT[:, c, :], xT[:, c, :], root, ALU.mult)
            link(ins)

        def modulate(shift, scale, gain):
            wait_emptied(dve, ("ada", max(shift, scale) // 4 + 1))
            link(dve.scalar_tensor_tensor(smod, mods[:, scale:scale + C, :], 1.0,
                                          vecT[:, gain:gain + C].unsqueeze(2).broadcast_to((P, C, 9)), ALU.add, ALU.mult))
            hs = hT[:, :, T:TT]
            link(dve.tensor_tensor(hs, hs, smod[:, :, 1:9], ALU.mult))
            dve.tensor_tensor(hs, hs, mods[:, shift:shift + C, 1:9], ALU.add)
            for c in range(C):
                dve.tensor_scalar(hT[:, c, 0:T], hT[:, c, 0:T], smod[:, c, 0:1], mods[:, shift + c, 0:1], ALU.mult, ALU.add).then_inc(h_ready, 1)

        def add_squares(c, cs):
            link(dve.tensor_tensor(squares[:, 0, cs], squares[:, 0, cs], squares[:, c, cs], ALU.add))

        for c in range(C):
            wait_emptied(dve, ("xT", c))
            link(dve.tensor_tensor(squares[:, c, 0:T], xT[:, c, 0:T], xT[:, c, 0:T], ALU.mult))
            if c:
                add_squares(c, slice(0, T))
        wait_emptied(dve, ("xTs",))
        link(dve.tensor_tensor(squares[:, :, T:TT], xT[:, :, T:TT], xT[:, :, T:TT], ALU.mult))
        link(dve.tensor_reduce(res_s, squares[:, :, T:TT].rearrange("p c s -> p s c"), X, ALU.add))
        dve.tensor_copy(squares[:, 0, T:TT], res_s).then_inc(square_sum_ready, 1)
        mean_squares(1)
        normalize(1)
        for i in range(4):
            ada(i)
        modulate(0, C, 48)
        wait_emptied(dve, ("xTs",))
        dve.memset(zqk[:, NB, :], 1.0).then_inc(filler_ready, 1)
        wait_emptied(dve, ("kv", NB))
        dve.wait_ge(small_loaded, 16 * N_SMALL)
        dve.wait_ge(filler_ready, 1)
        heads = zqk.rearrange("p b n -> p (b n)").rearrange("p (h e) -> p h e", e=HD)
        zsqh = zsq.rearrange("p (h e) -> p h e", e=HD)
        link(dve.tensor_tensor(zsqh, heads, heads, ALU.mult))
        link(dve.tensor_reduce(qk_rms, zsqh, X, ALU.add))
        dve.tensor_scalar(qk_rms, qk_rms, 1.0 / HD, EPS, ALU.mult, ALU.add).then_inc(qk_mean_ready, 1)
        dve.wait_ge(qk_root_ready, 1)
        link(dve.reciprocal(qk_rms, qk_rms))
        link(dve.tensor_tensor(heads, heads, qk_rms.unsqueeze(2).broadcast_to((P, 50, HD)), ALU.mult))
        for b in range(NB + 1):
            q, k = zqk[:, b, 0:512].rearrange("p (h e) -> p h e", e=HD), zqk[:, b, 512:640].rearrange("p (h e) -> p h e", e=HD)
            dve.tensor_tensor(q, q, gqk[:, 0:1, :].broadcast_to((P, HEADS, HD)), ALU.mult)
            ins = dve.tensor_tensor(k, k, gqk[:, 1:2, :].broadcast_to((P, KV, HD)), ALU.mult)
        ins.then_inc(qk_normed, 1)

        bias = kc[:, K_BIAS:K_OWN].rearrange("p (h s) -> p h s", h=HEADS)

        def scores(b):
            lo = P if b == 0 else 0
            if b >= 2:
                wait_filled(dve, ("pt", b - 2, 1, 1))
            for j in range(G):
                wait_filled(dve, ("s", b, j))
                dve.scalar_tensor_tensor(sS[b % 2][:, 2 * j:2 * j + 2, lo:], bank(("s", b, j)).rearrange("p (v s) -> p v s", v=KV)[:, :, lo:],
                                         HD ** -0.5, bias[:, 2 * j:2 * j + 2, lo:], ALU.mult, ALU.add).then_inc(emptied_by_dve, 1)

        def maxima(b):
            lo = P if b == 0 else 0
            wait_emptied(dve, ("s", b, G - 1))
            link(dve.tensor_reduce(nmax, sS[b % 2][:, :, lo:], X, ALU.max))
            link(dve.tensor_tensor(nmax, nmax, sinks, ALU.max))
            link(dve.tensor_scalar(nmax, nmax, -1.0, None, ALU.mult))
            dve.tensor_tensor(ssink, sinks, nmax, ALU.add).then_inc(max_ready, 1)

        def probabilities(b):
            lo = P if b == 0 else 0
            dve.wait_ge(exps_ready, b + 1)
            link(dve.tensor_tensor(srec, ssum, ssink, ALU.add))
            link(dve.reciprocal(srec, srec))
            s = sS[b % 2][:, :, lo:]
            dve.tensor_tensor(s, s, srec.unsqueeze(2).broadcast_to((P, HEADS, 2 * P - lo)), ALU.mult).then_inc(probs_ready, 1)

        scores(0)
        maxima(0)
        for b in range(1, NB):
            scores(b)
            probabilities(b - 1)
            maxima(b)
        probabilities(NB - 1)
        for i in (4, 5, 6):
            ada(i)
        biass = kc[0:G, K_BIASS:K_HEAD].rearrange("p (v s) -> p v s", v=KV)
        for kv in range(KV):
            for h in range(2):
                wait_filled(dve, ("sc4", kv, h))
                i = kv * S + h * 4
                dve.scalar_tensor_tensor(sSs[0:G, i:i + 4, 1:], bank(("sc4", kv, h))[0:G].rearrange("p (b s) -> p b s", b=4), HD ** -0.5,
                                         biass[:, kv:kv + 1, 1:].broadcast_to((G, 4, WIN)), ALU.mult, ALU.add).then_inc(emptied_by_dve, 1)
        for kv in range(KV):
            wait_filled(dve, ("sc0", kv))
            dve.scalar_tensor_tensor(sSs[0:G, kv * S:(kv + 1) * S, 0:1], bank(("sc0", kv))[0:G, 0:S].unsqueeze(2), HD ** -0.5,
                                           biass[:, kv:kv + 1, 0:1].broadcast_to((G, S, 1)), ALU.mult, ALU.add).then_inc(emptied_by_dve, 1)
        wait_emptied(dve, ("sc0", KV - 1))
        sk = sinks4[0:G, :].unsqueeze(2).broadcast_to((G, KV, S))
        m_max, m_sink, m_sum = (smisc[0:G, i, :] for i in range(3))
        link(dve.tensor_reduce(m_max, sSs[0:G], X, ALU.max))
        link(dve.tensor_tensor(m_max.rearrange("p (v b) -> p v b", v=KV), m_max.rearrange("p (v b) -> p v b", v=KV), sk, ALU.max))
        link(dve.tensor_tensor(m_sink.rearrange("p (v b) -> p v b", v=KV), sk, m_max.rearrange("p (v b) -> p v b", v=KV), ALU.subtract))
        dve.tensor_tensor(sSs[0:G], sSs[0:G], m_max.unsqueeze(2).broadcast_to((G, 16, WIN + 1)), ALU.subtract).then_inc(max_ready, 1)
        dve.wait_ge(exps_ready, NB + 1)
        link(dve.tensor_reduce(m_sum, sSs[0:G], X, ALU.add))
        link(dve.tensor_tensor(m_sum, m_sum, m_sink, ALU.add))
        link(dve.reciprocal(m_sum, m_sum))
        dve.tensor_tensor(sSs[0:G], sSs[0:G], m_sum.unsqueeze(2).broadcast_to((G, 16, WIN + 1)), ALU.mult).then_inc(probs_ready, 1)
        dve.wait_ge(windows_stored, 16 * 6)
        for h in range(2):
            hs = half(h)
            for n in range(C):
                wait_filled(dve, ("A", n, h))
                dve.tensor_tensor(mT[:, n, hs], bank(("A", n, h))[:, 0:HT], ga[:, n, hs], ALU.mult).then_inc(emptied_by_dve, 1)
                wait_filled(dve, ("B", n, h))
                dve.tensor_tensor(gb[:, n, hs], bank(("B", n, h))[:, 0:HT], gb[:, n, hs], ALU.mult).then_inc(emptied_by_dve, 1)
                wait_emptied(dve, ("B", n, h))
                dve.tensor_tensor(mT[:, n, hs], mT[:, n, hs], gb[:, n, hs], ALU.add).then_inc(merged_ready, 1)
        ada(7)
        for n in range(C):
            wait_filled(dve, ("o2", n, 0))
            dve.scalar_tensor_tensor(xT[:, n, half(0)], bank(("o2", n, 0))[:, 0:HT], mods[:, 16 + n, 0:1], xT[:, n, half(0)],
                                     ALU.mult, ALU.add).then_inc(emptied_by_dve, 1)
            wait_filled(dve, ("o2", n, 1))
            o = bank(("o2", n, 1))
            dve.scalar_tensor_tensor(xT[:, n, HT:T], o[:, 0:T - HT], mods[:, 16 + n, 0:1], xT[:, n, HT:T], ALU.mult, ALU.add)
            dve.tensor_tensor(res_s, o[:, T - HT:HT], mods[:, 16 + n, 1:9], ALU.mult).then_inc(emptied_by_dve, 1)
            wait_emptied(dve, ("o2", n, 1))
            dve.tensor_tensor(xT[:, n, T:TT], xT[:, n, T:TT], res_s, ALU.add).then_inc(x1_ready, 1)
            dve.wait_ge(x1_ready, n + 1)
            if n >= 2:
                dve.wait_ge(squares_ready, n)
                add_squares(n - 1, slice(0, TT))
        dve.wait_ge(squares_ready, C)
        dve.tensor_tensor(squares[:, 0, :], squares[:, 0, :], squares[:, C - 1, :], ALU.add).then_inc(square_sum_ready, 1)
        dve.memset(h2n[:, NB, :], 0.0)
        mean_squares(2)
        normalize(2)
        ada(8)
        ada(9)
        modulate(24, 32, 56)
        ada(10)
        ada(11)
        scv = sc.rearrange("p (b m) n -> p b m n", b=5)
        link(dve.memset(zeros, 0.0))
        dve.memset(gelus, 0.0).then_inc(u_used, AHEAD)
        dve.wait_ge(u_used, AHEAD)

        iota = kc[:, K_IOTA:K_IOTA + TOPK]

        def first8(values, index, src, cut):
            for v, s in zip(values, src):
                dve.max(v[:, 0:8], s)
            dve.drain()
            for v, i, s, c in zip(values, index, src, cut):
                dve.max_index(i[:, 0:8], v[:, 0:8], s)
                dve.match_replace(c, v[:, 0:8], s, -3e38)
            dve.drain()

        def next8(values, index, cut):
            for v, c in zip(values, cut):
                dve.max(v[:, 8:16], c)
            dve.drain()
            for v, i, c in zip(values, index, cut):
                dve.max_index(i[:, 8:16], v[:, 8:16], c)
            dve.drain()

        def route(R, scores_in, best_out, experts_out, part):
            halves = range(2)
            vals, idxs = [r_val[0:R, c, :] for c in halves], [r_idx[0:R, c, :] for c in halves]
            cuts = [r_cut[0:R, c, :] for c in halves]
            flat = r_cand[0:R].rearrange("p a b -> p (a b)")
            if part == 0:
                dve.tensor_copy(r_in[0:R], scores_in)
                dve.drain()
                first8(vals, idxs, [r_in[0:R, c, :] for c in halves], cuts)
            if part == 1:
                next8(vals, idxs, cuts)
                dve.tensor_copy(r_idxf[0:R], r_idx[0:R])
                dve.tensor_tensor(r_cand[0:R], r_val[0:R, 0, :].unsqueeze(2).broadcast_to((R, TOPK, TOPK)),
                                  r_val[0:R, 1, :].unsqueeze(1).broadcast_to((R, TOPK, TOPK)), ALU.add)
                dve.drain()
            if part == 2:
                first8([r_best[0:R]], [r_pos[0:R]], [flat], [r_cand2[0:R]])
                next8([r_best[0:R]], [r_pos[0:R]], [r_cand2[0:R]])
            if part == 3:
                dve.tensor_copy(best_out, r_best[0:R])
                dve.tensor_scalar(r_half[0:R, 0, :], r_pos[0:R], 4, None, ALU.logical_shift_right)
                dve.tensor_scalar(r_half[0:R, 1, :], r_pos[0:R], 15, None, ALU.bitwise_and)
                dve.drain()
                dve.tensor_copy(r_halff[0:R], r_half[0:R])
                dve.drain()
                hot = r_hot[0:R].rearrange("p (c k) i -> p c k i", c=2)
                dve.tensor_tensor(r_hot[0:R], r_halff[0:R].rearrange("p c k -> p (c k)").unsqueeze(2).broadcast_to((R, 2 * TOPK, TOPK)),
                                  iota[0:R].unsqueeze(1).broadcast_to((R, 2 * TOPK, TOPK)), ALU.is_equal)
                dve.drain()
                dve.tensor_tensor(hot, hot, r_idxf[0:R].unsqueeze(2).broadcast_to((R, 2, TOPK, TOPK)), ALU.mult)
                dve.drain()
                dve.tensor_reduce(r_pick[0:R].rearrange("p c k -> p (c k)"), r_hot[0:R], X, ALU.add)
                dve.drain()
                dve.scalar_tensor_tensor(r_e[0:R], r_pick[0:R, 0, :], float(NK), r_pick[0:R, 1, :], ALU.mult, ALU.add)
                dve.drain()
                dve.tensor_copy(experts_out, r_e[0:R])
                dve.drain()

        def route_head(b, h, part):
            hs = bass.ds(h * TOPK, TOPK)
            route(P, scv[:, b, bass.ds(h * 2, 2), :], best[:, b, hs], eidx[:, b, hs], part)

        def softmax_begin(v, top):
            link(dve.tensor_copy(top, v[:, :, 0:1]))
            dve.tensor_tensor(v, v, top.broadcast_to(v.shape), ALU.subtract).then_inc(best_ready, 1)

        softmaxes = [0]

        def softmax_end(v, total):
            softmaxes[0] += 1
            dve.wait_ge(best_exp_ready, softmaxes[0])
            link(dve.tensor_reduce(total, v, X, ALU.add))
            link(dve.reciprocal(total, total))
            link(dve.tensor_tensor(v, v, total.unsqueeze(2).broadcast_to(v.shape), ALU.mult))

        def block_softmax(b):
            v = best[:, b, :].rearrange("p (h k) -> p h k", k=TOPK)
            softmax_begin(v, r_max.unsqueeze(2))
            softmax_end(v, r_sum)

        def loop(first, end, body):
            with dve.Fori(first, end) as it:
                steps[1] = it
                body(it)
            steps[1] = None

        def step(b, it, k, routing):
            n, side = it * TURN + (b * STEPS + k), k % 2
            dve.wait_ge(u_landed[side], it * (TURN // 2 * GS * 16) + (b * STEPS // 2 + k // 2 + 1) * GS * 16)
            for i in range(GS):
                rows_i = u_rows[side * GS + i]
                ins = dve.tensor_tensor_reduce(rows_i, rows_i, h2n[:, b, :], 1.0, 0.0,
                                               ALU.mult, ALU.add, acts[:, side, i:i + 1])
            ins.then_inc(u_used, 1)
            routing(it, k)
            dve.wait_ge(gelu_done, n + 1)
            dve.tensor_tensor(coefs[:, side, :], gelus[:, side, :],
                              best[:, b, bass.ds(it * (TURN * GS) + k * GS, GS)], ALU.mult).then_inc(coef_ready, 1)

        wait_emptied(dve, ("h2n", NB, 1))
        others = best[:, 0, OVER * TOPK:].rearrange("p (h k) -> p h k", k=TOPK)
        first_parts = {17: (0, 1), 18: (2, 3)}
        for m in range(1, OVER_FROM + OVER * TURN):
            if m <= 16:
                wait_filled(dve, ("sc", m - 1))
                dve.tensor_copy(scv[:, 0:NB, m - 1, :], bank(("sc", m - 1)).rearrange("p (a b) -> p a b", a=NB)).then_inc(emptied_by_dve, 1)
            if m == 18:
                softmax_end(others, r_sum[:, OVER:])
            if m % 2 and 0 <= m // 2 - 1 < OVER:
                t = m // 2 - 1
                softmax_end(best[:, 0, t * TOPK:(t + 1) * TOPK].unsqueeze(1), r_sum[:, t:t + 1])
            if 0 <= m - OVER_FROM < OVER * TURN:
                turn, k = divmod(m - OVER_FROM, TURN)
                step(0, turn, k, lambda head, part: [route_head(1, 0, p) for p in first_parts.get(m, ())])
            if m % 2 == 0 and m <= 16:
                head = m // 2 - 1
                wait_emptied(dve, ("sc", m - 1))
                for part in range(4):
                    route_head(0, head, part)
                if head < OVER:
                    softmax_begin(best[:, 0, head * TOPK:(head + 1) * TOPK].unsqueeze(1), r_max[:, head:head + 1].unsqueeze(2))
                if head == PH - 1:
                    softmax_begin(others, r_max[:, OVER:].unsqueeze(2))
                if head < OVER or head == EARLY - 1:
                    dve.nop().then_inc(routed, 1)
        dve.nop().then_inc(routed, 1)

        def finish(b):
            dve.wait_ge(v_used, AHEAD + (b + 1) * STEPS)
            if b:
                dve.wait_ge(y_stored, 16 * b)
            for i in range(2):
                h = slice(i * 512, (i + 1) * 512)
                ins = dve.tensor_tensor(y_rows[:, h], psum[:, 2 * (b % 2) + i, :], g2b[:, h], ALU.mult)
            ins.then_inc(sum_read, 1)
            dve.wait_ge(sum_read, b + 1)
            dve.wait_ge(x1_rows_ready, b + 1)
            for i in range(2):
                h = slice(i * 512, (i + 1) * 512)
                ins = dve.tensor_tensor(y_rows[:, h], y_rows[:, h], psum[:, 4 + 2 * (b % 2) + i, :], ALU.add)
            ins.then_inc(y_ready, 1)

        for b in range(NB):
            def one_turn(it, routing):
                for k in range(TURN):
                    step(b, it, k, routing)

            if b < NB - 1:
                def turn(it):
                    one_turn(it, lambda head, part: route_head(b + 1, head, part))

                if b:
                    steps[1] = 0
                    turn(0)
                    steps[1] = None
                    finish(b - 1)
                else:
                    def turn_of_two(it):
                        def two_parts(it, k):
                            head = (it - OVER) * 2 + (k // 2 + 1)
                            route_head(1, head, k % 2 * 2)
                            route_head(1, head, k % 2 * 2 + 1)
                        one_turn(it, two_parts)

                    loop(OVER, TURNS - 1, turn_of_two)
                loop(1 if b else TURNS - 1, TURNS, turn)
                block_softmax(b + 1)
            else:
                HS = PH * S
                dve.wait_ge(sample_rows_loaded, 16 * PH)
                one_turn(0, lambda head, part: route(HS, hs_in[0:HS], hs_best[0:HS], hs_expert[0:HS], part))
                finish(b - 1)
                v = hs_best[0:HS].unsqueeze(1)
                softmax_begin(v, hs_max[0:HS].unsqueeze(2))
                softmax_end(v, hs_sum[0:HS])
                dve.tensor_copy(pick_s, ident[:, 0:S].unsqueeze(2).broadcast_to((P, S, P)))
                link(dve.memset(coef_s, 0.0))
                for i, src in enumerate((hs_expert, hs_best)):
                    dve.tensor_tensor(hs_spread[0:HS, i, :].rearrange("p (h k) -> p h k", h=PH), src[0:HS].unsqueeze(1).broadcast_to((HS, PH, TOPK)),
                                      kc[0:HS, K_HEAD:K_SEQ].unsqueeze(2).broadcast_to((HS, PH, TOPK)), ALU.mult).then_inc(sample_spread, 1)
                loop(1, 4, lambda it: one_turn(it, lambda head, part: None))
                dve.wait_ge(sample_turned, 1)
                dve.tensor_copy(idx_s, psum[:, 4, 0:S]).then_inc(sample_routed, 1)
                dve.tensor_copy(gate_s, psum[:, 4, S:2 * S]).then_inc(sample_routed, 1)
                loop(4, TURNS, lambda it: one_turn(it, lambda head, part: None))
        finish(NB - 1)
        def sample_coefs(q):
            dve.wait_ge(gelu_done, NB * STEPS + q + 1)
            qs, first = slice(q * GS, (q + 1) * GS), q * GS * (S + 1)
            dve.tensor_tensor(coef_s[:, first:first + 3 * (S + 1) + 1:S + 1], act_s[:, qs], gate_s[:, qs], ALU.mult).then_inc(sample_coef_ready, 1)

        for q in range(2):
            dve.wait_ge(sample_u_landed[q], 16 * GS)
            for t in range(q * GS, (q + 1) * GS):
                dve.wait_ge(sample_h_used, 2 * t + 2)
                if t == GS + 1:
                    sample_coefs(0)
                dve.tensor_tensor_reduce(u_rows[t], u_rows[t], h_all[:, t, :], 1.0, 0.0,
                                         ALU.mult, ALU.add, act_s[:, t:t + 1]).then_inc(sample_summed, 1)
        sample_coefs(1)
        dve.wait_ge(y_stored, 16 * NB)
        dve.wait_ge(sample_x_used, 2)
        for i in range(2):
            h = slice(i * 512, (i + 1) * 512)
            dve.wait_ge(sample_out_ready, i + 1)
            link(dve.tensor_tensor(y_rows[0:S, h], psum[0:S, 4 + i, :], g2s_rows[0:S, h], ALU.mult))
            ins = dve.tensor_tensor(y_rows[0:S, h], y_rows[0:S, h], xs_rows[0:S, h], ALU.add)
        ins.then_inc(y_ready, 1)

    @block.tensor
    def _(pe):
        def begin(key):
            before = content_before[order[key]]
            if before is not None:
                wait_emptied(pe, plan[before][0])
            return bank(key)

        def end(ins):
            ins.then_inc(bank_filled, 1)

        def chunk(key):
            i = chunk_at[key]
            pe.wait_ge(w_loaded[i % RING], slot_rounds(i))
            k = 4 if key[0] in ("wa", "wb") else 8
            return ring[i % RING].rearrange("p (k n) -> p k n", k=k)

        def product(out, pairs):
            for n, (a, b) in enumerate(pairs):
                ins = pe.matmul(out, a, b, start=(n == 0), stop=(n == len(pairs) - 1))
            return ins

        def mean_squares(n):
            for h in range(2):
                o = begin(("ss", n, h))[:, 0:HT]
                pe.wait_ge(square_sum_ready, n)
                ins = pe.matmul(o, ones, squares[:, 0, half(h)], start=True, stop=True)
                end(ins)

        def halves(key, w, n, x, ks):
            ns = slice(n * P, (n + 1) * P)
            for h in range(2):
                end(product(begin((*key, h))[:, 0:HT], [(w[:, k, ns], x[:, k, half(h)]) for k in range(ks)]))

        def ada_products(i):
            w = chunk(("ada", i))
            end(product(begin(("ada_rows", i))[0:9, :], [(scT[:, k, :], w[:, k, :]) for k in range(8)]))

        def ada(i):
            o = begin(("ada", i))
            wait_emptied(pe, ("ada_rows", i))
            for n in range(4):
                ins = pe.transpose(o[:, n * 9:(n + 1) * 9], ada_rows[i][0:9, n * P:(n + 1) * P], ident[0:9, 0:9])
            end(ins)

        pe.wait_ge(ident_loaded, 16)
        pe.wait_ge(vecs_loaded, 16 * 4)
        end(pe.transpose(begin(("vecT",))[:, 0:68], vec68[0:68, :], ident[0:68, 0:68]))
        pe.wait_ge(silu_ready, 1)
        o = begin(("cT",))
        for c in range(C):
            ins = pe.transpose(o[:, c * 9:(c + 1) * 9], silu9[0:9, c * P:(c + 1) * P], ident[0:9, 0:9])
        end(ins)
        pe.wait_ge(x_loaded, 16 * 5)
        for c in range(C):
            o = begin(("xT", c))
            for b in range(NB):
                ins = pe.transpose(o[:, b * P:(b + 1) * P], xnat[:, b, c * P:(c + 1) * P], ident)
            end(ins)
        o = begin(("xTs",))
        for c in range(C):
            ins = pe.transpose(o[:, c * S:(c + 1) * S], xnat[0:S, NB, c * P:(c + 1) * P], ident[0:S, 0:S])
        end(ins)
        wait_emptied(pe, ("cT",))
        ada_products(0)
        pe.wait_ge(ones_ready, 1)
        mean_squares(1)
        for i in range(1, 4):
            ada_products(i)
            ada(i - 1)
        ada(3)
        for w, n in (("q", 512), ("kv", 256), ("p", 512)):
            wt = chunk((w,))
            for b in range(NB + 1):
                o = begin((w, b))[0:rows(b), 0:n]
                for k in range(C):
                    if (w, b) == ("q", 0):
                        pe.wait_ge(h_ready, k + 1)
                    ins = pe.matmul(o, hT[:, k, cols(b)], wt[:, k, 0:n], start=(k == 0), stop=(k == C - 1))
                end(ins)

        def gates(ms):
            for m in ms:
                halves(("gate", m), chunk(("gate", m // 4)), m % 4, hT, C)

        gates(range(8))
        pe.wait_ge(qk_normed, 1)
        for b in range(NB):
            o = begin(("qT", b))
            for j in range(G):
                ins = pe.transpose(o[:, j * P:(j + 1) * P], zqk[:, b, j * P:(j + 1) * P], ident)
            end(ins)
            end(pe.transpose(begin(("kT", b))[:, 0:P], zqk[:, b, 512:640], ident))
        o = begin(("qkTs",))
        for j in range(G + 1):
            ins = pe.transpose(o[:, j * S:(j + 1) * S], zqk[0:S, NB, j * P:(j + 1) * P], ident[0:S, 0:S])
        end(ins)

        def scores(b):
            wait_emptied(pe, ("kT", b))
            lo = P if b == 0 else 0
            for j in range(G):
                o = begin(("s", b, j))
                r = slice(j // 2 * HD, (j // 2 + 1) * HD)
                for i in range(2):
                    ins = pe.matmul(o[:, i * 2 * P + lo:(i + 1) * 2 * P], qkT[r, j % 2 * 2 + i, cols(b)],
                                    qkT[r, 4, (b - 1) * P + lo:(b + 1) * P], start=True, stop=True)
                end(ins)

        def pooled(b):
            own = K_OWN if b else K_FIRST
            o = begin(("d", b))
            for g in range(PG):
                gs = slice(g * P, (g + 1) * P)
                pairs = [(zp[:, b, gs], kc[:, own + g * P:own + (g + 1) * P])]
                if b:
                    pairs += [(zp[:, b - 1, gs], kc[:, K_PREV + g * P:K_PREV + (g + 1) * P])]
                ins = product(o[:, gs], pairs)
            end(ins)

        def values(b):
            halves = (1,) if b == 0 else (0, 1)
            pe.wait_ge(probs_ready, b + 1)
            for kv in range(KV):
                for h in halves:
                    o = begin(("pt", b, kv, h))
                    for j in range(G):
                        ins = pe.transpose(o[:, j * P:(j + 1) * P], sS[b % 2][:, kv * G + j, h * P:(h + 1) * P], ident)
                    end(ins)
                o = begin(("o", b, kv))
                wait_emptied(pe, ("pt", b, kv, 1))
                end(product(o[kv * HD:(kv + 1) * HD, :], [(zv[:, b - 1 + h, kv * HD:(kv + 1) * HD], pT[:, h, :]) for h in halves]))

        pe.wait_ge(consts_loaded, 16)
        scores(0)
        pooled(0)
        gates((8, 9))
        scores(1)
        pooled(1)
        gates((10, 11))
        values(0)
        scores(2)
        pooled(2)
        gates((12, 13))
        values(1)
        scores(3)
        pooled(3)
        gates((14, 15))
        values(2)
        pe.wait_ge(tail_loaded, 32)
        o = begin(("ds",))
        for g in range(PG):
            ins = pe.matmul(o[:, g * S:(g + 1) * S], pext[:, g * P:(g + 1) * P], kc[:, K_POOLS + g * S:K_POOLS + (g + 1) * S],
                            start=True, stop=True)
        end(ins)
        ada_products(4)
        values(3)
        ada(4)
        ada_products(5)
        ada_products(6)
        ada(5)
        ada(6)
        pe.wait_ge(cache_loaded, 64)
        for i in range(2):
            o = begin(("ktT", i))
            for b in range(4):
                ins = pe.transpose(o[:, b * P:(b + 1) * P], ktile[:, 4 * i + b, :], ident)
            end(ins)
        end(pe.transpose(begin(("k0T",))[:, 0:S], k0[0:S, :], ident[0:S, 0:S]))
        wait_emptied(pe, ("k0T",))
        for kv in range(KV):
            r = slice(kv * HD, (kv + 1) * HD)
            for h in range(2):
                o = begin(("sc4", kv, h))
                for b in range(4):
                    s = 4 * h + b
                    ins = pe.matmul(o[0:G, b * P:(b + 1) * P], qkT[r, 0:G, T + s], kTs[r, s, :], start=True, stop=True)
                end(ins)
        for kv in range(KV):
            o = begin(("sc0", kv))
            r = slice(kv * HD, (kv + 1) * HD)
            for s in range(S):
                ins = pe.matmul(o[0:G, s:s + 1], qkT[r, 0:G, T + s], k0T[r, s:s + 1], start=True, stop=True)
            end(ins)
        wait_emptied(pe, ("ds",))
        for h in range(2):
            for g in range(PG):
                end(pe.matmul(begin(("y", g, h))[:, 0:HT], wpool[:, g, :], dT[:, g, half(h)], start=True, stop=True))
        wa, wb = chunk(("wa",)), chunk(("wb",))

        def branches(h):
            for n in range(C):
                ns = slice(n * P, (n + 1) * P)
                for key, w, x in (("A", wa, attT), ("B", wb, bT)):
                    end(product(begin((key, n, h))[:, 0:HT], [(w[:, k, ns], x[:, k, half(h)]) for k in range(4)]))

        wait_emptied(pe, ("y", PG - 1, 1))
        branches(0)
        pe.wait_ge(probs_ready, NB + 1)
        o = begin(("pts",))
        for i in range(16):
            pe.transpose(o[:, i * G:(i + 1) * G], sSs[0:G, i, 1:], ident[0:G, 0:G])
        for i in range(16):
            ins = pe.transpose(o[0:1, 64 + i * G:64 + (i + 1) * G], sSs[0:G, i, 0:1], ident[0:G, 0:G])
        end(ins)
        pe.wait_ge(oldest_v_loaded, 16)
        o = begin(("os",))
        wait_emptied(pe, ("pts",))
        for kv in range(KV):
            r = slice(kv * HD, (kv + 1) * HD)
            for s in range(S):
                i = (kv * S + s) * G
                out = o[r, s * G:(s + 1) * G]
                pe.matmul(out, vtile[:, s, r], pTs[:, i:i + G], start=True, stop=False)
                ins = pe.matmul(out, v0[0:1, s, r], pTs[0:1, 64 + i:64 + i + G], start=False, stop=True)
        end(ins)
        wait_emptied(pe, ("os",))
        branches(1)
        ada_products(7)
        ada(7)
        pe.wait_ge(merged_ready, 2 * C)
        for n in range(C):
            halves(("o2", n), chunk(("wo", n // 4)), n % 4, mT, C)
        pe.wait_ge(subkeys_loaded, 16)
        for i in range(4):
            o = begin(("skT", i))
            for m in range(4):
                ins = pe.transpose(o[:, m * P:(m + 1) * P], sk_rows[:, 4 * i + m, :], ident)
            end(ins)
        mean_squares(2)
        for i in (8, 10):
            ada_products(i)
            ada_products(i + 1)
            ada(i)
            ada(i + 1)
        pe.wait_ge(h_ready, 2 * C)
        for b in range(NB + 1):
            for i in range(2):
                o = begin(("h2n", b, i))
                for c in range(4):
                    ins = pe.transpose(o[0:rows(b), c * P:(c + 1) * P], hT[:, 4 * i + c, cols(b)], ident)
                end(ins)

        def subkey_scores(m):
            o = begin(("sc", m))
            wait_emptied(pe, ("pq", m, 1))
            for b in range(NB):
                ins = pe.matmul(o[:, b * P:(b + 1) * P], pq[:, m % 2, b * P:(b + 1) * P], skT[m], start=True, stop=True)
            end(ins)
            end(pe.matmul(begin(("scs", m))[0:S, 0:NK], pq[:, m % 2, T:TT], skT[m], start=True, stop=True))

        def clear_sums(b):
            for i in range(2):
                pe.matmul(psum[:, 2 * (b % 2) + i, :], zeros, zeros[:, 0:1].broadcast_to((P, 512)),
                          start=True, stop=False, skip_group_check=True)

        def expert_step(b, it, k):
            n, side = it * TURN + (b * STEPS + k), k % 2
            pe.wait_ge(v_landed[side], it * (TURN // 2 * GS * 16) + (b * STEPS // 2 + k // 2 + 1) * GS * 16)
            pe.wait_ge(diag_ready, n + 1)
            for i in range(GS):
                for h in range(2):
                    ins = pe.matmul(psum[:, 2 * (b % 2) + h, :], diags[:, side * GS + i, :],
                                    v_rows[side * GS + i][:, h * 512:(h + 1) * 512],
                                    start=False, stop=False, skip_group_check=True)
            ins.then_inc(v_used, 1)

        def expert_turns(b, first, count):
            with pe.Fori(first, first + count) as it:
                for k in range(TURN):
                    expert_step(b, it, k)

        pe.wait_ge(u_used, AHEAD)
        pe.nop().then_inc(v_used, AHEAD)
        for m in range(OVER_FROM + OVER * TURN + 1):
            if m < 16:
                pe.wait_ge(wq_loaded[m % WQ_RING], 16 * (m // WQ_RING + 1))
                halves(("pq", m), wq_ring[m % WQ_RING], 0, hT, C)
            for i in score_tiles(m) if m <= 16 else ():
                subkey_scores(i)
            if m == OVER_FROM:
                for i in range(2):
                    wait_emptied(pe, plan[max(j for j in range(len(plan)) if bank_of[j] == i)][0])
                clear_sums(0)
            if 0 <= m - 1 - OVER_FROM < OVER * TURN:
                expert_step(0, *divmod(m - 1 - OVER_FROM, TURN))
        wait_emptied(pe, ("ada", 11))
        for i in range(2):
            o = begin(("g2b", i))
            for c in range(4):
                ins = pe.matmul(o[:, c * P:(c + 1) * P], mods[:, 40 + 4 * i + c, 0:1].broadcast_to((P, P)), ident, start=True, stop=True)
            end(ins)
        for key, _ in plan[-BANKS:]:
            wait_emptied(pe, key)

        for b in range(NB):
            if b >= 2:
                pe.wait_ge(sum_read, b - 1)
            if b:
                clear_sums(b)
            if b >= 2:
                pe.wait_ge(y_ready, b - 1)
            for i in range(2):
                for c in range(4):
                    ins = pe.transpose(psum[:, 4 + 2 * (b % 2) + i, c * P:(c + 1) * P], xT[:, 4 * i + c, cols(b)], ident)
            ins.then_inc(x1_rows_ready, 1)
            if b < NB - 1:
                expert_turns(b, 0 if b else OVER, TURNS - (0 if b else OVER))
            else:
                expert_turns(b, 0, 2)
                pe.wait_ge(sample_spread, 2)
                pe.wait_ge(y_ready, b)
                for i in range(2):
                    ins = pe.matmul(psum[:, 4, i * S:(i + 1) * S], hs_spread[0:PH * S, i, :], kc[0:PH * S, K_SEQ:K_END], start=True, stop=True)
                ins.then_inc(sample_turned, 1)
                for i, (src, first) in enumerate(((xT, T), (mods[:, 40:48, :], 1))):
                    if i == 0:
                        pe.wait_ge(sum_read, b)
                    else:
                        pe.wait_ge(sample_x_used, 1)
                    for c in range(C):
                        ins = pe.transpose(psum[0:S, c // 4, c % 4 * P:(c % 4 + 1) * P], src[:, c, first:first + S], ident)
                    ins.then_inc(sample_x_ready, 1)
                    expert_turns(b, 2 + i, 1)
                pe.wait_ge(sample_x_used, 2)
                for t in range(S):
                    for h in range(2):
                        if t:
                            pe.wait_ge(sample_h_used, 2 * t + h - 1)
                        pe.matmul(psum[:, h, :], pick_s[:, t, :], h2n[:, NB, h * 512:(h + 1) * 512],
                                  start=True, stop=True).then_inc(sample_h_ready, 1)
                    if 4 + t < TURNS:
                        expert_turns(b, 4 + t, 1)
        pe.wait_ge(sample_routed, 2)
        for q in range(2):
            pe.wait_ge(sample_coef_ready, q + 1)
            for t in range(q * GS, (q + 1) * GS):
                pe.wait_ge(sample_v_landed[t], 16)
                for h in range(2):
                    ins = pe.matmul(psum[0:S, 4 + h, :], coef_s[:, t * S:(t + 1) * S], v_rows[t][:, h * 512:(h + 1) * 512],
                                    start=(t == 0), stop=(t == S - 1), skip_group_check=True)
                    if t == S - 1:
                        ins.then_inc(sample_out_ready, 1)

    block.__exit__(None, None, None)


_INS = ['x_prompt', 'x_sample', 'cache_k', 'cache_v', 'state_pool', 'c_prompt', 'c_sample', 'norm1_g', 'norm2_g', 'w_ada',
        'b_ada', 'w_in', 'q_norm_g', 'k_norm_g', 'attn_sinks', 'w_pool', 'pool_scale', 'w_branch_attn', 'w_branch_pool',
        'w_out', 'peer_wq', 'peer_subkeys', 'peer_u', 'peer_v']
_OUTS = [(1, T, D), (S, 1, D), (1, 1, WIN, KV, HD), (1, 1, WIN, KV, HD), (1, 1, HIST, PW),
         (1, S, WIN, KV, HD), (1, S, WIN, KV, HD), (1, S, HIST, PW)]


def kernel(**inputs):
    import concourse.bacc as bacc
    from concourse.bass_utils import run_bass_kernel_spmd

    nc = bacc.Bacc("TRN2", target_bir_lowering=False, num_devices=1)
    arrays, args = {}, []
    for name in _INS:
        a = np.ascontiguousarray(inputs[name])
        arrays[f"in_{name}"] = a
        args.append(nc.dram_tensor(f"in_{name}", a.shape, mybir.dt.from_np(a.dtype), kind="ExternalInput").ap())
    arrays["in_consts"] = constants()
    args.append(nc.dram_tensor("in_consts", arrays["in_consts"].shape, F32, kind="ExternalInput").ap())
    for i, shape in enumerate(_OUTS):
        args.append(nc.dram_tensor(f"out_{i}", shape, F32, kind="ExternalOutput").ap())
    decoder_layer(nc, *args)
    r = run_bass_kernel_spmd(nc, [arrays], core_ids=[0])
    return tuple(r.results[0][f"out_{i}"] for i in range(len(_OUTS)))
```
